# Optimizing a Trainium2 kernel written in Bass

```python
import jax
import jax.numpy as jnp
from jax import lax
import numpy as np

D_MODEL = 1024
BATCH = 1
SEQ = 512
DEPTH = 2
DEC_BATCH = 8
DEC_SEQ = 1
PAST_LEN = 1024
PAGE_SIZE = 128

HEAD_DIM = 64
ROT_DIM = HEAD_DIM // 4
ROPE_THETA = 500000.0
NSA_HEADS = 8
NSA_GROUPS = 2
NSA_HPG = NSA_HEADS // NSA_GROUPS
CMP_STRIDE = 16
CMP_BLOCK = 2 * CMP_STRIDE
SEL_BLOCK = 64
TOP_N = 16
WINDOW = 512
SB_HEADS = 4
FOX_HEADS = 4
FORGET_BIAS_INIT = 3.0
Q_BLOCK = 128
NSA_W = NSA_HEADS * HEAD_DIM
NSA_KV_W = NSA_GROUPS * HEAD_DIM
SB_W = SB_HEADS * HEAD_DIM
FOX_W = FOX_HEADS * HEAD_DIM
N_IN = NSA_W + 6 * NSA_KV_W + 3 * NSA_HEADS + 3 * SB_W + 3 * FOX_W + FOX_HEADS + 3 * D_MODEL
D_FF = ((8 * D_MODEL + 3 * 256 - 1) // (3 * 256)) * 256
SEL_FORCE_SCORE = 1.0e4
NEG_INF = -1.0e30
RMS_EPS = 1e-6

kernel_name = 'nsa_stickbreak_fox_hybrid_step'

def rmsnorm(x, g):
    xf = x.astype(jnp.float32)
    y = xf * lax.rsqrt(jnp.mean(xf * xf, axis=-1, keepdims=True) + RMS_EPS)
    return (y * g.astype(jnp.float32)).astype(x.dtype)

def rope(x, pos):
    half = ROT_DIM // 2
    inv = ROPE_THETA ** (-jnp.arange(half, dtype=jnp.float32) / half)
    ang = pos.astype(jnp.float32)[:, None] * inv[None, :]
    cos = jnp.cos(ang)[:, None, :]
    sin = jnp.sin(ang)[:, None, :]
    xr = x[..., :ROT_DIM].astype(jnp.float32)
    x1, x2 = xr[..., :half], xr[..., half:]
    rot = jnp.concatenate([x1 * cos - x2 * sin, x2 * cos + x1 * sin], axis=-1)
    return jnp.concatenate([rot.astype(x.dtype), x[..., ROT_DIM:]], axis=-1)

def masked_softmax(s, mask):
    s = jnp.where(mask, s.astype(jnp.float32), NEG_INF)
    e = jnp.where(mask, jnp.exp(s - jnp.max(s, axis=-1, keepdims=True)), 0.0)
    return e / jnp.maximum(jnp.sum(e, axis=-1, keepdims=True), 1e-30)

def pad_rows(a, length):
    return jnp.pad(a, [(0, 0), (0, length - a.shape[1])] + [(0, 0)] * (a.ndim - 2))

def compress(k, pos_emb, w):
    B, L, G, dh = k.shape
    ch = k.reshape(B, L // CMP_STRIDE, CMP_STRIDE, G, dh)
    blocks = jnp.concatenate([ch[:, :-1], ch[:, 1:]], axis=2) + pos_emb[None, None, :, None, :]
    return jnp.einsum('bnlgd,lde->bnge', blocks, w.reshape(CMP_BLOCK, HEAD_DIM, HEAD_DIM))

def sel_blocks(kv):
    B, L = kv.shape[:2]
    return kv.reshape(B, L // SEL_BLOCK, SEL_BLOCK, 2, NSA_GROUPS, HEAD_DIM).transpose(0, 4, 1, 2, 3, 5)

def project(h, pos, w_in, b_forget):
    B, T, _ = h.shape
    p = jnp.einsum('btd,dn->btn', h, w_in)
    sizes = (NSA_W, 2 * NSA_KV_W, 2 * NSA_KV_W, 2 * NSA_KV_W, 3 * NSA_HEADS,
             3 * SB_W, 3 * FOX_W, FOX_HEADS, 3 * D_MODEL)
    parts, start = [], 0
    for s in sizes:
        parts.append(p[..., start:start + s])
        start += s
    pq, pcmp, psel, pwin, pgate, psb, pfox, pf, pmerge = parts
    q_a = rope(pq.reshape(B, T, NSA_HEADS, HEAD_DIM), pos)

    def kv_rot(a):
        a = a.reshape(B, T, 2, NSA_GROUPS, HEAD_DIM)
        return jnp.stack([rope(a[:, :, 0], pos), a[:, :, 1]], axis=2)

    kv_cmp, kv_sel, kv_win = kv_rot(pcmp), kv_rot(psel), kv_rot(pwin)
    g_a = jax.nn.sigmoid(pgate.astype(jnp.float32)).reshape(B, T, NSA_HEADS, 3)
    qkv_b = psb.reshape(B, T, 3, SB_HEADS, HEAD_DIM)
    qkv_c = pfox.reshape(B, T, 3, FOX_HEADS, HEAD_DIM)
    logf = jax.nn.log_sigmoid(pf.astype(jnp.float32) + b_forget.astype(jnp.float32))
    g_m = jax.nn.sigmoid(pmerge.astype(jnp.float32)).reshape(B, T, 3, D_MODEL)
    return q_a, kv_cmp, kv_sel, kv_win, g_a, qkv_b, qkv_c, logf, g_m

def nsa_attend(q, pos_q, gates, ck, cv, kvb, k_win, v_win, pos_win):
    B, T = q.shape[:2]
    scale = HEAD_DIM ** -0.5
    qg = q.reshape(B, T, NSA_GROUPS, NSA_HPG, HEAD_DIM)
    n_cmp = ck.shape[1]
    c_end = jnp.arange(n_cmp, dtype=jnp.int32) * CMP_STRIDE + (CMP_BLOCK - 1)
    c_mask = c_end[None, :] <= pos_q[:, None]
    p_c = masked_softmax(jnp.einsum('btghd,bngd->bghtn', qg, ck).astype(jnp.float32) * scale, c_mask)
    o_c = jnp.einsum('bghtn,bngd->btghd', p_c, cv.astype(jnp.float32))
    p_grp = jnp.sum(p_c, axis=2)
    chunk = (jnp.pad(p_grp, ((0, 0), (0, 0), (0, 0), (1, 0)))
             + jnp.pad(p_grp, ((0, 0), (0, 0), (0, 0), (0, 1))))
    n_sel = kvb.shape[2]
    imp = chunk.reshape(B, NSA_GROUPS, T, n_sel, SEL_BLOCK // CMP_STRIDE).sum(-1)
    blk = jnp.arange(n_sel, dtype=jnp.int32)[None, :]
    cur = (pos_q // SEL_BLOCK)[:, None]
    valid = blk * SEL_BLOCK <= pos_q[:, None]
    forced = (blk == 0) | (blk == cur) | (blk == cur - 1)
    score = jnp.where(valid, jnp.where(forced, SEL_FORCE_SCORE, imp), -1.0)
    n_top = min(TOP_N, n_sel)
    _, idx = lax.top_k(score, n_top)
    bi = jnp.arange(B)[:, None, None, None]
    gi = jnp.arange(NSA_GROUPS)[None, :, None, None]
    kv_g = kvb[bi, gi, idx]
    n_key = n_top * SEL_BLOCK
    k_s = kv_g[..., 0, :].reshape(B, NSA_GROUPS, T, n_key, HEAD_DIM)
    v_s = kv_g[..., 1, :].reshape(B, NSA_GROUPS, T, n_key, HEAD_DIM)
    kpos = (idx[..., None] * SEL_BLOCK + jnp.arange(SEL_BLOCK, dtype=jnp.int32)).reshape(B, NSA_GROUPS, T, n_key)
    s_mask = (kpos <= pos_q[None, None, :, None])[:, :, None]
    p_s = masked_softmax(jnp.einsum('btghd,bgtkd->bghtk', qg, k_s).astype(jnp.float32) * scale, s_mask)
    o_s = jnp.einsum('bghtk,bgtkd->btghd', p_s, v_s.astype(jnp.float32))
    w_mask = ((pos_win[None, :] <= pos_q[:, None]) & (pos_q[:, None] - pos_win[None, :] <= WINDOW)
              & (pos_win[None, :] >= 0))
    p_w = masked_softmax(jnp.einsum('btghd,bsgd->bghts', qg, k_win).astype(jnp.float32) * scale, w_mask)
    o_w = jnp.einsum('bghts,bsgd->btghd', p_w, v_win.astype(jnp.float32))
    g = gates.reshape(B, T, NSA_GROUPS, NSA_HPG, 3)
    o = g[..., 0:1] * o_c + g[..., 1:2] * o_s + g[..., 2:3] * o_w
    return o.reshape(B, T, NSA_W).astype(q.dtype)

def stick_breaking(q, k, v, pos_q, pos_k):
    B, T = q.shape[:2]
    z = jnp.einsum('bthd,bshd->bhts', q, k).astype(jnp.float32) * (HEAD_DIM ** -0.5)
    mask = pos_k[None, :] < pos_q[:, None]
    log_keep = jnp.where(mask, jax.nn.log_sigmoid(-z), 0.0)
    after = lax.cumsum(log_keep, axis=3, reverse=True) - log_keep
    w = jnp.where(mask, jnp.exp(jax.nn.log_sigmoid(z) + after), 0.0)
    o = jnp.einsum('bhts,bshd->bthd', w, v.astype(jnp.float32))
    return o.reshape(B, T, SB_W).astype(q.dtype)

def forgetting_attn(q, k, v, cum_q, cum_k, pos_q, pos_k):
    B, T = q.shape[:2]
    s = (jnp.einsum('bthd,bshd->bhts', q, k).astype(jnp.float32) * (HEAD_DIM ** -0.5)
         + jnp.swapaxes(cum_q, 1, 2)[:, :, :, None] - jnp.swapaxes(cum_k, 1, 2)[:, :, None, :])
    mask = pos_k[None, :] <= pos_q[:, None]
    p = masked_softmax(s, mask)
    o = jnp.einsum('bhts,bshd->bthd', p, v.astype(jnp.float32))
    return o.reshape(B, T, FOX_W).astype(q.dtype)

def merge_branches(o_a, o_b, o_c, g_m, w_up_nsa, w_up_sb, w_up_fox, w_out):
    u = (g_m[:, :, 0] * jnp.einsum('btc,cd->btd', o_a, w_up_nsa)
         + g_m[:, :, 1] * jnp.einsum('btc,cd->btd', o_b, w_up_sb)
         + g_m[:, :, 2] * jnp.einsum('btc,cd->btd', o_c, w_up_fox))
    return jnp.einsum('btd,de->bte', u.astype(w_out.dtype), w_out)

def swiglu(h, w_gate, w_up, w_down):
    return jnp.einsum('btf,fd->btd', jax.nn.silu(jnp.einsum('btd,df->btf', h, w_gate))
                      * jnp.einsum('btd,df->btf', h, w_up), w_down)

def prompt_mixers(h, w_in, b_forget, cmp_pos, w_cmp_k, w_cmp_v):
    B, S, _ = h.shape
    pos = jnp.arange(S, dtype=jnp.int32)
    q_a, kv_cmp, kv_sel, kv_win, g_a, qkv_b, qkv_c, logf, g_m = project(h, pos, w_in, b_forget)
    l_pad = -(-S // SEL_BLOCK) * SEL_BLOCK
    kv_cmp_p = pad_rows(kv_cmp, l_pad)
    ck = compress(kv_cmp_p[:, :, 0], cmp_pos, w_cmp_k)
    cv = compress(kv_cmp_p[:, :, 1], cmp_pos, w_cmp_v)
    kvb = sel_blocks(pad_rows(kv_sel, l_pad))
    win_pad = jnp.pad(kv_win, ((0, 0), (WINDOW, 0), (0, 0), (0, 0), (0, 0)))
    q_b, k_b, v_b = qkv_b[:, :, 0], qkv_b[:, :, 1], qkv_b[:, :, 2]
    q_c, k_c, v_c = qkv_c[:, :, 0], qkv_c[:, :, 1], qkv_c[:, :, 2]
    cum = lax.cumsum(logf, axis=1)

    def block(i):
        q0 = i * Q_BLOCK
        pos_q = q0 + jnp.arange(Q_BLOCK, dtype=jnp.int32)
        rows = lambda a: lax.dynamic_slice_in_dim(a, q0, Q_BLOCK, axis=1)
        wkv = lax.dynamic_slice_in_dim(win_pad, q0, WINDOW + Q_BLOCK, axis=1)
        pos_w = q0 - WINDOW + jnp.arange(WINDOW + Q_BLOCK, dtype=jnp.int32)
        o_a = nsa_attend(rows(q_a), pos_q, rows(g_a), ck, cv, kvb, wkv[:, :, 0], wkv[:, :, 1], pos_w)
        o_b = stick_breaking(rows(q_b), k_b, v_b, pos_q, pos)
        o_c = forgetting_attn(rows(q_c), k_c, v_c, rows(cum), cum, pos_q, pos)
        return o_a, o_b, o_c

    o_a, o_b, o_c = lax.map(block, jnp.arange(S // Q_BLOCK, dtype=jnp.int32))
    unblock = lambda o: jnp.swapaxes(o, 0, 1).reshape(B, S, o.shape[-1])
    win_keep = min(WINDOW, S)
    states = (kv_cmp, kv_sel, qkv_b[:, :, 1:], qkv_c[:, :, 1:], logf, kv_win[:, S - win_keep:])
    return unblock(o_a), unblock(o_b), unblock(o_c), g_m, states

def sample_mixers(h, c_cmp, c_sel, c_sb, c_fox, c_logf, s_win, page_table,
                  w_in, b_forget, cmp_pos, w_cmp_k, w_cmp_v):
    Bd, T, _ = h.shape
    pos = PAST_LEN + jnp.arange(T, dtype=jnp.int32)
    q_a, kv_cmp, kv_sel, kv_win, g_a, qkv_b, qkv_c, logf, g_m = project(h, pos, w_in, b_forget)

    def past(pool):
        g = pool[page_table]
        return g.reshape((Bd, g.shape[1] * g.shape[2]) + pool.shape[2:])

    L = PAST_LEN + T
    l_pad = -(-L // SEL_BLOCK) * SEL_BLOCK
    all_cmp = pad_rows(jnp.concatenate([past(c_cmp), kv_cmp], axis=1), l_pad)
    ck = compress(all_cmp[:, :, 0], cmp_pos, w_cmp_k)
    cv = compress(all_cmp[:, :, 1], cmp_pos, w_cmp_v)
    kvb = sel_blocks(pad_rows(jnp.concatenate([past(c_sel), kv_sel], axis=1), l_pad))
    wb = s_win.shape[1]
    win_all = jnp.concatenate([s_win, kv_win], axis=1)
    pos_w = PAST_LEN - wb + jnp.arange(wb + T, dtype=jnp.int32)
    o_a = nsa_attend(q_a, pos, g_a, ck, cv, kvb, win_all[:, :, 0], win_all[:, :, 1], pos_w)
    pos_k = jnp.arange(L, dtype=jnp.int32)
    sb_all = jnp.concatenate([past(c_sb), qkv_b[:, :, 1:]], axis=1)
    o_b = stick_breaking(qkv_b[:, :, 0], sb_all[:, :, 0], sb_all[:, :, 1], pos, pos_k)
    fox_all = jnp.concatenate([past(c_fox), qkv_c[:, :, 1:]], axis=1)
    cum = lax.cumsum(jnp.concatenate([past(c_logf).astype(jnp.float32), logf], axis=1), axis=1)
    o_c = forgetting_attn(qkv_c[:, :, 0], fox_all[:, :, 0], fox_all[:, :, 1], cum[:, PAST_LEN:], cum, pos, pos_k)
    states = (kv_cmp, kv_sel, qkv_b[:, :, 1:], qkv_c[:, :, 1:], logf, win_all[:, T:])
    return o_a, o_b, o_c, g_m, states

def setup_inputs(seed: int = 0) -> dict:
    key = jax.random.key(seed)
    ks = jax.random.split(key, 32)
    n_pages = PAST_LEN // PAGE_SIZE
    n_pool = (DEC_BATCH * n_pages * 5) // 4
    win_buf = min(WINDOW, PAST_LEN)
    nrm = lambda k, shape, s: jax.random.normal(k, shape, jnp.float32) * s
    page_table = jax.random.permutation(ks[8], n_pool)[:DEC_BATCH * n_pages].reshape(DEC_BATCH, n_pages).astype(jnp.int32)
    return {
        'x_prompt': nrm(ks[0], (BATCH, SEQ, D_MODEL), 1.0),
        'x_sample': nrm(ks[1], (DEC_BATCH, DEC_SEQ, D_MODEL), 1.0),
        'cache_nsa_cmp_kv': nrm(ks[2], (DEPTH, n_pool, PAGE_SIZE, 2, NSA_GROUPS, HEAD_DIM), 1.0),
        'cache_nsa_sel_kv': nrm(ks[3], (DEPTH, n_pool, PAGE_SIZE, 2, NSA_GROUPS, HEAD_DIM), 1.0),
        'cache_sb_kv': nrm(ks[4], (DEPTH, n_pool, PAGE_SIZE, 2, SB_HEADS, HEAD_DIM), 1.0),
        'cache_fox_kv': nrm(ks[5], (DEPTH, n_pool, PAGE_SIZE, 2, FOX_HEADS, HEAD_DIM), 1.0),
        'cache_fox_logf': jax.nn.log_sigmoid(FORGET_BIAS_INIT + nrm(ks[6], (DEPTH, n_pool, PAGE_SIZE, FOX_HEADS), 1.0)),
        'state_nsa_win_kv': nrm(ks[7], (DEPTH, DEC_BATCH, win_buf, 2, NSA_GROUPS, HEAD_DIM), 1.0),
        'page_table': page_table,
        'norm_mix_g': 1.0 + nrm(ks[9], (DEPTH, D_MODEL), 0.02),
        'norm_ffn_g': 1.0 + nrm(ks[10], (DEPTH, D_MODEL), 0.02),
        'norm_final_g': 1.0 + nrm(ks[11], (D_MODEL,), 0.02),
        'w_in': nrm(ks[12], (DEPTH, D_MODEL, N_IN), D_MODEL ** -0.5),
        'b_forget': FORGET_BIAS_INIT + nrm(ks[13], (DEPTH, FOX_HEADS), 0.1),
        'cmp_pos': nrm(ks[14], (DEPTH, CMP_BLOCK, HEAD_DIM), 0.1),
        'w_cmp_k': nrm(ks[15], (DEPTH, CMP_BLOCK * HEAD_DIM, HEAD_DIM), (CMP_BLOCK * HEAD_DIM) ** -0.5),
        'w_cmp_v': nrm(ks[16], (DEPTH, CMP_BLOCK * HEAD_DIM, HEAD_DIM), (CMP_BLOCK * HEAD_DIM) ** -0.5),
        'w_up_nsa': nrm(ks[17], (DEPTH, NSA_W, D_MODEL), NSA_W ** -0.5),
        'w_up_sb': nrm(ks[18], (DEPTH, SB_W, D_MODEL), SB_W ** -0.5),
        'w_up_fox': nrm(ks[19], (DEPTH, FOX_W, D_MODEL), FOX_W ** -0.5),
        'w_out': nrm(ks[20], (DEPTH, D_MODEL, D_MODEL), D_MODEL ** -0.5),
        'w_ffn_gate': nrm(ks[21], (DEPTH, D_MODEL, D_FF), D_MODEL ** -0.5),
        'w_ffn_up': nrm(ks[22], (DEPTH, D_MODEL, D_FF), D_MODEL ** -0.5),
        'w_ffn_down': nrm(ks[23], (DEPTH, D_FF, D_MODEL), D_FF ** -0.5),
    }

def reference(x_prompt, x_sample, cache_nsa_cmp_kv, cache_nsa_sel_kv, cache_sb_kv, cache_fox_kv,
              cache_fox_logf, state_nsa_win_kv, page_table, norm_mix_g, norm_ffn_g, norm_final_g,
              w_in, b_forget, cmp_pos, w_cmp_k, w_cmp_v, w_up_nsa, w_up_sb, w_up_fox, w_out,
              w_ffn_gate, w_ffn_up, w_ffn_down):
    xp, xs = x_prompt, x_sample
    p_states, s_states = [], []
    for l in range(DEPTH):
        hp = rmsnorm(xp, norm_mix_g[l])
        a_p, b_p, c_p, gm_p, st_p = prompt_mixers(hp, w_in[l], b_forget[l], cmp_pos[l], w_cmp_k[l], w_cmp_v[l])
        xp = xp + merge_branches(a_p, b_p, c_p, gm_p, w_up_nsa[l], w_up_sb[l], w_up_fox[l], w_out[l])
        hs = rmsnorm(xs, norm_mix_g[l])
        a_s, b_s, c_s, gm_s, st_s = sample_mixers(
            hs, cache_nsa_cmp_kv[l], cache_nsa_sel_kv[l], cache_sb_kv[l], cache_fox_kv[l],
            cache_fox_logf[l], state_nsa_win_kv[l], page_table,
            w_in[l], b_forget[l], cmp_pos[l], w_cmp_k[l], w_cmp_v[l])
        xs = xs + merge_branches(a_s, b_s, c_s, gm_s, w_up_nsa[l], w_up_sb[l], w_up_fox[l], w_out[l])
        xp = xp + swiglu(rmsnorm(xp, norm_ffn_g[l]), w_ffn_gate[l], w_ffn_up[l], w_ffn_down[l])
        xs = xs + swiglu(rmsnorm(xs, norm_ffn_g[l]), w_ffn_gate[l], w_ffn_up[l], w_ffn_down[l])
        p_states.append(st_p)
        s_states.append(st_s)
    y_prompt = rmsnorm(xp, norm_final_g)
    y_sample = rmsnorm(xs, norm_final_g)
    stk = lambda sts, i: jnp.stack([st[i] for st in sts], axis=0)
    return (y_prompt, y_sample,
            stk(p_states, 0), stk(p_states, 1), stk(p_states, 2), stk(p_states, 3), stk(p_states, 4), stk(p_states, 5),
            stk(s_states, 0), stk(s_states, 1), stk(s_states, 2), stk(s_states, 3), stk(s_states, 4), stk(s_states, 5))


_drawn_inputs = setup_inputs


def setup_inputs(seed=0):
    import zlib

    import numpy as np

    out = dict(_drawn_inputs(seed))
    spreads = {}
    factors = {'norm_ffn_g': 2.902, 'norm_final_g': 2.828}
    for name, (base, spread) in spreads.items():
        noise = np.random.default_rng([zlib.crc32(name.encode()), seed]).standard_normal(out[name].shape)
        drawn = base * np.exp(spread * noise) if base else spread * noise
        out[name] = jnp.asarray(drawn.astype(out[name].dtype))
    for name, factor in factors.items():
        out[name] = (out[name] * factor).astype(out[name].dtype)
    return out
```

```python
import concourse.bass as bass
from concourse import mybir
from contextlib import ExitStack
import numpy as np

P = 128
D = 1024
KD = D // P
SEQ, NS = 512, 8
T = SEQ + NS
H2 = T // 2
TT = SEQ // P
DEPTH = 2
PAST, PAGE = 1024, 128
NPG = PAST // PAGE
NPOOL = NS * NPG * 5 // 4
DH = 64
G = 2
STRIDE, CBLK = 16, 32
NCP = SEQ // STRIDE - 1
NCS = PAST // STRIDE - 1
NBLK = PAST // 64
WIN = 512
DFF = 2816
NF = DFF // P
N_IN = 5916
NEG = -1.0e30
EPS = 1e-6
SCALE = DH ** -0.5
CMPK, CMPV, SELK, SELV, WINK, WINV, SBQ, SBK, SBV, FXQ, FXK, FXV = 4, 5, 6, 7, 8, 9, 10, 12, 14, 16, 18, 20
NT = 22
QTILES = (0, 1, 2, 3, SBQ, SBQ + 1, FXQ, FXQ + 1)
ROPE = (0, 1, 2, 3, CMPK, SELK, WINK)
NAT = (CMPK, CMPV, SELK, SELV, WINK, WINV, SBK, SBK + 1, SBV, SBV + 1, FXK, FXK + 1, FXV, FXV + 1)
NATV = (SELV, WINV, SBV, SBV + 1, FXV, FXV + 1)
NATK = tuple(t for t in NAT if t not in NATV)
CONST, _c = {}, 0
for _n, _w in (("ident", P), ("rot", P), ("upper", P), ("ones", 7 * P), ("later", P), ("nupper", P),
               ("nones", P), ("cos", T), ("sin", T), ("group", 64), ("row8", 8), ("row4", 8),
               ("blk", NBLK - 2), ("onehot", 4 * P), ("cmp01", TT * 32),
               ("mcausal", P), ("mstrict", P), ("mcmp", TT * 32)):
    CONST[_n] = (_c, _w)
    _c += _w
NCONST = _c
NKEEP = CONST["mcausal"][0]
CHUNKS = ([("in", c) for c in range(6)] + [("cmp", 0)]
          + [x for h in range(2) for x in [("up", h)] + [("mg", h, b) for b in range(3)]]
          + [("out", 0), ("out", 1)] + [("ffn", j) for j in range(NF // 2)]
          + [("down", n, h) for n in range(4) for h in range(2)])
RING = 3
NCH = len(CHUNKS)
assert NCH % RING == 0
UNITS = ([("cmp", b, h) for b in range(NS) for h in range(2)] + [("selk", b, 0) for b in range(NS)]
         + [("wink", b, 0) for b in range(NS)] + [("lf", 0, 0)]
         + [(k, b, h) for k in ("fxk", "sbk") for b in range(NS) for h in range(2)]
         + [(k, b, h) for k in ("fxv", "sbv") for b in range(NS) for h in range(2)]
         + [("selv", b, 0) for b in range(NS)] + [("winv", b, 0) for b in range(NS)])
NU = len(UNITS)
USLOTS = 6
NKU = UNITS.index(("fxv", 0, 0))
KSTEPS = {"cmp": 2, "selk": 2, "wink": 1, "lf": 1, "fxk": 2, "sbk": 2}
UT = (4, 5, 6, 7, 8, 9, 12, 13)
ACT_CHAIN, DVE_CHAIN = 12, 229
PAIRS = [("nsa", t) for t in range(4)] + [("fox", 0), ("fox", 1)]
SOFT = [(p, br) for p in range(4) for br in ("cmp", "sel", "win")] + [(4, "fox"), (5, "fox")]
ITEMS = [(u, i) for u in range(len(SOFT)) for i in range(TT)]


class Layer:
    def __init__(self, more):
        self.more = more


def w_dmas(ch):
    return {"cmp": 4, "up": 4, "ffn": 2}.get(ch[0], {("in", 0): 8, ("in", 2): 2}.get(ch, 1))


def u_dmas(u):
    return {"cmp": 4, "selk": 8, "selv": 8, "wink": 1, "winv": 1, "lf": NS * NPG}.get(u[0], 4)


def layer_counts():
    items = len(ITEMS)
    ksteps = sum(KSTEPS[u[0]] for u in UNITS[:NKU])
    c = dict(sq_ready=2 * KD, sq_used=2 * KD, rs_ready=2, h_ready=2 * KD, x_upd=2 * KD,
             proj_ps=NT, proj_ev=NT, rot_ps=len(ROPE), rope_done=len(ROPE), nat_ps=len(NAT), nat_ev=len(NAT),
             new_ps=1, new_ev=1, gate_ps=1, gate_ev=1, gate_sig=1, lf_abs=1, lf_ln=1, lf_done=1, cum_ps=1, cum_ev=1,
             sig_dma=32, out_dma=16 * (2 * len(NAT) + 2), q_ev=1, new_ready=1,
             ck_ps=1, ck_ev=1, cvt_ps=1, cvt_ev=1,
             kt_ps=ksteps, kt_ev=ksteps, cs_ps=4, cs_ev=4, cvs_ps=2, cvs_ev=2,
             s_ps=items, nm_ready=items, exp_done=items, p_scaled=items, pt_ps=2 * items,
             pt_ev_a=items, pt_ev_d=items, pv_done=len(SOFT), o_ev=8,
             sbz_ps=4, sb_ln=4, sb_sp=4, sbc_ps=4, sb_w=4, sb_pv=4,
             smm=sum(KSTEPS[u[0]] for u in UNITS[:NKU] if u[0] in ("selk", "wink", "fxk", "sbk")),
             sc_ps=1, sc_nm=1, sc_exp=1, sc_p=1, pg_ps=1, drop=1, snew=3, s_ev=4, s_nm=3, s_exp=3, s_p=3,
             zt_ps=1, z_abs=1, z_sp=1, zc_ps=1, z_w=1, ptt_ps=3, ptt_ev=3, z_sum=1, dg=3, dm_ps=1, dm_ev=1,
             v_used=NU - NKU, so_ps=1, so_ev=1, sct=1, sce=1,
             mt_ps=56, mt_ev=48, mul=24, u_ready=8, ffn_g=NF, ffn_s=NF, ffn_u=NF, hid=NF, down_ps=8)
    return c


def build(nc, A, out):
    f32, bf16, i32 = mybir.dt.float32, mybir.dt.bfloat16, mybir.dt.int32
    ALU, ACT, AX = mybir.AluOpType, mybir.ActivationFunctionType, mybir.AxisListType
    PER = layer_counts()
    ctx = ExitStack()
    with ctx:
        def sb(name, shape, dt=f32):
            return ctx.enter_context(nc.sbuf_tensor(name, shape, dt))

        xT = sb("xT", [P, KD, T])
        hT = sb("hT", [P, KD, T])
        PT = sb("PT", [P, NT, T])
        ring = sb("ring", [P, RING, 4096])
        ARENA = 6500
        arena = sb("arena", [P, ARENA])
        units = sb("units", [P, USLOTS, 1024])
        vnat = sb("vnat", [P, len(NATV), TT, P])
        cst = sb("cst", [P, NKEEP])
        maskb = sb("maskb", [P, 4 * P], bf16)
        ckT = sb("ckT", [P, NS, NCS])
        cvS = sb("cvS", [NCS, NS, P])
        qn = sb("qn", [P, NS, 64])
        qs = sb("qs", [P, 2, NS, 32])
        qf = sb("qf", [P, 2, NS, 32])
        gnat = sb("gnat", [P, TT, 28])
        gsmp = sb("gsmp", [NS, 28])
        lfn = sb("lfn", [P, TT, 4])
        lft = sb("lft", [P, TT, 4])
        lfs = sb("lfs", [NS, 4])
        lfst = sb("lfst", [NS, 4])
        g64 = sb("g64", [64, 3])
        l32 = sb("l32", [32, 1])
        bfb = sb("bfb", [P, DEPTH, 4])
        gam = sb("gam", [P, 2 * DEPTH + 1, KD])
        ncum = sb("ncum", [4, SEQ])
        ckP = sb("ckP", [P, 2, 32])
        cvP = sb("cvP", [32, P])
        cbias = sb("cbias", [P, 2])
        posT = sb("posT", [P, DEPTH, CBLK])
        LF = sb("LF", [P, NPG, NS, 4])
        nm = sb("nm", [P, 2, 2])
        sm = sb("sm", [P, 2, 2])
        rr = sb("rr", [P, 2, 2])
        vnew = sb("vnew", [NS, len(NATV), P])
        pc = sb("pc", [64, 64])
        pgb = sb("pgb", [64, 72])
        s1 = sb("s1", [64, 32])
        pgt = sb("pgt", [1, NS * NPG], i32)
        epsb = sb("epsb", [P, 1])
        gl = sb("gl", [P, 2, KD])
        posL = sb("posL", [P, CBLK])
        bfl = sb("bfl", [P, 4])
        ps = ctx.enter_context(nc.psum_tensor("ps", [P, 8, 512], f32))

        def ar(at, *shape):
            n = int(np.prod(shape))
            v = arena[:, at:at + n]
            if len(shape) == 1:
                return v
            names = "abcd"[:len(shape)]
            return v.rearrange(f"p ({' '.join(names)}) -> p {' '.join(names)}", **dict(zip(names, shape)))

        posn = ar(5120, DEPTH, G, DH)[0:CBLK]
        sq, rs, rinv = ar(0, 2, T), ar(2 * T, T), ar(3 * T, T)
        ropet, knat, natS = ar(0, T), ar(T, len(NATV) + 2, TT * P), ar(T + 7 * 512 + 512, len(NAT), P)
        KC = ar(0, 2, 2, PAST)
        cvT = ar(4096, 2, NCS)
        Pb, PTb = ar(0, 2, 2, 512), ar(2048, 2, TT, 512)
        zt, spb, wb = ar(0, 1280), ar(1280, 1280), ar(2560, 1280)
        SS, PTs, SW, PTw = ar(0, 1025), ar(1028, NPG, 64), ar(1544, 513), ar(2060, 4, 64)
        SF, PTf = ar(2320, 1025), ar(3348, NPG, 32)
        za, zsp, zw, ZS = ar(3604, 256), ar(3860, 256), ar(4116, NPG, 32), ar(4372, 1024)
        KT = ar(5396, 2, 512)
        sg = [vnat[:, :, :, :].rearrange("p a b c -> p (a b c)")[:, i * T:(i + 1) * T] for i in range(2)]
        vflat = vnat[:, :, :, :].rearrange("p a b c -> p (a b c)")
        dg = vflat[0:64, 1040:1232].rearrange("p (a b) -> p a b", a=3)
        DM, pcT = vflat[0:NS, 1232:1392], vflat[0:64, 1392:1456]
        t17 = vflat[0:64, 1456:1536].rearrange("p (a b) -> p a b", a=4)
        UP = ar(0, 12, T)
        fs = ar(0, 2, T)

        def C(name, rows=P):
            a, n = CONST[name]
            return cst[0:rows, a:a + n]

        identb, mcausal, mstrict, mcmpb = (maskb[:, i * P:(i + 1) * P] for i in range(4))
        ident, rot = C("ident"), C("rot")
        o0 = CONST["upper"][0]
        cum_fwd = cst[:, o0:o0 + 4 * P]
        o1 = CONST["ones"][0]
        cum_bwd = cst[:, o1:o1 + 8 * P]

        sems = {}
        for name in list(PER) + ["const_in", "const_ok", "xt_ps", "xt_in", "y_ps", "y_ev", "y_dma", "win_dma", "pg_in",
                                 "post_ps", "dve_chain", "act_chain", "init_z"] \
                + [f"w{i}" for i in range(RING)] + [f"u{i}" for i in range(USLOTS)]:
            sems[name] = ctx.enter_context(nc.semaphore(name))
        CREDIT = {"down_ps": PER["down_ps"], "v_used": PER["v_used"]}
        BASE = {"x_upd": KD}

        regs = {}

        def in_layers(eng, l):
            if "layer" not in regs.setdefault(eng.engine, {}):
                regs[eng.engine].update(layer=eng.alloc_register("layer"), value=eng.alloc_register("wait_value"))
            eng.reg_mov(regs[eng.engine]["layer"], l)
            return Layer(0)

        def count(eng, l, per, n):
            if not isinstance(l, Layer):
                return l * per + n
            layer, value = regs[eng.engine]["layer"], regs[eng.engine]["value"]
            eng.reg_mul(value, layer, per)
            eng.reg_add(value, value, n + l.more * per)
            return value

        def at(eng, name, l, n):
            assert n >= 1, name
            return count(eng, l, PER[name], n + CREDIT.get(name, 0) + BASE.get(name, 0))

        def apart(eng):
            value = regs[eng.engine]["value"]
            eng.reg_add(value, value, 1)
            eng.reg_mul(value, value, 2)

        chunk_read, up, mg, ou = {}, 0, 0, 0
        for n, ch in enumerate(CHUNKS):
            k = ch[0]
            chunk_read[n] = {"in": lambda: ("proj_ps", (4, 8, None, 14, 18, 22)[ch[1]]), "cmp": lambda: ("cs_ps", 4),
                             "up": lambda: ("mt_ps", 24 * ch[1] + 12),
                             "mg": lambda: ("mt_ps", 24 * ch[1] + 12 + 4 * (ch[2] + 1)),
                             "out": lambda: ("mt_ps", 48 + 4 * (ch[1] + 1)), "ffn": lambda: ("ffn_u", 2 * (ch[1] + 1)),
                             "down": lambda: ("down_ps", 2 * ch[1] + ch[2] + 1)}[k]()
        chunk_read[2] = ("gate_ps", 1)
        w_at, cnt = [], [0] * RING
        for n, ch in enumerate(CHUNKS):
            cnt[n % RING] += 16 * w_dmas(ch)
            w_at.append(cnt[n % RING])
        w_per = cnt
        u_at, cnt, last_in = [], [0] * USLOTS, {}
        for n, u in enumerate(UNITS):
            cnt[n % USLOTS] += 16 * u_dmas(u)
            u_at.append(cnt[n % USLOTS])
            last_in[n % USLOTS] = n
        u_per = cnt
        unit_read, k = [], 0
        for n, u in enumerate(UNITS):
            if n < NKU:
                k += KSTEPS[u[0]]
                unit_read.append(("kt_ps", k))
            else:
                unit_read.append(("v_used", n - NKU + 1))

        def weights_in(eng, l, ch):
            n = CHUNKS.index(ch)
            eng.wait_ge(sems[f"w{n % RING}"], count(eng, l, w_per[n % RING], w_at[n]))
            return ring[:, n % RING, :]

        def unit_in(eng, l, u):
            n = UNITS.index(u)
            eng.wait_ge(sems[f"u{n % USLOTS}"], count(eng, l, u_per[n % USLOTS], u_at[n]))
            return units[:, n % USLOTS, :]

        def half(ap):
            return ap.rearrange("p (h t) -> p h t", h=2)

        def pair(b):
            return ps[:, b:b + 2, 0:H2]

        block = ctx.enter_context(nc.Block())

        @block.sync
        def _(sp):
            dma = sp.dma_start
            dma(cst[:, :], A["consts"][:, 0:NKEEP]).then_inc(sems["const_in"], 16)
            dma(hT[:, :, :].rearrange("p a b -> p (a b)")[:, 0:NCONST - NKEEP], A["consts"][:, NKEEP:NCONST]).then_inc(sems["const_in"], 16)
            dma(ar(0, TT, D), A["x_prompt"][0].rearrange("(t p) d -> p t d", p=P)).then_inc(sems["const_in"], 16)
            dma(ar(TT * D, D)[0:NS], A["x_sample"].rearrange("b s d -> (b s) d")).then_inc(sems["const_in"], 16)
            with nc.allow_non_contiguous_dma(reason="norm gains and biases: a few kilobytes, once"):
                for i in range(DEPTH):
                    dma(gam[:, 2 * i, :], A["norm_mix_g"][i].rearrange("(k p) -> p k", p=P)).then_inc(sems["const_in"], 16)
                    dma(gam[:, 2 * i + 1, :], A["norm_ffn_g"][i].rearrange("(k p) -> p k", p=P)).then_inc(sems["const_in"], 16)
                dma(gam[:, 2 * DEPTH, :], A["norm_final_g"].rearrange("(k p) -> p k", p=P)).then_inc(sems["const_in"], 16)
            for g in range(G):
                dma(posn[:, :, g, :], A["cmp_pos"].rearrange("l c d -> c l d")).then_inc(sems["const_in"], 16)
            dma(bfb[:, :, :], A["b_forget"].rearrange("l h -> (l h)").partition_broadcast(P)).then_inc(sems["const_in"], 16)
            dma(pgt[:, :], A["page_table"].rearrange("(a b) n -> a (b n)", a=1)).then_inc(sems["pg_in"], 16)
            sp.wait_ge(sems["pg_in"], 16)

            def load_chunk(l, n):
                ch = CHUNKS[n]
                m = (n - RING) % NCH
                sp.wait_ge(sems[chunk_read[m][0]], at(sp, chunk_read[m][0], Layer(0 if n >= RING else -1), chunk_read[m][1]))
                slot, sem = ring[:, n % RING, :], sems[f"w{n % RING}"]
                w_in = A["w_in"][l].rearrange("(k p) n -> p k n", p=P)

                def put(at, k, cols, src):
                    dma(slot[:, at:at + k * cols].rearrange("p (k n) -> p k n", k=k), src).then_inc(sem, 16)

                if ch == ("in", 0):
                    for g in range(G):
                        for t in range(4):
                            dst = slot.rearrange("p (k t g d) -> p k t g d", k=KD, g=G, d=DH)[:, :, t, g, :]
                            dma(dst, w_in[:, :, g * 256 + t * DH:g * 256 + (t + 1) * DH]).then_inc(sem, 16)
                elif ch == ("in", 2):
                    v = slot.rearrange("p (k n) -> p k n", k=KD)
                    dma(v[:, :, 0:280], w_in[:, :, 1024:1304]).then_inc(sem, 16)
                    dma(v[:, :, 280:284], w_in[:, :, 2840:2844]).then_inc(sem, 16)
                elif ch[0] == "in":
                    c0 = (0, 512, 1024, 1304, 1816, 2328)[ch[1]]
                    put(0, KD, 512, w_in[:, :, c0:c0 + 512])
                elif ch[0] == "cmp":
                    for j, w in enumerate(("w_cmp_k", "w_cmp_v")):
                        for g in range(G):
                            dst = slot[g * DH:(g + 1) * DH, j * 2048:(j + 1) * 2048].rearrange("d (l e) -> d l e", e=DH)
                            dma(dst, A[w][l].rearrange("(l d) e -> d l e", d=DH)).then_inc(sem, 16)
                elif ch[0] == "mg":
                    c0 = 2844 + ch[2] * D + ch[1] * 512
                    put(0, KD, 512, w_in[:, :, c0:c0 + 512])
                elif ch[0] == "up":
                    cs = slice(ch[1] * 512, ch[1] * 512 + 512)
                    for g in range(G):
                        dst = slot[g * DH:(g + 1) * DH, 0:2048].rearrange("d (t n) -> d t n", t=4)
                        src = A["w_up_nsa"][l].rearrange("(g t d) n -> g d t n", g=G, t=4)[g][:, :, cs]
                        dma(dst, src).then_inc(sem, 16)
                    dst = slot[:, 2048:3072].rearrange("p (k n) -> p k n", k=2)
                    dma(dst, A["w_up_sb"][l].rearrange("(k p) n -> p k n", p=P)[:, :, cs]).then_inc(sem, 16)
                    dst = slot[:, 3072:4096].rearrange("p (k n) -> p k n", k=2)
                    dma(dst, A["w_up_fox"][l].rearrange("(k p) n -> p k n", p=P)[:, :, cs]).then_inc(sem, 16)
                elif ch[0] == "out":
                    put(0, KD, 512, A["w_out"][l].rearrange("(k p) n -> p k n", p=P)[:, :, ch[1] * 512:ch[1] * 512 + 512])
                elif ch[0] == "ffn":
                    for j, w in enumerate(("w_ffn_gate", "w_ffn_up")):
                        put(j * 2048, KD, 256, A[w][l].rearrange("(k p) n -> p k n", p=P)[:, :, ch[1] * 256:ch[1] * 256 + 256])
                else:
                    put(0, NF // 2, 256, A["w_ffn_down"][l].rearrange("(h k p) n -> h p k n", h=2, p=P)[ch[2]][:, :, ch[1] * 256:ch[1] * 256 + 256])

            def load_unit(l, n):
                kind, b, h = UNITS[n]
                m = n - USLOTS
                src = unit_read[m] if m >= 0 else unit_read[last_in[n % USLOTS]]
                slot, sem = units[:, n % USLOTS, :], sems[f"u{n % USLOTS}"]

                def page(i):
                    return sp.value_load(pgt[0:1, i:i + 1], min_val=0, max_val=NPOOL - 1)

                def rows(name):
                    a = A[name]
                    spec = "l n r t h d -> (l n) r (t h d)" if len(a.shape) == 6 else "l n r h -> (l n) (r h)"
                    return a.rearrange(spec)

                def free():
                    sp.wait_ge(sems[src[0]], at(sp, src[0], Layer(0 if m >= 0 else -1), src[1]))

                if kind == "lf":
                    for i in range(NS * NPG):
                        pg = page(i)
                        if i == 0:
                            free()
                        dma(slot[i:i + 1, 0:512], rows("cache_fox_logf")[bass.ds(l * NPOOL + pg, 1)]).then_inc(sem, 16)
                elif kind in ("wink", "winv"):
                    c0 = 0 if kind == "wink" else P
                    free()
                    w = A["state_nsa_win_kv"].rearrange("l b (j p) t h d -> (l b) p j (t h d)", p=P)
                    dma(slot[:, 0:512].rearrange("p (j c) -> p j c", j=4), w[l * NS + b][:, :, c0:c0 + P]).then_inc(sem, 16)
                else:
                    name, c0, cols = {"cmp": ("cache_nsa_cmp_kv", 0, 256), "selk": ("cache_nsa_sel_kv", 0, 128),
                                      "selv": ("cache_nsa_sel_kv", 128, 128), "fxk": ("cache_fox_kv", 0, 256),
                                      "fxv": ("cache_fox_kv", 256, 256), "sbk": ("cache_sb_kv", 0, 256),
                                      "sbv": ("cache_sb_kv", 256, 256)}[kind]
                    k = 1024 // cols
                    pages = [page(b * NPG + h * k + j) for j in range(k)]
                    free()
                    for j, pg in enumerate(pages):
                        dma(slot[:, j * cols:(j + 1) * cols], rows(name)[l * NPOOL + pg][:, c0:c0 + cols]).then_inc(sem, 16)

            with sp.Fori(0, DEPTH) as l:
                in_layers(sp, l)
                dma(out["s_win"].rearrange("l b r t h d -> (l b) r (t h d)")[bass.ds(l * NS, NS), 0:WIN - 1],
                    A["state_nsa_win_kv"].rearrange("l b r t h d -> (l b) r (t h d)")[bass.ds(l * NS, NS), 1:WIN]).then_inc(sems["win_dma"], 16)
                n_cmp = CHUNKS.index(("cmp", 0))
                for n in range(n_cmp + 1):
                    load_chunk(l, n)
                for n in range(NU):
                    load_unit(l, n)
                for n in range(n_cmp + 1, NCH):
                    load_chunk(l, n)
            sp.wait_ge(sems["win_dma"], 16 * DEPTH)

        @block.tensor
        def _(pe):
            mm = nc.tensor.matmul

            def tp(o, i, n):
                return nc.tensor.transpose(o, i, ident[0:n, 0:n])

            pe.sem_inc(sems["down_ps"], PER["down_ps"])
            pe.sem_inc(sems["v_used"], PER["v_used"])
            pe.wait_ge(sems["const_in"], 16 * 12)
            for k in range(KD):
                if k >= 2:
                    pe.wait_ge(sems["x_upd"], k - 1)
                for t in range(TT):
                    tp(ps[:, 2 * (k % 2), t * P:(t + 1) * P], ar(0, TT, D)[:, t, k * P:(k + 1) * P], P)
                tp(ps[:, 2 * (k % 2) + 1, 0:NS], ar(TT * D, D)[0:NS, k * P:(k + 1) * P], NS).then_inc(sems["xt_ps"], 1)
            for i in range(DEPTH):
                last = tp(ps[:, 4, i * CBLK:(i + 1) * CBLK], posn[:, i, :, :].rearrange("c g d -> c (g d)"), CBLK)
            last.then_inc(sems["post_ps"], 1)

            def norm(l, w):
                pe.wait_ge(sems["x_upd"], count(pe, l, PER["x_upd"], w * KD + KD - 2))
                for k in range(KD):
                    pe.wait_ge(sems["sq_ready"], at(pe, "sq_ready", l, w * KD + k + 1))
                    mm(ps[:, 0, 0:H2], C("ones")[:, 0:P], sq[:, k % 2, 0:H2], start=k == 0, stop=k == KD - 1)
                    mm(ps[:, 1, 0:H2], C("ones")[:, 0:P], sq[:, k % 2, H2:T], start=k == 0, stop=k == KD - 1).then_inc(sems["sq_used"], 1)

            def tile(b, pairs):
                n = len(pairs)
                for k, (w, a) in enumerate(pairs):
                    mm(ps[:, b, 0:H2], w, a[:, 0:H2], start=k == 0, stop=k == n - 1)
                    last = mm(ps[:, b + 1, 0:H2], w, a[:, H2:T], start=k == 0, stop=k == n - 1)
                return last

            def project(l):
                def post(i):
                    pe.wait_ge(sems["proj_ev"], at(pe, "proj_ev", l, i + 1))
                    if i in ROPE:
                        r = ROPE.index(i)
                        if r >= 1:
                            pe.wait_ge(sems["rope_done"], at(pe, "rope_done", l, r))
                        if i == WINK:
                            pe.wait_ge(sems["gate_ev"], at(pe, "gate_ev", l, 1))
                        mm(ps[:, 4, 0:H2], rot, PT[:, i, 0:H2], start=True, stop=True)
                        mm(ps[:, 5, 0:H2], rot, PT[:, i, H2:T], start=True, stop=True).then_inc(sems["rot_ps"], 1)

                def nat(i):
                    if i not in NAT:
                        return
                    n = NAT.index(i)
                    if i in ROPE:
                        pe.wait_ge(sems["rope_done"], at(pe, "rope_done", l, ROPE.index(i) + 1))
                    if n >= 2:
                        pe.wait_ge(sems["nat_ev"], at(pe, "nat_ev", l, n - 1))
                    for t in range(TT):
                        last = tp(ps[:, 6 + n % 2, t * P:(t + 1) * P], PT[:, i, t * P:(t + 1) * P], P)
                    last.then_inc(sems["nat_ps"], 1)

                for i in range(NT):
                    c = i // 4 if i < 8 else 2 if i < 10 else 3 + (i - 10) // 4
                    w = weights_in(pe, l, ("in", c)).rearrange("p (k n) -> p k n", k=KD)
                    j = i - (0, 4, 8, 10, 14, 18)[c]
                    if i >= 2:
                        pe.wait_ge(sems["proj_ev"], at(pe, "proj_ev", l, i - 1))
                    for k in range(KD):
                        if i == 0:
                            pe.wait_ge(sems["h_ready"], at(pe, "h_ready", l, k + 1))
                        mm(ps[:, 2 * (i % 2), 0:H2], w[:, k, j * P:(j + 1) * P], hT[:, k, 0:H2], start=k == 0, stop=k == KD - 1)
                        last = mm(ps[:, 2 * (i % 2) + 1, 0:H2], w[:, k, j * P:(j + 1) * P], hT[:, k, H2:T], start=k == 0, stop=k == KD - 1)
                    last.then_inc(sems["proj_ps"], 1)
                    if i == WINV:
                        pe.wait_ge(sems["rope_done"], at(pe, "rope_done", l, ROPE.index(WINK)))
                        for t in range(TT):
                            for k in range(KD):
                                mm(ps[:, 5, 264 + 28 * t:292 + 28 * t], hT[:, k, t * P:(t + 1) * P], w[:, k, 256:284], start=k == 0, stop=k == KD - 1)
                        for k in range(KD):
                            last = mm(ps[0:NS, 4, 264:292], hT[:, k, SEQ:T], w[:, k, 256:284], start=k == 0, stop=k == KD - 1)
                        last.then_inc(sems["gate_ps"], 1)
                    if i >= 1:
                        post(i - 1)
                    if i >= 2:
                        nat(i - 2)
                post(NT - 1)
                nat(NT - 2)
                nat(NT - 1)
                for n, i in enumerate(NAT):
                    last = tp(ps[0:NS, n // 4, n % 4 * P:(n % 4 + 1) * P], PT[:, i, SEQ:T], P)
                last.then_inc(sems["new_ps"], 1)

            def cumulate(l):
                pe.wait_ge(sems["lf_done"], at(pe, "lf_done", l, 1))
                for t in range(TT):
                    last = mm(ps[0:4, 4, t * P:SEQ], lfn[:, t, :], cum_fwd[:, 0:SEQ - t * P], start=t == 0, stop=True, skip_group_check=True)
                last.then_inc(sems["cum_ps"], 1)

            def compress(l):
                pe.wait_ge(sems["cum_ev"], at(pe, "cum_ev", l, 1))
                pe.wait_ge(sems["nat_ev"], at(pe, "nat_ev", l, len(NAT)))
                pe.wait_ge(sems["new_ev"], at(pe, "new_ev", l, 1))
                w = weights_in(pe, l, ("cmp", 0)).rearrange("p (j l e) -> p j l e", j=2, l=CBLK)
                apart(pe)
                for j in range(2):
                    for g in range(G):
                        r = slice(g * DH, (g + 1) * DH)
                        for c in range(CBLK):
                            mm(ps[r, 2 + j, 0:NCP], w[r, j, c, :], PT[r, CMPK + j, c:c + STRIDE * (NCP - 1) + 1:STRIDE], start=c == 0, stop=c == CBLK - 1)
                        for c in range(CBLK):
                            last = mm(ps[r, 2 + j, 64:65], w[r, j, c, :], posL[r, c:c + 1], start=c == 0, stop=c == CBLK - 1)
                last.then_inc(sems["ck_ps"], 1)
                pe.wait_ge(sems["ck_ev"], at(pe, "ck_ev", l, 1))
                tp(ps[0:NCP, 1, 0:P], ckP[:, 1, 0:NCP], P).then_inc(sems["cvt_ps"], 1)
                step = 0
                for q in range(4):
                    for u in range(4):
                        b, h = 2 * q + u // 2, u % 2
                        s = unit_in(pe, l, ("cmp", b, h)).rearrange("p (j c) -> p j c", j=4)
                        for kv in range(2):
                            if step >= 2:
                                pe.wait_ge(sems["kt_ev"], at(pe, "kt_ev", l, step - 1))
                            for j in range(4):
                                last = tp(ps[:, 6 + step % 2, j * P:(j + 1) * P], s[:, j, kv * P:(kv + 1) * P], P)
                            last.then_inc(sems["kt_ps"], 1)
                            step += 1
                    pe.wait_ge(sems["kt_ev"], at(pe, "kt_ev", l, step))
                    if q:
                        pe.wait_ge(sems["cs_ev"], at(pe, "cs_ev", l, q))
                    apart(pe)
                    for kv in range(2):
                        for g in range(G):
                            r = slice(g * DH, (g + 1) * DH)
                            for c in range(CBLK):
                                last = mm(ps[r, 4 + kv, 0:2 * NCS], w[r, kv, c, :],
                                          KC[r, kv, :, c:c + STRIDE * (NCS - 1) + 1:STRIDE], start=c == 0, stop=c == CBLK - 1)
                    last.then_inc(sems["cs_ps"], 1)
                    pe.wait_ge(sems["cs_ev"], at(pe, "cs_ev", l, q + 1))
                    apart(pe)
                    for i in range(2):
                        bb = 2 * (q % 2) + i
                        last = tp(ps[0:NCS, 0, bb * P:(bb + 1) * P], cvT[:, i, :], P)
                    if q % 2:
                        last.then_inc(sems["cvs_ps"], 1)
                        if q == 1:
                            pe.wait_ge(sems["cvs_ev"], at(pe, "cvs_ev", l, 1))

            def heads(idx):
                kind, t = PAIRS[idx]
                return t if kind == "nsa" else FXQ + t

            def scores(l, n):
                u, i = ITEMS[n]
                idx, br = SOFT[u]
                qt = heads(idx)
                if n >= 2:
                    pe.wait_ge(sems["exp_done"], at(pe, "exp_done", l, n - 1))
                for hh in range(2):
                    r = slice(hh * DH, (hh + 1) * DH)
                    o = ps[:, 2 * (n % 2) + hh, :]
                    q = PT[r, qt, i * P:(i + 1) * P]
                    if br == "cmp":
                        mm(o[:, 0:NCP], q, ckP[r, 0, 0:NCP], start=True, stop=True, skip_group_check=True)
                        last = mm(o[:, 0:NCP], identb, mcmpb[:, i * 32:i * 32 + NCP], start=False, stop=True, skip_group_check=True)
                        continue
                    kt = {"sel": SELK, "win": WINK}.get(br) or FXK + idx - 4
                    w = (i + 1) * P
                    mm(o[:, 0:w], q, PT[r, kt, 0:w], start=True, stop=True, skip_group_check=True)
                    if br == "fox":
                        h = 2 * (idx - 4) + hh
                        mm(o[:, 0:w], C("onehot", 4)[:, h * P:(h + 1) * P], ncum[:, 0:w], start=False, stop=True, skip_group_check=True)
                    last = mm(o[:, i * P:w], identb, mcausal, start=False, stop=True, skip_group_check=True)
                last.then_inc(sems["s_ps"], 1)

            def turn(l, n):
                u, i = ITEMS[n]
                idx, br = SOFT[u]
                pe.wait_ge(sems["p_scaled"], at(pe, "p_scaled", l, n + 1))
                if n >= 1:
                    pe.wait_ge(sems["pt_ev_a"], at(pe, "pt_ev_a", l, n))
                    pe.wait_ge(sems["pt_ev_d"], at(pe, "pt_ev_d", l, n))
                for hh in range(2):
                    if br == "cmp":
                        last = tp(ps[0:NCP, 4 + hh, 0:P], Pb[:, n % 2, hh, 0:NCP], P)
                    else:
                        for j in range(i + 1):
                            last = tp(ps[:, 4 + hh, j * P:(j + 1) * P], Pb[:, n % 2, hh, j * P:(j + 1) * P], P)
                    last.then_inc(sems["pt_ps"], 1)
                if i < TT - 1:
                    return

            def values(l, u):
                idx, br = SOFT[u]
                n = u * TT + TT - 1
                pe.wait_ge(sems["pt_ev_a"], at(pe, "pt_ev_a", l, n + 1))
                pe.wait_ge(sems["pt_ev_d"], at(pe, "pt_ev_d", l, n + 1))
                if idx >= 2 and br in ("cmp", "fox"):
                    pe.wait_ge(sems["o_ev"], at(pe, "o_ev", l, idx - 1))
                first, end = br in ("cmp", "fox"), br in ("win", "fox")
                for hh in range(2):
                    r = slice(hh * DH, (hh + 1) * DH)
                    o = ps[r, 6 + idx % 2, :]
                    if br == "cmp":
                        last = mm(o, cvP[0:NCP, r], PTb[0:NCP, hh, 0, :], start=True, stop=True, skip_group_check=True)
                        continue
                    v = {"sel": 0, "win": 1}.get(br)
                    v = 4 + idx - 4 if v is None else v
                    for j in range(TT):
                        last = mm(o[:, j * P:SEQ], vnat[:, v, j, r], PTb[:, hh, j, j * P:SEQ], start=first and j == 0,
                                  stop=True, skip_group_check=True)
                last.then_inc(sems["pv_done"], 1)

            ZO = (0, 512, 1024, 896)

            def stick(l, hd):
                f, hh = hd // 2, hd % 2
                r = slice(hh * DH, (hh + 1) * DH)
                z = ps[:, 3 * (hd % 2):3 * (hd % 2) + 3, :].rearrange("p b c -> p (b c)")
                for j in (0, 1, 3, 2):
                    w = SEQ - j * P
                    mm(z[:, ZO[j]:ZO[j] + w], PT[r, SBK + f, j * P:(j + 1) * P], PT[r, SBQ + f, j * P:SEQ], start=j != 3, stop=True, skip_group_check=True)
                    last = mm(z[:, ZO[j]:ZO[j] + P], identb, mstrict, start=False, stop=True, skip_group_check=True)
                last.then_inc(sems["sbz_ps"], 1)
                pe.wait_ge(sems["sb_sp"], at(pe, "sb_sp", l, hd + 1))
                for j in range(TT):
                    w = SEQ - j * P
                    last = mm(z[:, ZO[j]:ZO[j] + w], C("nupper"), spb[:, ZO[j]:ZO[j] + w], start=False, stop=True, skip_group_check=True)
                    for i in range(j + 1, TT):
                        w = SEQ - i * P
                        o = ZO[j] + (i - j) * P
                        last = mm(z[:, o:o + w], C("nones"), spb[:, ZO[i]:ZO[i] + w], start=False, stop=True, skip_group_check=True)
                last.then_inc(sems["sbc_ps"], 1)
                pe.wait_ge(sems["sb_w"], at(pe, "sb_w", l, hd + 1))
                if hh == 0:
                    pe.wait_ge(sems["o_ev"], at(pe, "o_ev", l, 5 + f))
                for j in range(TT):
                    w = SEQ - j * P
                    last = mm(ps[r, 6 + f, j * P:SEQ], vnat[:, 2 + f, j, r], wb[:, ZO[j]:ZO[j] + w], start=j == 0, stop=True, skip_group_check=True)
                last.then_inc(sems["sb_pv"], 1)

            def prompt(l):
                pe.wait_ge(sems["cum_ev"], at(pe, "cum_ev", l, 1))
                pe.wait_ge(sems["cvt_ev"], at(pe, "cvt_ev", l, 1))
                pe.wait_ge(sems["cvs_ev"], at(pe, "cvs_ev", l, 2))
                scores(l, 0)
                for n in range(len(ITEMS)):
                    if n + 1 < len(ITEMS):
                        scores(l, n + 1)
                    turn(l, n)
                    if ITEMS[n][1] == TT - 1:
                        values(l, ITEMS[n][0])
                for hd in range(4):
                    if hd == 0:
                        pe.wait_ge(sems["exp_done"], at(pe, "exp_done", l, len(ITEMS)))
                        pe.wait_ge(sems["pt_ev_a"], at(pe, "pt_ev_a", l, len(ITEMS)))
                        pe.wait_ge(sems["pt_ev_d"], at(pe, "pt_ev_d", l, len(ITEMS)))
                    stick(l, hd)

            def sample(l):
                pe.wait_ge(sems["q_ev"], at(pe, "q_ev", l, 1))
                pe.wait_ge(sems["o_ev"], at(pe, "o_ev", l, 8))
                for b in range(NS):
                    last = mm(ps[0:64, 3, 64:64 + NCS], qn[:, b, :], ckT[:, b, :], start=b == 0, stop=b == NS - 1)
                last.then_inc(sems["sc_ps"], 1)
                steps, m = [], 0
                for u in UNITS[NS * 2:NKU]:
                    for j in range(KSTEPS[u[0]]):
                        steps.append((u, j))
                first = 4 * NS

                def turn_step(n):
                    u, j = steps[n]
                    s = unit_in(pe, l, u)
                    pe.wait_ge(sems["kt_ev"], at(pe, "kt_ev", l, first + n - 1))
                    bank = ps[:, 6 + n % 2, :]
                    if u[0] == "lf":
                        apart(pe)
                        for h in range(4):
                            last = tp(bank[:, h * 64:(h + 1) * 64], s[0:64, h:512:4], 64)
                    else:
                        v = s.rearrange("p (j c) -> p j c", c={"selk": 128, "wink": 128}.get(u[0], 256))
                        for i in range(4):
                            if u[0] in ("selk", "wink"):
                                last = tp(bank[:, i * P:(i + 1) * P], v[:, 4 * j + i, :], P)
                            else:
                                last = tp(bank[:, i * P:(i + 1) * P], v[:, i, j * P:(j + 1) * P], P)
                    last.then_inc(sems["kt_ps"], 1)

                def score_step(n):
                    nonlocal m
                    (kind, b, h), j = steps[n]
                    pe.wait_ge(sems["kt_ev"], at(pe, "kt_ev", l, first + n + 1))
                    if kind == "lf":
                        return
                    kt = KT[:, m % 2, :]
                    m += 1
                    if kind == "selk":
                        last = mm(ps[0:64, j, :], qn[:, b, :], kt, start=b == 0, stop=b == NS - 1)
                    elif kind == "wink":
                        last = mm(ps[0:64, 2, :], qn[:, b, :], kt, start=b == 0, stop=b == NS - 1)
                    elif kind == "fxk":
                        last = mm(ps[0:32, 4 + h, :], qf[:, j, b, :], kt, start=b == 0 and j == 0, stop=True, skip_group_check=True)
                    else:
                        if b == 0 and h == 0 and j == 0:
                            pe.wait_ge(sems["s_ev"], at(pe, "s_ev", l, 1))
                        last = mm(ps[0:32, h, :], qs[:, j, b, :], kt, start=b == 0 and j == 0, stop=b == NS - 1 and j == 1)
                    last.then_inc(sems["smm"], 1)

                def news(kind):
                    c = {"selk": 0, "wink": 1, "fxk": 2}[kind]
                    if c:
                        pe.wait_ge(sems["s_ev"], at(pe, "s_ev", l, c))
                    else:
                        pe.wait_ge(sems["drop"], at(pe, "drop", l, 1))
                    pts = {"selk": [SELK], "wink": [WINK], "fxk": [FXK, FXK + 1]}[kind]
                    rows = 32 if kind == "fxk" else 64
                    n = 0
                    for b in range(NS):
                        for f, t in enumerate(pts):
                            q = qf[:, f, b, :] if kind == "fxk" else qn[:, b, :]
                            last = mm(ps[0:rows, 3, c:c + 1], q, PT[:, t, SEQ + b:SEQ + b + 1], start=n == 0, stop=n == NS * len(pts) - 1)
                            n += 1
                    last.then_inc(sems["snew"], 1)

                pe.wait_ge(sems["sc_p"], at(pe, "sc_p", l, 1))
                apart(pe)
                mm(ps[0:64, 3, 128:128 + 64], C("group", 64), pc[:, :], start=True, stop=True).then_inc(sems["pg_ps"], 1)
                turn_step(0)
                for n in range(len(steps)):
                    if n + 1 < len(steps):
                        turn_step(n + 1)
                    score_step(n)
                    if n + 1 == len(steps) or steps[n + 1][0][0] != steps[n][0][0]:
                        if steps[n][0][0] in ("selk", "wink", "fxk"):
                            if steps[n][0][0] == "fxk":
                                for j in range(NPG):
                                    for h in range(2):
                                        w = min((j + 1) * P - h * 512, 512)
                                        if w > 0:
                                            a = (7 - j) * P + h * 512
                                            mm(ps[0:32, 4 + h, 0:w], LF[:, j, :, :].rearrange("p b h -> p (b h)"), cum_bwd[:, a:a + w],
                                               start=False, stop=True, skip_group_check=True)
                            news(steps[n][0][0])
                pe.wait_ge(sems["s_ev"], at(pe, "s_ev", l, 4))
                apart(pe)
                for j in range(NPG):
                    last = tp(ps[:, 5, j * 32:(j + 1) * 32], ZS[0:32, j * P:(j + 1) * P], 32)
                last.then_inc(sems["zt_ps"], 1)
                pe.wait_ge(sems["z_sp"], at(pe, "z_sp", l, 1))
                mm(ps[:, 6, 0:256], C("nupper"), zsp[:, :], start=True, stop=True, skip_group_check=True)
                for k in range(1, NPG):
                    last = mm(ps[:, 6, 0:(NPG - k) * 32], C("nones"), zsp[:, k * 32:256], start=False, stop=True, skip_group_check=True)
                last.then_inc(sems["zc_ps"], 1)
                pe.wait_ge(sems["drop"], at(pe, "drop", l, 1))
                apart(pe)
                tp(ps[0:NCS, 7, 0:64], pc[:, 0:NCS], 64).then_inc(sems["sct"], 1)
                pe.wait_ge(sems["s_p"], at(pe, "s_p", l, 1))
                apart(pe)
                for j in range(NPG):
                    last = tp(ps[:, 2, j * 64:(j + 1) * 64], SS[0:64, j * P:(j + 1) * P], 64)
                last.then_inc(sems["ptt_ps"], 1)
                pe.wait_ge(sems["s_p"], at(pe, "s_p", l, 2))
                apart(pe)
                for j in range(4):
                    last = tp(ps[:, 3, j * 64:(j + 1) * 64], SW[0:64, j * P:(j + 1) * P], 64)
                last.then_inc(sems["ptt_ps"], 1)
                pe.wait_ge(sems["s_p"], at(pe, "s_p", l, 3))
                apart(pe)
                for j in range(NPG):
                    last = tp(ps[:, 4, j * 32:(j + 1) * 32], SF[0:32, j * P:(j + 1) * P], 32)
                last.then_inc(sems["ptt_ps"], 1)
                pe.wait_ge(sems["dg"], at(pe, "dg", l, 3))
                pe.wait_ge(sems["sce"], at(pe, "sce", l, 1))
                apart(pe)
                mm(ps[0:NS, 7, 0:64], C("row8", 64), dg[:, 0, :], start=True, stop=True)
                mm(ps[0:NS, 7, 64:128], C("row8", 64), dg[:, 1, :], start=True, stop=True)
                mm(ps[0:NS, 7, 128:160], C("row4", 32), dg[0:32, 2, 0:32], start=True, stop=True).then_inc(sems["dm_ps"], 1)
                pe.wait_ge(sems["ptt_ev"], at(pe, "ptt_ev", l, 3))
                pe.wait_ge(sems["dm_ev"], at(pe, "dm_ev", l, 1))
                sk = dict(skip_group_check=True)
                for f in range(2):
                    mm(ps[:, 1, f * 16:(f + 1) * 16], vnew[:, 4 + f, :],
                       DM[:, 128:160].rearrange("a (b h) -> a b h", h=4)[:, :, 2 * f:2 * f + 2], start=f == 0, stop=True, **sk)
                for b in range(NS):
                    for h in range(2):
                        s = unit_in(pe, l, ("fxv", b, h)).rearrange("p (j c) -> p j c", j=4)
                        for j in range(4):
                            for f in range(2):
                                o = f * 16 + b * 2
                                last = mm(ps[:, 1, o:o + 2], s[:, j, f * P:(f + 1) * P], PTf[:, 4 * h + j, b * 4 + 2 * f:b * 4 + 2 * f + 2],
                                          start=False, stop=True, **sk)
                        last.then_inc(sems["v_used"], 1)
                pe.wait_ge(sems["z_w"], at(pe, "z_w", l, 1))
                for b in range(NS):
                    for h in range(2):
                        s = unit_in(pe, l, ("sbv", b, h)).rearrange("p (j c) -> p j c", j=4)
                        for j in range(4):
                            for f in range(2):
                                o = f * 16 + b * 2
                                last = mm(ps[:, 6, o:o + 2], s[:, j, f * P:(f + 1) * P], zw[:, 4 * h + j, b * 4 + 2 * f:b * 4 + 2 * f + 2],
                                          start=b == 0 and h == 0 and j == 0 and f == 0, stop=True, **sk)
                        last.then_inc(sems["v_used"], 1)
                pe.wait_ge(sems["sce"], at(pe, "sce", l, 1))
                mm(ps[:, 0, 0:64], vnew[:, 0, :], DM[:, 0:64], start=True, stop=True, **sk)
                mm(ps[:, 0, 0:64], vnew[:, 1, :], DM[:, 64:128], start=False, stop=True, **sk)
                for b in range(NS):
                    mm(ps[:, 0, b * 8:(b + 1) * 8], cvS[:, b, :], pcT[0:NCS, b * 8:(b + 1) * 8], start=False, stop=True, **sk)
                for b in range(NS):
                    s = unit_in(pe, l, ("selv", b, 0)).rearrange("p (j c) -> p j c", j=8)
                    for j in range(NPG):
                        last = mm(ps[:, 0, b * 8:(b + 1) * 8], s[:, j, :], PTs[:, j, b * 8:(b + 1) * 8], start=False, stop=True, **sk)
                    last.then_inc(sems["v_used"], 1)
                for b in range(NS):
                    s = unit_in(pe, l, ("winv", b, 0)).rearrange("p (j c) -> p j c", j=8)
                    for j in range(4):
                        last = mm(ps[:, 0, b * 8:(b + 1) * 8], s[:, j, :], PTw[:, j, b * 8:(b + 1) * 8], start=False, stop=True, **sk)
                    last.then_inc(sems["v_used"], 1)

            OT = [[0, 1, 2, 3], [SBQ, SBQ + 1], [FXQ, FXQ + 1]]

            def merge(l):
                pe.wait_ge(sems["so_ev"], at(pe, "so_ev", l, 1))
                n = 0
                for hf in range(2):
                    w = weights_in(pe, l, ("up", hf))
                    for br in range(3):
                        k0 = (0, 4, 6)[br]
                        for c in range(4):
                            if n >= 4:
                                pe.wait_ge(sems["mt_ev"], at(pe, "mt_ev", l, n - 3))
                            tile(2 * (n % 4), [(w[:, (k0 + k) * 512 + c * P:(k0 + k) * 512 + (c + 1) * P], PT[:, t, :]) for k, t in enumerate(OT[br])]
                                 ).then_inc(sems["mt_ps"], 1)
                            n += 1
                    for br in range(3):
                        w = weights_in(pe, l, ("mg", hf, br)).rearrange("p (k n) -> p k n", k=KD)
                        for c in range(4):
                            pe.wait_ge(sems["mt_ev"], at(pe, "mt_ev", l, n - 3))
                            tile(2 * (n % 4), [(w[:, k, c * P:(c + 1) * P], hT[:, k, :]) for k in range(KD)]).then_inc(sems["mt_ps"], 1)
                            n += 1
                for hf in range(2):
                    w = weights_in(pe, l, ("out", hf)).rearrange("p (k n) -> p k n", k=KD)
                    for c in range(4):
                        if n < 52:
                            pe.wait_ge(sems["mt_ev"], at(pe, "mt_ev", l, n - 3))
                        else:
                            pe.wait_ge(sems["x_upd"], at(pe, "x_upd", l, n - 51))
                        if hf == 0 and c == 0:
                            pe.wait_ge(sems["u_ready"], at(pe, "u_ready", l, 8))
                        tile(2 * (n % 4), [(w[:, k, c * P:(c + 1) * P], PT[:, UT[k], :]) for k in range(KD)]).then_inc(sems["mt_ps"], 1)
                        n += 1

            def ffn(l):
                for i in range(NF):
                    w = weights_in(pe, l, ("ffn", i // 2)).rearrange("p (j k n) -> p j k n", j=2, k=KD)
                    c = slice((i % 2) * P, (i % 2 + 1) * P)
                    if i >= 2:
                        pe.wait_ge(sems["ffn_s"], at(pe, "ffn_s", l, i - 1))
                    if i == 0:
                        pe.wait_ge(sems["h_ready"], at(pe, "h_ready", l, 2 * KD))
                    tile(2 * (i % 2), [(w[:, 0, k, c], hT[:, k, :]) for k in range(KD)]).then_inc(sems["ffn_g"], 1)
                    if i >= 2:
                        pe.wait_ge(sems["hid"], at(pe, "hid", l, i - 1))
                    tile(4 + 2 * (i % 2), [(w[:, 1, k, c], hT[:, k, :]) for k in range(KD)]).then_inc(sems["ffn_u"], 1)
                pe.wait_ge(sems["hid"], at(pe, "hid", l, NF))
                for n in range(4):
                    if n >= 2:
                        pe.wait_ge(sems["x_upd"], at(pe, "x_upd", l, KD + 2 * (n - 1)))
                    for h in range(2):
                        w = weights_in(pe, l, ("down", n, h))[:, 0:NF // 2 * 256].rearrange("p (k n) -> p k n", k=NF // 2)
                        for k in range(NF // 2):
                            for c in range(2):
                                for t in range(2):
                                    last = mm(ps[:, 4 * (n % 2) + 2 * c + t, 0:H2], w[:, k, c * P:(c + 1) * P], PT[:, h * (NF // 2) + k, t * H2:(t + 1) * H2],
                                              start=h == 0 and k == 0, stop=h == 1 and k == NF // 2 - 1)
                        last.then_inc(sems["down_ps"], 1)

            with pe.Fori(0, DEPTH) as i:
                l = in_layers(pe, i)
                norm(l, 0)
                project(l)
                cumulate(l)
                compress(l)
                prompt(l)
                sample(l)
                merge(l)
                norm(l, 1)
                ffn(l)
            norm(DEPTH, 0)
            for k in range(KD):
                pe.wait_ge(sems["h_ready"], at(pe, "h_ready", DEPTH, k + 1))
                if k >= 2:
                    pe.wait_ge(sems["y_ev"], k - 1)
                for t in range(TT):
                    tp(ps[:, 4 + 2 * (k % 2), t * P:(t + 1) * P], hT[:, k, t * P:(t + 1) * P], P)
                tp(ps[0:NS, 5 + 2 * (k % 2), 0:P], hT[:, k, SEQ:T], P).then_inc(sems["y_ps"], 1)

        @block.scalar
        def _(act):
            fn = nc.scalar.activation
            act.wait_ge(sems["const_ok"], 1)
            act.wait_ge(sems["init_z"], 2)

            def norm(l, w):
                for k in range(KD):
                    act.wait_ge(sems["x_upd"], at(act, "x_upd", l, k + 1)) if w else act.wait_ge(sems["x_upd"], count(act, l, PER["x_upd"], k + 1))
                    if k >= 2:
                        act.wait_ge(sems["sq_used"], at(act, "sq_used", l, w * KD + k - 1))
                    fn(sq[:, k % 2, :], xT[:, k, :], ACT.Square).then_inc(sems["sq_ready"], 1)
                act.wait_ge(sems["sq_used"], at(act, "sq_used", l, (w + 1) * KD))
                fn(half(rs), pair(0), ACT.Sqrt, bias=epsb[:, 0:1], scale=1.0 / D).then_inc(sems["rs_ready"], 1)

            def project(l):
                rows = lambda a: a.rearrange("p (t c) -> p t c", t=TT)
                names = {CMPK: ("cmp", 0), CMPV: ("cmp", P), SELK: ("sel", 0), SELV: ("sel", P), WINK: ("win", 0), WINV: ("win", P),
                         SBK: ("sb", 0), SBK + 1: ("sb", P), SBV: ("sb", 256), SBV + 1: ("sb", 256 + P),
                         FXK: ("fox", 0), FXK + 1: ("fox", P), FXV: ("fox", 256), FXV + 1: ("fox", 256 + P)}

                def store(n):
                    t = NAT[n]
                    act.wait_ge(sems["nat_ev"], at(act, "nat_ev", l, n + 1))
                    src = vnat[:, NATV.index(t), :, :] if t in NATV else rows(knat[:, NATK.index(t), :])
                    name, c0 = names[t]
                    dst = out["p_" + name].rearrange("l a (t p) k h d -> (l a) p t (k h d)", p=P)[dl[0]][:, :, c0:c0 + P]
                    act.dma_start(dst, src).then_inc(sems["out_dma"], 16)

                def store_new(n):
                    name, c0 = names[NAT[n]]
                    if name == "win":
                        dst = out["s_win"].rearrange("l b r k h d -> l b r (k h d)")[dl[0]][:, WIN - 1, c0:c0 + P]
                    else:
                        dst = out["s_" + name].rearrange("l b s k h d -> l (b s) (k h d)")[dl[0]][:, c0:c0 + P]
                    act.dma_start(dst, natS[0:NS, n, :]).then_inc(sems["out_dma"], 16)

                stored = 0
                for i in range(NT):
                    act.wait_ge(sems["proj_ps"], at(act, "proj_ps", l, i + 1))
                    fn(half(PT[:, i, :]), pair(2 * (i % 2)), ACT.Copy, scale=SCALE if i in QTILES else 1.0).then_inc(sems["proj_ev"], 1)
                    while stored < len(NAT) and NAT[stored] <= i - 4:
                        store(stored)
                        stored += 1
                while stored < len(NAT):
                    store(stored)
                    stored += 1
                act.wait_ge(sems["new_ev"], at(act, "new_ev", l, 1))
                for n in range(len(NAT)):
                    store_new(n)
                act.wait_ge(sems["gate_ev"], at(act, "gate_ev", l, 1))
                fn(gnat[:, :, 0:24], gnat[:, :, 0:24], ACT.Sigmoid)
                fn(gsmp[:, 0:24], gsmp[:, 0:24], ACT.Sigmoid).then_inc(sems["gate_sig"], 1)
                fn(lft[:, :, :], lfn[:, :, :], ACT.Abs)
                fn(lfst[:, :], lfs[:, :], ACT.Abs).then_inc(sems["lf_abs"], 1)
                act.wait_ge(sems["lf_abs"], at(act, "lf_abs", l, 1))
                link(fn(lft[:, :, :], lft[:, :, :], ACT.Exp, scale=-1.0))
                link(fn(lfst[:, :], lfst[:, :], ACT.Exp, scale=-1.0))
                fn(lft[:, :, :], lft[:, :, :], ACT.Ln, bias=1.0)
                fn(lfst[:, :], lfst[:, :], ACT.Ln, bias=1.0).then_inc(sems["lf_ln"], 1)
                act.wait_ge(sems["lf_done"], at(act, "lf_done", l, 1))
                with nc.allow_non_contiguous_dma(reason="gates and log-forget values: a few kilobytes"):
                    act.dma_start(out["p_logf"].rearrange("l a (t p) h -> (l a) p t h", p=P)[dl[0]], lfn[:, :, :]).then_inc(sems["out_dma"], 16)
                    act.dma_start(out["s_logf"].rearrange("l b s h -> l (b s) h")[dl[0]], lfs[:, :]).then_inc(sems["out_dma"], 16)
                    act.wait_ge(sems["gate_sig"], at(act, "gate_sig", l, 1))
                    act.dma_start(g64[:, :], gsmp[:, 0:24]).then_inc(sems["sig_dma"], 16)
                    act.dma_start(l32[:, :], lfs[:, :]).then_inc(sems["sig_dma"], 16)
                act.wait_ge(sems["sig_dma"], at(act, "sig_dma", l, 32))
                act.wait_ge(sems["out_dma"], at(act, "out_dma", l, PER["out_dma"]))
                act.sem_inc(sems["new_ready"], 1)

            acts, layer, dl = [0], [0], [0]

            def link(ins):
                acts[0] += 1
                ins.then_inc(sems["act_chain"], 1)
                act.wait_ge(sems["act_chain"], count(act, layer[0], ACT_CHAIN, acts[0]))

            def prompt(l):
                def expo(n):
                    u, i = ITEMS[n]
                    br = SOFT[u][1]
                    w = NCP if br == "cmp" else (i + 1) * P
                    act.wait_ge(sems["nm_ready"], at(act, "nm_ready", l, n + 1))
                    if n >= 2:
                        act.wait_ge(sems["pt_ps"], at(act, "pt_ps", l, 2 * (n - 1)))
                    for hh in range(2):
                        last = fn(Pb[:, n % 2, hh, 0:w], ps[:, 2 * (n % 2) + hh, 0:w], ACT.Exp, bias=nm[:, n % 2, hh:hh + 1],
                                  accum_out=sm[:, n % 2, hh:hh + 1])
                    last.then_inc(sems["exp_done"], 1)

                expo(0)
                for n, (u, i) in enumerate(ITEMS):
                    if n + 1 < len(ITEMS):
                        expo(n + 1)
                    idx, br = SOFT[u]
                    act.wait_ge(sems["pt_ps"], at(act, "pt_ps", l, 2 * n + 1))
                    if i == 0 and u >= 1:
                        act.wait_ge(sems["pv_done"], at(act, "pv_done", l, u))
                    if br == "cmp":
                        fn(PTb[0:NCP, 0, 0, i * P:(i + 1) * P], ps[0:NCP, 4, 0:P], ACT.Copy).then_inc(sems["pt_ev_a"], 1)
                    else:
                        fn(PTb[:, 0, 0:i + 1, i * P:(i + 1) * P], ps[:, 4, 0:(i + 1) * P].rearrange("p (j c) -> p j c", c=P), ACT.Copy
                           ).then_inc(sems["pt_ev_a"], 1)
                    if i == TT - 1 and br in ("win", "fox"):
                        act.wait_ge(sems["pv_done"], at(act, "pv_done", l, u + 1))
                        fn(PT[:, idx if idx < 4 else FXQ + idx - 4, 0:SEQ], ps[:, 6 + idx % 2, :], ACT.Copy).then_inc(sems["o_ev"], 1)
                for hd in range(4):
                    z = ps[:, 3 * (hd % 2):3 * (hd % 2) + 3, :].rearrange("p b c -> p (b c)")[:, 0:1280]
                    act.wait_ge(sems["sbz_ps"], at(act, "sbz_ps", l, hd + 1))
                    if hd == 0:
                        act.wait_ge(sems["pv_done"], at(act, "pv_done", l, len(SOFT)))
                    else:
                        act.wait_ge(sems["sb_sp"], at(act, "sb_sp", l, hd))
                    link(fn(zt, z, ACT.Abs))
                    link(fn(zt, zt, ACT.Exp, scale=-1.0))
                    fn(zt, zt, ACT.Ln, bias=1.0).then_inc(sems["sb_ln"], 1)
                    act.wait_ge(sems["sbc_ps"], at(act, "sbc_ps", l, hd + 1))
                    if hd:
                        act.wait_ge(sems["sb_pv"], at(act, "sb_pv", l, hd))
                    fn(wb, z, ACT.Exp).then_inc(sems["sb_w"], 1)
                    if hd % 2:
                        act.wait_ge(sems["sb_pv"], at(act, "sb_pv", l, hd + 1))
                        fn(PT[:, SBQ + hd // 2, 0:SEQ], ps[:, 6 + hd // 2, :], ACT.Copy).then_inc(sems["o_ev"], 1)

            def sample(l):
                act.wait_ge(sems["sc_nm"], at(act, "sc_nm", l, 1))
                fn(pc[:, 0:NCS], ps[0:64, 3, 64:64 + NCS], ACT.Exp, bias=s1[:, 0:1], accum_out=s1[:, 1:2]).then_inc(sems["sc_exp"], 1)
                for i, (S, rows, n) in enumerate(((SS, 64, 1025), (SW, 64, 513), (SF, 32, 1025))):
                    act.wait_ge(sems["s_nm"], at(act, "s_nm", l, i + 1))
                    fn(S[0:rows], S[0:rows], ACT.Exp, bias=s1[0:rows, 4 + 4 * i:5 + 4 * i], accum_out=s1[0:rows, 5 + 4 * i:6 + 4 * i]).then_inc(sems["s_exp"], 1)
                act.wait_ge(sems["zt_ps"], at(act, "zt_ps", l, 1))
                link(fn(za, ps[:, 5, 0:256], ACT.Abs))
                link(fn(za, za, ACT.Exp, scale=-1.0))
                fn(za, za, ACT.Ln, bias=1.0).then_inc(sems["z_abs"], 1)
                act.wait_ge(sems["z_sum"], at(act, "z_sum", l, 1))
                fn(zw[:, :, :].rearrange("p j c -> p (j c)"), za, ACT.Exp).then_inc(sems["z_w"], 1)

            def merge(l):
                for n in range(48):
                    act.wait_ge(sems["mt_ps"], at(act, "mt_ps", l, n + 1))
                    hf, m = n // 24, n % 24
                    if m < 12:
                        if n >= 24:
                            act.wait_ge(sems["u_ready"], at(act, "u_ready", l, 4))
                        fn(half(UP[:, m, :]), pair(2 * (n % 4)), ACT.Copy).then_inc(sems["mt_ev"], 1)
                    else:
                        k = 12 * hf + m - 12
                        if k >= 2:
                            act.wait_ge(sems["mul"], at(act, "mul", l, k - 1))
                        fn(half(sg[k % 2]), pair(2 * (n % 4)), ACT.Sigmoid).then_inc(sems["mt_ev"], 1)

            def ffn(l):
                for i in range(NF):
                    act.wait_ge(sems["ffn_g"], at(act, "ffn_g", l, i + 1))
                    if i >= 2:
                        act.wait_ge(sems["hid"], at(act, "hid", l, i - 1))
                    fn(half(fs[:, i % 2, :]), pair(2 * (i % 2)), ACT.Silu).then_inc(sems["ffn_s"], 1)

            with act.Fori(0, DEPTH) as i:
                dl[0] = i
                l = layer[0] = in_layers(act, i)
                norm(l, 0)
                project(l)
                prompt(l)
                sample(l)
                merge(l)
                norm(l, 1)
                ffn(l)
            assert acts[0] == ACT_CHAIN, acts
            norm(DEPTH, 0)
            act.wait_ge(sems["y_ev"], KD)
            act.dma_start(out["y_prompt"][0].rearrange("(t p) d -> p t d", p=P), PT[:, 0:8, :].rearrange("p a b -> p (a b)")[:, 0:4096]
                          .rearrange("p (t d) -> p t d", t=TT)).then_inc(sems["y_dma"], 16)
            act.dma_start(out["y_sample"].rearrange("b s d -> (b s) d"), PT[0:NS, 8:10, :].rearrange("p a b -> p (a b)")[:, 0:D]).then_inc(sems["y_dma"], 16)
            act.wait_ge(sems["y_dma"], 32)
            act.wait_ge(sems["out_dma"], DEPTH * PER["out_dma"])

        @block.vector
        def _(dve):
            v = nc.vector
            chain, layer = [0], [0]

            def link(ins):
                chain[0] += 1
                ins.then_inc(sems["dve_chain"], 1)
                dve.wait_ge(sems["dve_chain"], count(dve, layer[0], DVE_CHAIN, chain[0]))

            def own(ins, name, l, n):
                ins.then_inc(sems[name], 1)
                dve.wait_ge(sems[name], at(dve, name, l, n))

            dve.wait_ge(sems["const_in"], 16 * 12)
            v.memset(epsb[:, :], EPS)
            v.tensor_copy(identb, ident)
            last = v.tensor_copy(maskb[:, P:4 * P], hT[:, :, :].rearrange("p a b -> p (a b)")[:, 0:3 * P])
            last.then_inc(sems["const_ok"], 1)
            for b in (qn[:, :, :], qs[:, :, :, :], qf[:, :, :, :], pc[:, :], pgb[:, :]):
                last = v.memset(b, 0.0)
            last.then_inc(sems["init_z"], 1)
            dve.wait_ge(sems["init_z"], 1)
            for k in range(KD):
                dve.wait_ge(sems["xt_ps"], k + 1)
                v.tensor_copy(xT[:, k, 0:SEQ], ps[:, 2 * (k % 2), :])
                v.tensor_copy(xT[:, k, SEQ:T], ps[:, 2 * (k % 2) + 1, 0:NS]).then_inc(sems["x_upd"], 1)
            dve.wait_ge(sems["post_ps"], 1)
            v.tensor_copy(posT[:, :, :], ps[:, 4, 0:DEPTH * CBLK].rearrange("p (l c) -> p l c", l=DEPTH)).then_inc(sems["init_z"], 1)
            dve.wait_ge(sems["init_z"], 2)

            def norm(l, w, g):
                dve.wait_ge(sems["rs_ready"], at(dve, "rs_ready", l, w + 1))
                link(v.reciprocal(rinv, rs))
                if w:
                    dve.wait_ge(sems["mt_ps"], at(dve, "mt_ps", l, 48))
                for k in range(KD):
                    v.scalar_tensor_tensor(hT[:, k, :], xT[:, k, :], g(k), rinv, ALU.mult, ALU.mult).then_inc(sems["h_ready"], 1)

            def project(l):
                def rope(i):
                    r = ROPE.index(i)
                    dve.wait_ge(sems["proj_ev"], at(dve, "proj_ev", l, i + 1))
                    dve.wait_ge(sems["rot_ps"], at(dve, "rot_ps", l, r + 1))
                    v.tensor_tensor(half(ropet), pair(4), half(C("sin")), ALU.mult)
                    link(v.tensor_tensor(PT[:, i, :], PT[:, i, :], C("cos"), ALU.mult))
                    v.tensor_tensor(PT[:, i, :], PT[:, i, :], ropet, ALU.add).then_inc(sems["rope_done"], 1)

                def nat(i):
                    n = NAT.index(i)
                    dve.wait_ge(sems["nat_ps"], at(dve, "nat_ps", l, n + 1))
                    dst = vnat[:, NATV.index(i), :, :].rearrange("p t c -> p (t c)") if i in NATV else knat[:, NATK.index(i), :]
                    v.tensor_copy(dst, ps[:, 6 + n % 2, :]).then_inc(sems["nat_ev"], 1)

                for i in range(NT + 2):
                    if i == WINK:
                        dve.wait_ge(sems["gate_ps"], at(dve, "gate_ps", l, 1))
                        v.tensor_copy(gnat[:, :, :], ps[:, 5, 264:264 + 28 * TT].rearrange("p (t c) -> p t c", t=TT))
                        link(v.tensor_copy(gsmp[:, :], ps[0:NS, 4, 264:292]))
                        b = bfl[:, :]
                        v.tensor_tensor(lfn[:, :, :], gnat[:, :, 24:28], b.rearrange("p (a h) -> p a h", a=1).broadcast_to([P, TT, 4]), ALU.add)
                        v.tensor_tensor(lfs[:, :], gsmp[:, 24:28], b[0:NS, :], ALU.add).then_inc(sems["gate_ev"], 1)
                    if i < NT and i in ROPE:
                        rope(i)
                    if i - 1 in NAT:
                        nat(i - 1)
                dve.wait_ge(sems["new_ps"], at(dve, "new_ps", l, 1))
                for n in range(0, len(NAT), 4):
                    w = min(4, len(NAT) - n)
                    last = v.tensor_copy(natS[0:NS, n:n + w, :].rearrange("p a b -> p (a b)"), ps[0:NS, n // 4, 0:w * P])
                last.then_inc(sems["new_ev"], 1)
                dve.wait_ge(sems["new_ev"], at(dve, "new_ev", l, 1))
                for i, t in enumerate(NATV):
                    v.tensor_copy(vnew[:, i, :], natS[0:NS, NAT.index(t), :])
                dve.wait_ge(sems["gate_ev"], at(dve, "gate_ev", l, 1))
                dve.wait_ge(sems["lf_ln"], at(dve, "lf_ln", l, 1))
                v.scalar_tensor_tensor(lfn[:, :, :], lfn[:, :, :], 0.0, lft[:, :, :], ALU.min, ALU.subtract)
                v.scalar_tensor_tensor(lfs[:, :], lfs[:, :], 0.0, lfst[:, :], ALU.min, ALU.subtract).then_inc(sems["lf_done"], 1)
                for g in range(G):
                    r = slice(g * DH, (g + 1) * DH)
                    dst = qn[r, :, :].rearrange("p b c -> p (b c)")
                    for t in range(4):
                        v.tensor_copy(dst[:, g * 4 + t:g * 4 + t + 72 * 7 + 1:72], PT[r, t, SEQ:T])
                    for f in range(2):
                        c = 2 * f + g
                        v.tensor_copy(qs[r, f, :, :].rearrange("p b c -> p (b c)")[:, c:c + 36 * 7 + 1:36], PT[r, SBQ + f, SEQ:T])
                        last = v.tensor_copy(qf[r, f, :, :].rearrange("p b c -> p (b c)")[:, c:c + 36 * 7 + 1:36], PT[r, FXQ + f, SEQ:T])
                last.then_inc(sems["q_ev"], 1)
                dve.wait_ge(sems["cum_ps"], at(dve, "cum_ps", l, 1))
                v.tensor_scalar(ncum[:, :], ps[0:4, 4, :], -1.0, None, ALU.mult).then_inc(sems["cum_ev"], 1)

            def compress(l):
                dve.wait_ge(sems["ck_ps"], at(dve, "ck_ps", l, 1))
                link(v.tensor_copy(cbias[:, :], ps[:, 2:4, 64]))
                for j in range(2):
                    last = v.tensor_scalar(ckP[:, j, 0:NCP], ps[:, 2 + j, 0:NCP], cbias[:, j:j + 1], None, ALU.add)
                last.then_inc(sems["ck_ev"], 1)
                dve.wait_ge(sems["cvt_ps"], at(dve, "cvt_ps", l, 1))
                v.tensor_copy(cvP[0:NCP, :], ps[0:NCP, 1, 0:P]).then_inc(sems["cvt_ev"], 1)
                step = 0
                dve.wait_ge(sems["new_ready"], at(dve, "new_ready", l, 1))
                for q in range(4):
                    if q:
                        dve.wait_ge(sems["cs_ps"], at(dve, "cs_ps", l, q))
                    for u in range(4):
                        for kv in range(2):
                            dve.wait_ge(sems["kt_ps"], at(dve, "kt_ps", l, step + 1))
                            v.tensor_copy(KC[:, kv, u // 2, (u % 2) * 512:(u % 2 + 1) * 512], ps[:, 6 + step % 2, :]).then_inc(sems["kt_ev"], 1)
                            step += 1
                    dve.wait_ge(sems["cs_ps"], at(dve, "cs_ps", l, q + 1))
                    v.tensor_scalar(ckT[:, 2 * q:2 * q + 2, :].rearrange("p b n -> p (b n)"), ps[:, 4, 0:2 * NCS], cbias[:, 0:1], None, ALU.add)
                    v.tensor_scalar(cvT[:, :, :].rearrange("p b n -> p (b n)"), ps[:, 5, 0:2 * NCS], cbias[:, 1:2], None, ALU.add).then_inc(sems["cs_ev"], 1)
                    if q % 2:
                        dve.wait_ge(sems["cvs_ps"], at(dve, "cvs_ps", l, q // 2 + 1))
                        v.tensor_copy(cvS[:, 2 * q - 2:2 * q + 2, :].rearrange("p b n -> p (b n)"), ps[0:NCS, 0, :]).then_inc(sems["cvs_ev"], 1)

            def prompt(l):
                def maxima(n):
                    u, i = ITEMS[n]
                    w = NCP if SOFT[u][1] == "cmp" else (i + 1) * P
                    dve.wait_ge(sems["s_ps"], at(dve, "s_ps", l, n + 1))
                    v.tensor_reduce(nm[:, n % 2, :], ps[:, 2 * (n % 2):2 * (n % 2) + 2, 0:w], AX.X, ALU.max, negate=True).then_inc(sems["nm_ready"], 1)

                dve.wait_ge(sems["sig_dma"], at(dve, "sig_dma", l, 32))
                maxima(0)
                for n, (u, i) in enumerate(ITEMS):
                    if n + 1 < len(ITEMS):
                        maxima(n + 1)
                    idx, br = SOFT[u]
                    b = n % 2
                    w = NCP if br == "cmp" else (i + 1) * P
                    dve.wait_ge(sems["exp_done"], at(dve, "exp_done", l, n + 1))
                    if br == "cmp":
                        m = CONST["cmp01"][0] + i * 32
                        link(v.tensor_tensor(Pb[:, b, :, 0:w], Pb[:, b, :, 0:w],
                                             cst[:, m:m + w].rearrange("p (a c) -> p a c", a=1).broadcast_to([P, 2, w]), ALU.mult))
                        link(v.reduce_sum(sm[:, b, :], Pb[:, b, :, 0:w], AX.X))
                    link(v.tensor_scalar(rr[:, b, :], sm[:, b, :], 1e-30, None, ALU.max))
                    link(v.reciprocal(rr[:, b, :], rr[:, b, :]))
                    if br != "fox":
                        c = idx * 3 + ("cmp", "sel", "win").index(br)
                        link(v.tensor_tensor(rr[:, b, :], rr[:, b, :], gnat[:, i, c:c + 13:12], ALU.mult))
                    for hh in range(2):
                        last = v.tensor_scalar(Pb[:, b, hh, 0:w], Pb[:, b, hh, 0:w], rr[:, b, hh:hh + 1], None, ALU.mult)
                    last.then_inc(sems["p_scaled"], 1)
                    dve.wait_ge(sems["pt_ps"], at(dve, "pt_ps", l, 2 * n + 2))
                    if i == 0 and u >= 1:
                        dve.wait_ge(sems["pv_done"], at(dve, "pv_done", l, u))
                    if br == "cmp":
                        v.tensor_copy(PTb[0:NCP, 1, 0, i * P:(i + 1) * P], ps[0:NCP, 5, 0:P]).then_inc(sems["pt_ev_d"], 1)
                    else:
                        v.tensor_copy(PTb[:, 1, 0:i + 1, i * P:(i + 1) * P], ps[:, 5, 0:(i + 1) * P].rearrange("p (j c) -> p j c", c=P)
                                      ).then_inc(sems["pt_ev_d"], 1)
                for hd in range(4):
                    z = ps[:, 3 * (hd % 2):3 * (hd % 2) + 3, :].rearrange("p b c -> p (b c)")[:, 0:1280]
                    dve.wait_ge(sems["sb_ln"], at(dve, "sb_ln", l, hd + 1))
                    if hd:
                        dve.wait_ge(sems["sbc_ps"], at(dve, "sbc_ps", l, hd))
                    v.scalar_tensor_tensor(spb, z, 0.0, zt, ALU.max, ALU.add).then_inc(sems["sb_sp"], 1)

            def sample(l):
                dve.wait_ge(sems["sc_ps"], at(dve, "sc_ps", l, 1))
                v.tensor_reduce(s1[:, 0:1], ps[0:64, 3, 64:64 + NCS], AX.X, ALU.max, negate=True).then_inc(sems["sc_nm"], 1)
                dve.wait_ge(sems["sc_exp"], at(dve, "sc_exp", l, 1))
                link(v.tensor_scalar(s1[:, 2:3], s1[:, 1:2], 1e-30, None, ALU.max))
                link(v.reciprocal(s1[:, 2:3], s1[:, 2:3]))
                v.tensor_scalar(pc[:, 0:NCS], pc[:, 0:NCS], s1[:, 2:3], None, ALU.mult).then_inc(sems["sc_p"], 1)
                dve.wait_ge(sems["pg_ps"], at(dve, "pg_ps", l, 1))
                link(v.tensor_copy(pgb[:, 1:65], ps[0:64, 3, 128:192]))
                nb = NBLK
                link(v.tensor_tensor(dg[:, 0, :], pgb[:, 0:64], pgb[:, 1:65], ALU.add))
                link(v.reduce_sum(t17[:, 0, 0:nb], dg[:, 0, :].rearrange("p (b c) -> p b c", c=4), AX.X))
                imp = t17[:, 0, 1:nb - 1]
                link(v.tensor_reduce(s1[:, 3:4], imp, AX.X, ALU.min))
                link(v.tensor_scalar(t17[:, 1, 1:nb - 1], imp, s1[:, 3:4], None, ALU.is_le))
                link(v.tensor_tensor(t17[:, 1, 1:nb - 1], t17[:, 1, 1:nb - 1], C("blk", 64), ALU.mult))
                link(v.tensor_reduce(s1[:, 3:4], t17[:, 1, 1:nb - 1], AX.X, ALU.max))
                v.memset(t17[:, 2, 0:nb], 0.0)
                link(v.memset(t17[:, 3, 0:nb], 0.0))
                link(v.tensor_scalar(t17[:, 2, 1:nb - 1], C("blk", 64), s1[:, 3:4], NEG, ALU.is_equal, ALU.mult))
                own(v.tensor_scalar(pc[:, 0:NCS], pc[:, 0:NCS], g64[:, 0:1], None, ALU.mult), "drop", l, 1)

                steps = [(u, j) for u in UNITS[NS * 2:NKU] for j in range(KSTEPS[u[0]])]
                first, m = 4 * NS, 0

                def soft(i, S, rows, n):
                    c = 4 + 4 * i
                    v.tensor_reduce(s1[0:rows, c:c + 1], S[0:rows], AX.X, ALU.max, negate=True).then_inc(sems["s_nm"], 1)
                    dve.wait_ge(sems["s_exp"], at(dve, "s_exp", l, i + 1))
                    link(v.reciprocal(s1[0:rows, c + 2:c + 3], s1[0:rows, c + 1:c + 2]))
                    if i < 2:
                        link(v.tensor_tensor(s1[0:rows, c + 2:c + 3], s1[0:rows, c + 2:c + 3], g64[:, i + 1:i + 2], ALU.mult))
                    own(v.tensor_scalar(S[0:rows], S[0:rows], s1[0:rows, c + 2:c + 3], None, ALU.mult), "s_p", l, i + 1)
                    v.tensor_scalar(dg[0:rows, i, 0:rows], ident[0:rows, 0:rows], S[0:rows, n:n + 1], None, ALU.mult).then_inc(sems["dg"], 1)

                for n, ((kind, b, h), j) in enumerate(steps):
                    dve.wait_ge(sems["kt_ps"], at(dve, "kt_ps", l, first + n + 1))
                    if kind == "lf":
                        for hh in range(4):
                            last = v.tensor_copy(LF[:, :, :, hh], ps[:, 6 + n % 2, hh * 64:(hh + 1) * 64].rearrange("p (b j) -> p j b", b=NS))
                        last.then_inc(sems["kt_ev"], 1)
                        continue
                    if m >= 2:
                        dve.wait_ge(sems["smm"], at(dve, "smm", l, m - 1))
                    v.tensor_copy(KT[:, m % 2, :], ps[:, 6 + n % 2, :]).then_inc(sems["kt_ev"], 1)
                    m += 1
                    if n == 17:
                        dve.wait_ge(sems["snew"], at(dve, "snew", l, 1))
                        v.tensor_copy(SS[0:64, 1024:1025], ps[0:64, 3, 0:1])
                        own(v.tensor_tensor(SS[0:64, 0:1024].rearrange("p (b c) -> p b c", c=64),
                                            ps[0:64, 0:2, :].rearrange("p a (b c) -> p (a b) c", c=64),
                                            t17[:, 2, 0:nb].rearrange("p (b a) -> p b a", a=1).broadcast_to([64, nb, 64]), ALU.add), "s_ev", l, 1)
                        soft(0, SS, 64, 1024)
                    if n == 26:
                        dve.wait_ge(sems["snew"], at(dve, "snew", l, 2))
                        v.tensor_copy(SW[0:64, 0:512], ps[0:64, 2, :])
                        own(v.tensor_copy(SW[0:64, 512:513], ps[0:64, 3, 1:2]), "s_ev", l, 2)
                        soft(1, SW, 64, 512)
                    if n == 58:
                        dve.wait_ge(sems["snew"], at(dve, "snew", l, 3))
                        v.tensor_scalar(SF[0:32, 0:1024], ps[0:32, 4:6, :].rearrange("p a c -> p (a c)"), l32[:, 0:1], None, ALU.add)
                        own(v.tensor_copy(SF[0:32, 1024:1025], ps[0:32, 3, 2:3]), "s_ev", l, 3)
                        soft(2, SF, 32, 1024)
                dve.wait_ge(sems["smm"], at(dve, "smm", l, m))
                v.tensor_copy(ZS[0:32, :], ps[0:32, 0:2, :].rearrange("p a c -> p (a c)")).then_inc(sems["s_ev"], 1)
                dve.wait_ge(sems["z_abs"], at(dve, "z_abs", l, 1))
                own(v.scalar_tensor_tensor(zsp, ps[:, 5, 0:256], 0.0, za, ALU.max, ALU.add), "z_sp", l, 1)
                dve.wait_ge(sems["zc_ps"], at(dve, "zc_ps", l, 1))
                link(v.tensor_copy(za, ps[:, 6, 0:256]))
                own(v.tensor_tensor(za, za, ps[:, 5, 0:256], ALU.add), "z_sum", l, 1)
                dve.wait_ge(sems["sct"], at(dve, "sct", l, 1))
                v.tensor_copy(pcT[0:NCS, :], ps[0:NCS, 7, 0:64]).then_inc(sems["sce"], 1)
                dve.wait_ge(sems["ptt_ps"], at(dve, "ptt_ps", l, 1))
                v.tensor_copy(PTs[:, :, :].rearrange("p j c -> p (j c)"), ps[:, 2, :]).then_inc(sems["ptt_ev"], 1)
                dve.wait_ge(sems["ptt_ps"], at(dve, "ptt_ps", l, 2))
                v.tensor_copy(PTw[:, :, :].rearrange("p j c -> p (j c)"), ps[:, 3, 0:256]).then_inc(sems["ptt_ev"], 1)
                dve.wait_ge(sems["ptt_ps"], at(dve, "ptt_ps", l, 3))
                v.tensor_copy(PTf[:, :, :].rearrange("p j c -> p (j c)"), ps[:, 4, 0:256]).then_inc(sems["ptt_ev"], 1)
                dve.wait_ge(sems["dm_ps"], at(dve, "dm_ps", l, 1))
                v.tensor_copy(DM[:, :], ps[0:NS, 7, 0:160]).then_inc(sems["dm_ev"], 1)
                dve.wait_ge(sems["v_used"], at(dve, "v_used", l, NU - NKU))
                for g in range(G):
                    r = slice(g * DH, (g + 1) * DH)
                    for t in range(4):
                        v.tensor_copy(PT[r, t, SEQ:T], ps[r, 0, g * 4 + t:g * 4 + t + 57:8])
                    for f in range(2):
                        v.tensor_copy(PT[r, FXQ + f, SEQ:T], ps[r, 1, f * 16 + g:f * 16 + g + 15:2])
                        last = v.tensor_copy(PT[r, SBQ + f, SEQ:T], ps[r, 6, f * 16 + g:f * 16 + g + 15:2])
                last.then_inc(sems["so_ev"], 1)

            def merge(l):
                for k in range(24):
                    hf, br, c = k // 12, k % 12 // 4, k % 4
                    dve.wait_ge(sems["mt_ev"], at(dve, "mt_ev", l, 24 * hf + 12 + k % 12 + 1))
                    u = PT[:, UT[4 * hf + c], :]
                    if br == 0:
                        v.tensor_tensor(u, sg[k % 2], UP[:, 4 * br + c, :], ALU.mult).then_inc(sems["mul"], 1)
                        continue
                    own(v.tensor_tensor(UP[:, 4 * br + c, :], sg[k % 2], UP[:, 4 * br + c, :], ALU.mult), "mul", l, k + 1)
                    if br == 1:
                        link(v.tensor_tensor(u, u, UP[:, 4 * br + c, :], ALU.add))
                    else:
                        v.tensor_tensor(u, u, UP[:, 4 * br + c, :], ALU.add).then_inc(sems["u_ready"], 1)
                for n in range(8):
                    dve.wait_ge(sems["mt_ps"], at(dve, "mt_ps", l, 48 + n + 1))
                    v.tensor_tensor(half(xT[:, n, :]), half(xT[:, n, :]), pair(2 * (n % 4)), ALU.add).then_inc(sems["x_upd"], 1)

            def ffn(l):
                for i in range(NF):
                    dve.wait_ge(sems["ffn_s"], at(dve, "ffn_s", l, i + 1))
                    dve.wait_ge(sems["ffn_u"], at(dve, "ffn_u", l, i + 1))
                    v.tensor_tensor(half(PT[:, i, :]), half(fs[:, i % 2, :]), pair(4 + 2 * (i % 2)), ALU.mult).then_inc(sems["hid"], 1)
                for n in range(4):
                    dve.wait_ge(sems["down_ps"], at(dve, "down_ps", l, 2 * n + 2))
                    for c in range(2):
                        v.tensor_tensor(half(xT[:, 2 * n + c, :]), half(xT[:, 2 * n + c, :]), pair(4 * (n % 2) + 2 * c), ALU.add).then_inc(sems["x_upd"], 1)

            with dve.Fori(0, DEPTH) as i:
                l = layer[0] = in_layers(dve, i)
                v.tensor_copy(gl[:, :, :], gam[:, bass.ds(2 * i, 2), :])
                v.tensor_copy(posL[:, :], posT[:, bass.ds(i, 1), :].rearrange("p a c -> p (a c)"))
                link(v.tensor_copy(bfl[:, :], bfb[:, bass.ds(i, 1), :].rearrange("p a c -> p (a c)")))
                norm(l, 0, lambda k: gl[:, 0, k:k + 1])
                project(l)
                compress(l)
                prompt(l)
                sample(l)
                merge(l)
                norm(l, 1, lambda k: gl[:, 1, k:k + 1])
                ffn(l)
            assert chain[0] == DVE_CHAIN, chain
            layer[0] = DEPTH
            chain[0] = 0
            norm(DEPTH, 0, lambda k: gam[:, 2 * DEPTH, k:k + 1])
            yp = PT[:, 0:8, :].rearrange("p a b -> p (a b)")[:, 0:4096].rearrange("p (t d) -> p t d", t=TT)
            ysm = PT[0:NS, 8:10, :].rearrange("p a b -> p (a b)")[:, 0:D]
            for k in range(KD):
                dve.wait_ge(sems["y_ps"], k + 1)
                v.tensor_copy(yp[:, :, k * P:(k + 1) * P], ps[:, 4 + 2 * (k % 2), :].rearrange("p (t c) -> p t c", t=TT))
                v.tensor_copy(ysm[:, k * P:(k + 1) * P], ps[0:NS, 5 + 2 * (k % 2), 0:P]).then_inc(sems["y_ev"], 1)


def constants():
    t = np.zeros((P, NCONST), np.float32)

    def put(name, a):
        c, n = CONST[name]
        t[0:a.shape[0], c:c + n] = a.reshape(a.shape[0], n)

    i, j = np.arange(P)[:, None], np.arange(P)[None, :]
    put("ident", np.eye(P))
    rot = np.zeros((P, P))
    for h in range(P // DH):
        for d in range(8):
            rot[h * DH + d + 8, h * DH + d] = -1.0
            rot[h * DH + d, h * DH + d + 8] = 1.0
    put("rot", rot)
    put("upper", (i <= j).astype(np.float32))
    put("ones", np.ones((P, 7 * P)))
    put("later", (i > j).astype(np.float32))
    put("nupper", -(i >= j).astype(np.float32))
    put("nones", -np.ones((P, P)))
    inv = (np.float32(500000.0) ** (-np.arange(8, dtype=np.float32) / np.float32(8))).astype(np.float32)
    pos = np.concatenate([np.arange(SEQ), np.full(NS, PAST)]).astype(np.float32)
    ang = (pos[None, :] * inv[:, None]).astype(np.float32)
    cos, sin = np.ones((P, T), np.float32), np.zeros((P, T), np.float32)
    for h in range(P // DH):
        for o in (0, 8):
            cos[h * DH + o:h * DH + o + 8], sin[h * DH + o:h * DH + o + 8] = np.cos(ang), np.sin(ang)
    put("cos", cos)
    put("sin", sin)
    r, c = np.arange(64)[:, None], np.arange(64)[None, :]
    put("group", (r // 4 == c // 4).astype(np.float32))
    put("row8", (r // 8 == np.arange(8)[None, :]).astype(np.float32))
    put("row4", (np.arange(32)[:, None] // 4 == np.arange(8)[None, :]).astype(np.float32))
    put("blk", np.tile(np.arange(1, NBLK - 1), (64, 1)).astype(np.float32))
    put("onehot", np.repeat(np.eye(4), P, axis=1))
    tok = np.arange(TT)[None, :, None] * P + np.arange(P)[:, None, None]
    sees = (np.arange(32)[None, None, :] * STRIDE + CBLK - 1 <= tok) & (np.arange(32) < NCP)
    put("cmp01", sees.astype(np.float32))
    put("mcausal", np.where(j > i, NEG, 0.0))
    put("mstrict", np.where(i >= j, NEG, 0.0))
    put("mcmp", np.where(sees, 0.0, NEG))
    return t


_INS = ["x_prompt", "x_sample", "cache_nsa_cmp_kv", "cache_nsa_sel_kv", "cache_sb_kv", "cache_fox_kv", "cache_fox_logf",
        "state_nsa_win_kv", "page_table", "norm_mix_g", "norm_ffn_g", "norm_final_g", "w_in", "b_forget", "cmp_pos",
        "w_cmp_k", "w_cmp_v", "w_up_nsa", "w_up_sb", "w_up_fox", "w_out", "w_ffn_gate", "w_ffn_up", "w_ffn_down"]
_OUTS = [("y_prompt", (1, SEQ, D)), ("y_sample", (NS, 1, D)),
         ("p_cmp", (DEPTH, 1, SEQ, 2, G, DH)), ("p_sel", (DEPTH, 1, SEQ, 2, G, DH)), ("p_sb", (DEPTH, 1, SEQ, 2, 4, DH)),
         ("p_fox", (DEPTH, 1, SEQ, 2, 4, DH)), ("p_logf", (DEPTH, 1, SEQ, 4)), ("p_win", (DEPTH, 1, WIN, 2, G, DH)),
         ("s_cmp", (DEPTH, NS, 1, 2, G, DH)), ("s_sel", (DEPTH, NS, 1, 2, G, DH)), ("s_sb", (DEPTH, NS, 1, 2, 4, DH)),
         ("s_fox", (DEPTH, NS, 1, 2, 4, DH)), ("s_logf", (DEPTH, NS, 1, 4)), ("s_win", (DEPTH, NS, WIN, 2, G, DH))]


def kernel(**inputs):
    import concourse.bacc as bacc
    from concourse.bass_utils import run_bass_kernel_spmd

    nc = bacc.Bacc("TRN2", target_bir_lowering=False, num_devices=1, dynamic_dma_scratch_size=1024)
    arrays = {f"in_{n}": np.ascontiguousarray(inputs[n]) for n in _INS}
    arrays["in_consts"] = constants()
    args = {n[3:]: nc.dram_tensor(n, a.shape, mybir.dt.from_np(a.dtype), kind="ExternalInput").ap() for n, a in arrays.items()}
    outs = {n: nc.dram_tensor(f"out_{n}", s, mybir.dt.float32, kind="ExternalOutput").ap() for n, s in _OUTS}
    build(nc, args, outs)
    r = run_bass_kernel_spmd(nc, [arrays], core_ids=[0])
    return tuple(r.results[0][f"out_{n}"] for n, _ in _OUTS)
```

```python
import concourse.bass as bass
from concourse import mybir
from contextlib import ExitStack
import numpy as np

P = 128
D = 1024
KD = D // P
SEQ, NS = 512, 8
T = SEQ + NS
H2 = T // 2
TT = SEQ // P
DEPTH = 2
PAST, PAGE = 1024, 128
NPG = PAST // PAGE
NPOOL = NS * NPG * 5 // 4
DH = 64
G = 2
STRIDE, CBLK = 16, 32
NCP = SEQ // STRIDE - 1
NCS = PAST // STRIDE - 1
NBLK = PAST // 64
WIN = 512
DFF = 2816
NF = DFF // P
N_IN = 5916
NEG = -1.0e30
EPS = 1e-6
SCALE = DH ** -0.5
CMPK, CMPV, SELK, SELV, WINK, WINV, SBQ, SBK, SBV, FXQ, FXK, FXV = 4, 5, 6, 7, 8, 9, 10, 12, 14, 16, 18, 20
NT = 22
QTILES = (0, 1, 2, 3, SBQ, SBQ + 1, FXQ, FXQ + 1)
ROPE = (0, 1, 2, 3, CMPK, SELK, WINK)
NAT = (CMPK, CMPV, SELK, SELV, WINK, WINV, SBK, SBK + 1, SBV, SBV + 1, FXK, FXK + 1, FXV, FXV + 1)
STORED = (("cmp", 0, 2), ("sel", 2, 2), ("win", 4, 2), ("sb", 6, 4), ("fox", 10, 4))
NATV = (SELV, WINV, SBV, SBV + 1, FXV, FXV + 1)
NATK = tuple(t for t in NAT if t not in NATV)
CONST, _c = {}, 0
for _n, _w in (("ident", P), ("rot", P), ("upper", P), ("ones", 7 * P), ("later", P), ("nupper", P),
               ("nones", P), ("cos", T), ("sin", T), ("group", 64), ("row8", 8), ("row4", 8), ("mine", 8),
               ("blk", NBLK - 2), ("onehot", 4 * P), ("cmp01", TT * 32),
               ("mcausal", P), ("mstrict", P), ("mcmp", TT * 32)):
    CONST[_n] = (_c, _w)
    _c += _w
NCONST = _c
NKEEP = CONST["mcausal"][0]
CHUNKS = ([("in", c) for c in range(6)] + [("cmp", 0)]
          + [x for h in range(2) for x in [("up", h)] + [("mg", h, b) for b in range(3)]]
          + [("out", 0), ("out", 1)] + [("ffn", j) for j in range(NF // 2)]
          + [("down", n, h) for n in range(4) for h in range(2)])
RING = 3
NCH = len(CHUNKS)
assert NCH % RING == 0
UNITS = ([("cmp", b, h) for b in range(NS) for h in range(2)] + [("selk", b, 0) for b in range(NS)]
         + [("wink", b, 0) for b in range(NS)]
         + [(k, b, h) for b in range(NS) for h in range(2) for k in ("fxk", "sbk")]
         + [u for b in range(NS) for u in [("selv", b, 0)] + [(k, b, h) for h in range(2) for k in ("fxv", "sbv")] + [("winv", b, 0)]])
NU = len(UNITS)
USLOTS = 6
NKU = UNITS.index(("selv", 0, 0))
KSTEPS = {"cmp": 2, "selk": 2, "wink": 1, "fxk": 2, "sbk": 2}
UT = (4, 5, 6, 7, 8, 9, 12, 13)
ACT_CHAIN, DVE_CHAIN = 12, 86
PAIRS = [("nsa", t) for t in range(4)] + [("fox", 0), ("fox", 1)]
SOFT = [(p, br) for p in range(4) for br in ("cmp", "sel", "win")] + [(4, "fox"), (5, "fox")]
ITEMS = [(u, i) for u in range(len(SOFT)) for i in range(TT)]

TURNS = [(u, j) for u in UNITS[2 * NS:NKU] for j in range(KSTEPS[u[0]])]
_fx = TURNS.index((("fxk", 0, 0), 0))
TURNS[_fx + 16:_fx + 16] = [(("p_win",), 0)]
TURNS[_fx:_fx] = [(("p_cmp",), 0), (("p_sel",), 0)]
TURNS += [(("lf",), 0), (("p_fox",), 0), (("p_new",), 0)]
TURN_OF = {t: n for n, t in enumerate(TURNS)}
BEHIND = CHUNKS.index(("mg", 0, 0))
CMPT = 4 * NS


def in_order():
    dec = [("sc", 0), ("sc", 1), ("sc", 2)]
    last = {u[0]: n for n, (u, j) in enumerate(TURNS) if u[0][0] != "p"}
    done = {last["selk"]: 0, last["wink"]: 1}
    for n in range(len(TURNS) - 2):
        dec.append(("turn_s", n))
        if n:
            dec.append(("score_s", n - 1))
            if n - 1 in done:
                dec += [("news", done[n - 1]), ("soft", done[n - 1])]
            if n - 3 in done:
                dec.append(("weigh_s", done[n - 3]))
    n = len(TURNS) - 2
    dec += [("score_s", n - 1), ("news", 2), ("soft", 2), ("zs", 0)]
    val = [("weigh_s", 2), ("zs", 1), ("turn_s", n), ("zs", 2), ("turn_s", n + 1), ("zs", 3)]
    val += [("value_s", u) for u in range(NKU, NU)]
    parts = [("scores", 0), ("exp", 0), ("weigh", 0)]
    for n, (u, i) in enumerate(ITEMS):
        if n + 1 < len(ITEMS):
            parts += [("scores", n + 1)]
        parts += [("turn", n, 0), ("turn", n, 1)]
        if n + 1 < len(ITEMS):
            parts += [("exp", n + 1), ("weigh", n + 1)]
        if i == TT - 1:
            parts += [("values", u)]
    for hd in range(4):
        parts += [("stick", hd), ("behind", hd), ("stick_v", hd)]
    cutoff = parts.index(("turn", 41, 0))
    plan = []
    for a, b in ((parts[:cutoff], dec), (parts[cutoff:], val)):
        k = 0
        weight = [3 if p[0] in ("stick", "behind", "stick_v") else 1 for p in a]
        for n, p in enumerate(a):
            plan.append(p)
            want = sum(weight[:n + 1]) * len(b) // sum(weight)
            plan += b[k:want]
            k = want
    return plan


PLAN = in_order()
SCORE_OF = {n: k for k, n in enumerate(n for n, (u, j) in enumerate(TURNS) if u[0][0] != "p" and u[0] != "lf")}


class Layer:
    def __init__(self, more):
        self.more = more


def w_dmas(ch):
    return {"cmp": 2, "up": 4, "ffn": 2}.get(ch[0], {("in", 0): 8, ("in", 2): 2}.get(ch, 1))


def u_dmas(u):
    return {"cmp": 4, "selk": 8, "selv": 8, "wink": 1, "winv": 1}.get(u[0], 4)


def layer_counts():
    items = len(ITEMS)
    ksteps = CMPT + len(TURNS)
    c = dict(sq_ready=2 * KD, sq_used=2 * KD, rs_ready=2, h_ready=2 * KD, x_upd=2 * KD,
             proj_ps=NT, proj_ev=NT, rot_ps=len(ROPE), rope_done=len(ROPE), nat_ps=len(NAT), nat_ev=len(NAT),
             new_ps=1, new_ev=1, gate_ps=1, gate_ev=1, gate_sig=1, lf_abs=1, lf_ln=1, lf_done=1, cum_ps=1, cum_ev=1,
             sig_dma=32, lf_in=16 * NS * NPG, out_dma=16 * (len(NAT) + len(STORED) + 2), q_ev=1, new_ready=1,
             kc_own=2, ck_ev=1, cvt_ps=1, cvt_ev=1,
             kt_ps=ksteps, kt_ev=ksteps, cs_ps=8, cs_ev=8, cvs_ps=2, cvs_ev=2, wv_in=32, cmp_zero=2,
             s_ps=items, nm_ready=items, exp_done=items, rr_ready=items, p_scaled=items, pt_ps=2 * items,
             pt_ev_a=items, pt_ev_d=items, pv_done=len(SOFT), o_ev=8,
             sbz_ps=4, sb_ln=4, sb_sp=4, sbc_ps=4, sb_w=4, sb_pv=4,
             smm=sum(KSTEPS[u[0]] for u in UNITS[:NKU] if u[0] in ("selk", "wink", "fxk", "sbk")),
             sc_ps=1, sc_nm=1, sc_exp=1, sc_p=1, pg_ps=1, drop=1, snew=3, s_ev=4, s_nm=3, s_exp=3, s_p=3,
             zt_ps=1, z_abs=1, z_sp=1, zc_ps=1, z_w=1, z_sum=1, dg=3,
             v_used=NU - NKU, acc_up=NS, so_ps=1, so_ev=1,
             mt_ps=56, mt_ev=48, mul=24, u_ready=8, ffn_g=NF, ffn_s=NF, ffn_u=NF, hid=NF, down_ps=8)
    return c


def build(nc, A, out):
    f32, bf16, i32 = mybir.dt.float32, mybir.dt.bfloat16, mybir.dt.int32
    ALU, ACT, AX = mybir.AluOpType, mybir.ActivationFunctionType, mybir.AxisListType
    PER = layer_counts()
    ctx = ExitStack()
    with ctx:
        def sb(name, shape, dt=f32):
            return ctx.enter_context(nc.sbuf_tensor(name, shape, dt))

        xT = sb("xT", [P, KD, T])
        hT = sb("hT", [P, KD, T])
        PT = sb("PT", [P, NT, T])
        ring = sb("ring", [P, RING, 4096])
        ARENA = 6500
        arena = sb("arena", [P, ARENA])
        units = sb("units", [P, USLOTS, 1024])
        vnat = sb("vnat", [P, len(NATV), TT, P])
        cst = sb("cst", [P, NKEEP])
        maskb = sb("maskb", [P, 4 * P], bf16)
        ckT = sb("ckT", [P, NS, NCS])
        cvS = sb("cvS", [NCS, NS, P])
        qn = sb("qn", [P, NS, 64])
        qs = sb("qs", [P, 2, NS, 32])
        qf = sb("qf", [P, 2, NS, 32])
        gnat = sb("gnat", [P, TT, 28])
        gsmp = sb("gsmp", [NS, 28])
        lfn = sb("lfn", [P, TT, 4])
        lft = sb("lft", [P, TT, 4])
        lfs = sb("lfs", [NS, 4])
        lfst = sb("lfst", [NS, 4])
        g64 = sb("g64", [64, 3])
        l32 = sb("l32", [32, 1])
        bfb = sb("bfb", [P, DEPTH, 4])
        gam = sb("gam", [P, 2 * DEPTH + 1, KD])
        ncum = sb("ncum", [4, SEQ])
        ckP = sb("ckP", [P, 2, 32])
        cvP = sb("cvP", [32, P])
        cbias = sb("cbias", [P, 2])
        posT = sb("posT", [P, DEPTH, CBLK])
        LF = sb("LF", [P, NPG, NS, 4])
        nm = sb("nm", [P, 2, 2])
        sm = sb("sm", [P, 2, 2])
        rr = sb("rr", [P, 2, 2])
        vnew = sb("vnew", [NS, len(NATV), P])
        pc = sb("pc", [64, 64])
        pgb = sb("pgb", [64, 72])
        s1 = sb("s1", [64, 32])
        pgt = sb("pgt", [1, NS * NPG], i32)
        epsb = sb("epsb", [P, 1])
        gl = sb("gl", [P, 2, KD])
        posL = sb("posL", [P, CBLK])
        bfl = sb("bfl", [P, 4])
        ps = ctx.enter_context(nc.psum_tensor("ps", [P, 8, 512], f32))

        def ar(at, *shape):
            n = int(np.prod(shape))
            v = arena[:, at:at + n]
            if len(shape) == 1:
                return v
            names = "abcd"[:len(shape)]
            return v.rearrange(f"p ({' '.join(names)}) -> p {' '.join(names)}", **dict(zip(names, shape)))

        posn = ar(5120, DEPTH, G, DH)[0:CBLK]
        sq, rs, rinv = ar(0, 2, T), ar(2 * T, T), ar(3 * T, T)
        ropet, knat, natS = ar(0, T), ar(T, len(NATV) + 2, TT * P), ar(T + 7 * 512 + 512, len(NAT), P)
        KC = ar(0, 2, 2 * PAST + SEQ + CBLK)
        W_OWN, W_POS = 2 * PAST // STRIDE, (2 * PAST + SEQ) // STRIDE
        cvT = ar(5184, 2, NCS)
        WC = [ring[:, 2 * j, :].rearrange("p (l e) -> p l e", l=CBLK) for j in range(2)]
        PTb = ring[:, 0, :].rearrange("p (a b c) -> p a b c", a=2, b=TT)
        Pb = ring[:, 2, 0:2048].rearrange("p (a b c) -> p a b c", a=2, b=2)
        zt, spb, wb = (ring[:, 0, i * 1280:(i + 1) * 1280] for i in range(3))
        SS, PTs, SW, PTw = ar(0, 1025), ar(1028, NPG, 64), ar(1544, 513), ar(2060, 4, 64)
        SF, PTf = ar(2320, 1025), ar(3348, NPG, 32)
        za, zsp, zw = ar(3604, 256), ar(3860, 256), ar(4116, NPG, 32)
        acc = ar(0, 256)
        ZS = arena[64:96, 0:1024]
        LFP = ar(4880, 512)[0:NS * NPG]
        KT = ar(5396, 2, 512)
        sg = [vnat[:, :, :, :].rearrange("p a b c -> p (a b c)")[:, i * T:(i + 1) * T] for i in range(2)]
        dg = ar(4372, 3, 64)[0:64]
        DM, pcT, t17 = ar(4564, 160)[0:NS], ar(4724, 64)[0:64], ar(4788, 4, 20)[0:64]
        UP = ar(0, 12, T)
        fs = ar(0, 2, T)

        def C(name, rows=P):
            a, n = CONST[name]
            return cst[0:rows, a:a + n]

        identb, mcausal, mstrict, mcmpb = (maskb[:, i * P:(i + 1) * P] for i in range(4))
        ident, rot = C("ident"), C("rot")
        o0 = CONST["upper"][0]
        cum_fwd = cst[:, o0:o0 + 4 * P]
        o1 = CONST["ones"][0]
        cum_bwd = cst[:, o1:o1 + 8 * P]

        sems = {}
        for name in list(PER) + ["const_in", "const_ok", "xt_ps", "xt_in", "y_ps", "y_ev", "y_dma", "win_dma", "pg_in",
                                 "post_ps", "dve_chain", "act_chain", "init_z"] \
                + [f"w{i}" for i in range(RING)] + [f"u{i}" for i in range(USLOTS)]:
            sems[name] = ctx.enter_context(nc.semaphore(name))
        CREDIT = {"down_ps": PER["down_ps"], "v_used": PER["v_used"]}
        BASE = {"x_upd": KD}

        regs = {}

        def in_layers(eng, l):
            if "layer" not in regs.setdefault(eng.engine, {}):
                regs[eng.engine].update(layer=eng.alloc_register("layer"), value=eng.alloc_register("wait_value"))
            eng.reg_mov(regs[eng.engine]["layer"], l)
            return Layer(0)

        def count(eng, l, per, n):
            if not isinstance(l, Layer):
                return l * per + n
            layer, value = regs[eng.engine]["layer"], regs[eng.engine]["value"]
            eng.reg_mul(value, layer, per)
            eng.reg_add(value, value, n + l.more * per)
            return value

        def at(eng, name, l, n):
            assert n >= 1, name
            return count(eng, l, PER[name], n + CREDIT.get(name, 0) + BASE.get(name, 0))

        def apart(eng):
            value = regs[eng.engine]["value"]
            eng.reg_add(value, value, 1)
            eng.reg_mul(value, value, 2)

        chunk_read, up, mg, ou = {}, 0, 0, 0
        for n, ch in enumerate(CHUNKS):
            k = ch[0]
            chunk_read[n] = {"in": lambda: ("proj_ps", (4, 8, None, 14, 18, 22)[ch[1]]), "cmp": lambda: ("cs_ps", 7),
                             "up": lambda: ("mt_ps", 24 * ch[1] + 12),
                             "mg": lambda: ("mt_ps", 24 * ch[1] + 12 + 4 * (ch[2] + 1)),
                             "out": lambda: ("mt_ps", 48 + 4 * (ch[1] + 1)), "ffn": lambda: ("ffn_u", 2 * (ch[1] + 1)),
                             "down": lambda: ("down_ps", 2 * ch[1] + ch[2] + 1)}[k]()
        chunk_read[2] = ("gate_ps", 1)
        w_at, cnt = [], [0] * RING
        for n, ch in enumerate(CHUNKS):
            cnt[n % RING] += 16 * w_dmas(ch)
            w_at.append(cnt[n % RING])
        w_per = cnt
        u_at, cnt, last_in = [], [0] * USLOTS, {}
        for n, u in enumerate(UNITS):
            cnt[n % USLOTS] += 16 * u_dmas(u)
            u_at.append(cnt[n % USLOTS])
            last_in[n % USLOTS] = n
        u_per = cnt
        unit_read = []
        for n, u in enumerate(UNITS):
            if n < 2 * NS:
                unit_read.append(("kt_ps", 8 * (n // 4) + 4 + n % 4 + 1))
            elif n < NKU:
                unit_read.append(("kt_ps", CMPT + TURN_OF[u, KSTEPS[u[0]] - 1] + 1))
            else:
                unit_read.append(("v_used", n - NKU + 1))

        def weights_in(eng, l, ch):
            n = CHUNKS.index(ch)
            eng.wait_ge(sems[f"w{n % RING}"], count(eng, l, w_per[n % RING], w_at[n]))
            return ring[:, n % RING, :]

        def unit_in(eng, l, u):
            n = UNITS.index(u)
            eng.wait_ge(sems[f"u{n % USLOTS}"], count(eng, l, u_per[n % USLOTS], u_at[n]))
            return units[:, n % USLOTS, :]

        def half(ap):
            return ap.rearrange("p (h t) -> p h t", h=2)

        def pair(b):
            return ps[:, b:b + 2, 0:H2]

        block = ctx.enter_context(nc.Block())

        @block.sync
        def _(sp):
            dma = sp.dma_start
            dma(cst[:, :], A["consts"][:, 0:NKEEP]).then_inc(sems["const_in"], 16)
            dma(hT[:, :, :].rearrange("p a b -> p (a b)")[:, 0:NCONST - NKEEP], A["consts"][:, NKEEP:NCONST]).then_inc(sems["const_in"], 16)
            dma(ar(0, TT, D), A["x_prompt"][0].rearrange("(t p) d -> p t d", p=P)).then_inc(sems["const_in"], 16)
            dma(ar(TT * D, D)[0:NS], A["x_sample"].rearrange("b s d -> (b s) d")).then_inc(sems["const_in"], 16)
            with nc.allow_non_contiguous_dma(reason="norm gains and biases: a few kilobytes, once"):
                for i in range(DEPTH):
                    dma(gam[:, 2 * i, :], A["norm_mix_g"][i].rearrange("(k p) -> p k", p=P)).then_inc(sems["const_in"], 16)
                    dma(gam[:, 2 * i + 1, :], A["norm_ffn_g"][i].rearrange("(k p) -> p k", p=P)).then_inc(sems["const_in"], 16)
                dma(gam[:, 2 * DEPTH, :], A["norm_final_g"].rearrange("(k p) -> p k", p=P)).then_inc(sems["const_in"], 16)
            for g in range(G):
                dma(posn[:, :, g, :], A["cmp_pos"].rearrange("l c d -> c l d")).then_inc(sems["const_in"], 16)
            dma(bfb[:, :, :], A["b_forget"].rearrange("l h -> (l h)").partition_broadcast(P)).then_inc(sems["const_in"], 16)
            dma(pgt[:, :], A["page_table"].rearrange("(a b) n -> a (b n)", a=1)).then_inc(sems["pg_in"], 16)
            sp.wait_ge(sems["pg_in"], 16)

            def compression(l, name, slot, sem):
                for g in range(G):
                    dst = slot.rearrange("p (l e) -> p l e", e=P)[g * DH:(g + 1) * DH, :, g * DH:(g + 1) * DH]
                    dma(dst, A[name][l].rearrange("(l d) e -> d l e", d=DH)).then_inc(sem, 16)

            def load_chunk(l, n):
                ch = CHUNKS[n]
                m = (n - RING) % NCH
                if n in (BEHIND, BEHIND + 1):
                    sp.wait_ge(sems["sb_pv"], at(sp, "sb_pv", Layer(0), 4))
                sp.wait_ge(sems[chunk_read[m][0]], at(sp, chunk_read[m][0], Layer(0 if n >= RING else -1), chunk_read[m][1]))
                slot, sem = ring[:, n % RING, :], sems[f"w{n % RING}"]
                w_in = A["w_in"][l].rearrange("(k p) n -> p k n", p=P)

                def put(at, k, cols, src):
                    dma(slot[:, at:at + k * cols].rearrange("p (k n) -> p k n", k=k), src).then_inc(sem, 16)

                if ch == ("in", 0):
                    for g in range(G):
                        for t in range(4):
                            dst = slot.rearrange("p (k t g d) -> p k t g d", k=KD, g=G, d=DH)[:, :, t, g, :]
                            dma(dst, w_in[:, :, g * 256 + t * DH:g * 256 + (t + 1) * DH]).then_inc(sem, 16)
                elif ch == ("in", 2):
                    v = slot.rearrange("p (k n) -> p k n", k=KD)
                    dma(v[:, :, 0:280], w_in[:, :, 1024:1304]).then_inc(sem, 16)
                    dma(v[:, :, 280:284], w_in[:, :, 2840:2844]).then_inc(sem, 16)
                elif ch[0] == "in":
                    c0 = (0, 512, 1024, 1304, 1816, 2328)[ch[1]]
                    put(0, KD, 512, w_in[:, :, c0:c0 + 512])
                elif ch[0] == "cmp":
                    compression(l, "w_cmp_k", slot, sem)
                elif ch[0] == "mg":
                    c0 = 2844 + ch[2] * D + ch[1] * 512
                    put(0, KD, 512, w_in[:, :, c0:c0 + 512])
                elif ch[0] == "up":
                    cs = slice(ch[1] * 512, ch[1] * 512 + 512)
                    for g in range(G):
                        dst = slot[g * DH:(g + 1) * DH, 0:2048].rearrange("d (t n) -> d t n", t=4)
                        src = A["w_up_nsa"][l].rearrange("(g t d) n -> g d t n", g=G, t=4)[g][:, :, cs]
                        dma(dst, src).then_inc(sem, 16)
                    dst = slot[:, 2048:3072].rearrange("p (k n) -> p k n", k=2)
                    dma(dst, A["w_up_sb"][l].rearrange("(k p) n -> p k n", p=P)[:, :, cs]).then_inc(sem, 16)
                    dst = slot[:, 3072:4096].rearrange("p (k n) -> p k n", k=2)
                    dma(dst, A["w_up_fox"][l].rearrange("(k p) n -> p k n", p=P)[:, :, cs]).then_inc(sem, 16)
                elif ch[0] == "out":
                    put(0, KD, 512, A["w_out"][l].rearrange("(k p) n -> p k n", p=P)[:, :, ch[1] * 512:ch[1] * 512 + 512])
                elif ch[0] == "ffn":
                    for j, w in enumerate(("w_ffn_gate", "w_ffn_up")):
                        put(j * 2048, KD, 256, A[w][l].rearrange("(k p) n -> p k n", p=P)[:, :, ch[1] * 256:ch[1] * 256 + 256])
                else:
                    put(0, NF // 2, 256, A["w_ffn_down"][l].rearrange("(h k p) n -> h p k n", h=2, p=P)[ch[2]][:, :, ch[1] * 256:ch[1] * 256 + 256])

            page_regs = [sp.alloc_register(f"pages{i}") for i in range(NS * NPG // 2)]
            page_reg = sp.alloc_register("page")
            held = set()

            def load_unit(l, n):
                kind, b, h = UNITS[n]
                m = n - USLOTS
                src = unit_read[m] if m >= 0 else unit_read[last_in[n % USLOTS]]
                slot, sem = units[:, n % USLOTS, :], sems[f"u{n % USLOTS}"]

                def page(i):
                    (sp.reg_div if i % 2 else sp.reg_mod)(page_reg, page_regs[i // 2], NPOOL)
                    return sp.snap(page_reg, min_val=0, max_val=NPOOL - 1)

                def pages_known(first, n):
                    for k in range(first // 2, (first + n) // 2):
                        if k not in held:
                            held.add(k)
                            sp.reg_load(page_regs[k], pgt[0:1, 2 * k:2 * k + 1])
                            sp.reg_load(page_reg, pgt[0:1, 2 * k + 1:2 * k + 2])
                            sp.reg_mul(page_reg, page_reg, NPOOL)
                            sp.reg_add(page_regs[k], page_regs[k], page_reg)

                def rows(name):
                    a = A[name]
                    spec = "l n r t h d -> (l n) r (t h d)" if len(a.shape) == 6 else "l n r h -> (l n) (r h)"
                    return a.rearrange(spec)

                def free():
                    sp.wait_ge(sems[src[0]], at(sp, src[0], Layer(0 if m >= 0 else -1), src[1]))

                if kind == "fxk" and h == 1:
                    first = page(b * NPG)
                    if b == 0:
                        sp.wait_ge(sems["cvs_ps"], at(sp, "cvs_ps", Layer(0), 2))
                    for i in range(b * NPG, (b + 1) * NPG):
                        pg = page(i) if i > b * NPG else first
                        dma(LFP[i:i + 1, :], rows("cache_fox_logf")[bass.ds(l * NPOOL + pg, 1)]).then_inc(sems["lf_in"], 16)
                if kind in ("wink", "winv"):
                    c0 = 0 if kind == "wink" else P
                    free()
                    w = A["state_nsa_win_kv"].rearrange("l b (j p) t h d -> (l b) p j (t h d)", p=P)
                    dma(slot[:, 0:512].rearrange("p (j c) -> p j c", j=4), w[l * NS + b][:, :, c0:c0 + P]).then_inc(sem, 16)
                else:
                    name, c0, cols = {"cmp": ("cache_nsa_cmp_kv", 0, 256), "selk": ("cache_nsa_sel_kv", 0, 128),
                                      "selv": ("cache_nsa_sel_kv", 128, 128), "fxk": ("cache_fox_kv", 0, 256),
                                      "fxv": ("cache_fox_kv", 256, 256), "sbk": ("cache_sb_kv", 0, 256),
                                      "sbv": ("cache_sb_kv", 256, 256)}[kind]
                    k = 1024 // cols
                    pages_known(b * NPG + h * k, k)
                    first = page(b * NPG + h * k)
                    free()
                    for j in range(k):
                        pg = page(b * NPG + h * k + j) if j else first
                        dma(slot[:, j * cols:(j + 1) * cols], rows(name)[l * NPOOL + pg][:, c0:c0 + cols]).then_inc(sem, 16)

            with sp.Fori(0, DEPTH) as l:
                in_layers(sp, l)
                dma(out["s_win"].rearrange("l b r t h d -> (l b) r (t h d)")[bass.ds(l * NS, NS), 0:WIN - 1],
                    A["state_nsa_win_kv"].rearrange("l b r t h d -> (l b) r (t h d)")[bass.ds(l * NS, NS), 1:WIN]).then_inc(sems["win_dma"], 16)
                for n in range(RING + 3):
                    load_chunk(l, n)
                for n in range(USLOTS):
                    load_unit(l, n)
                for n in range(RING + 3, BEHIND):
                    load_chunk(l, n)
                sp.wait_ge(sems["proj_ps"], at(sp, "proj_ps", Layer(0), NT))
                compression(l, "w_cmp_v", ring[:, 2, :], sems["wv_in"])
                for n in range(USLOTS, NU):
                    load_unit(l, n)
                for n in range(BEHIND, NCH):
                    load_chunk(l, n)
            sp.wait_ge(sems["win_dma"], 16 * DEPTH)

        @block.tensor
        def _(pe):
            mm = nc.tensor.matmul

            def tp(o, i, n):
                return nc.tensor.transpose(o, i, ident[0:n, 0:n])

            pe.sem_inc(sems["down_ps"], PER["down_ps"])
            pe.sem_inc(sems["v_used"], PER["v_used"])
            pe.wait_ge(sems["const_in"], 16 * 12)
            for k in range(KD):
                if k >= 2:
                    pe.wait_ge(sems["x_upd"], k - 1)
                for t in range(TT):
                    tp(ps[:, 2 * (k % 2), t * P:(t + 1) * P], ar(0, TT, D)[:, t, k * P:(k + 1) * P], P)
                tp(ps[:, 2 * (k % 2) + 1, 0:NS], ar(TT * D, D)[0:NS, k * P:(k + 1) * P], NS).then_inc(sems["xt_ps"], 1)
            for i in range(DEPTH):
                last = tp(ps[:, 4, i * CBLK:(i + 1) * CBLK], posn[:, i, :, :].rearrange("c g d -> c (g d)"), CBLK)
            last.then_inc(sems["post_ps"], 1)

            def norm(l, w):
                pe.wait_ge(sems["x_upd"], count(pe, l, PER["x_upd"], w * KD + KD - 2))
                for k in range(KD):
                    pe.wait_ge(sems["sq_ready"], at(pe, "sq_ready", l, w * KD + k + 1))
                    mm(ps[:, 0, 0:H2], C("ones")[:, 0:P], sq[:, k % 2, 0:H2], start=k == 0, stop=k == KD - 1)
                    mm(ps[:, 1, 0:H2], C("ones")[:, 0:P], sq[:, k % 2, H2:T], start=k == 0, stop=k == KD - 1).then_inc(sems["sq_used"], 1)

            def tile(b, pairs, before=lambda k: None):
                n = len(pairs)
                for k, (w, a) in enumerate(pairs):
                    before(k)
                    mm(ps[:, b, 0:H2], w, a[:, 0:H2], start=k == 0, stop=k == n - 1)
                    last = mm(ps[:, b + 1, 0:H2], w, a[:, H2:T], start=k == 0, stop=k == n - 1)
                return last

            def project(l):
                def post(i):
                    pe.wait_ge(sems["proj_ev"], at(pe, "proj_ev", l, i + 1))
                    if i in ROPE:
                        r = ROPE.index(i)
                        if r >= 1:
                            pe.wait_ge(sems["rope_done"], at(pe, "rope_done", l, r))
                        if i == WINK:
                            pe.wait_ge(sems["gate_ev"], at(pe, "gate_ev", l, 1))
                        mm(ps[:, 4, 0:H2], rot, PT[:, i, 0:H2], start=True, stop=True)
                        mm(ps[:, 5, 0:H2], rot, PT[:, i, H2:T], start=True, stop=True).then_inc(sems["rot_ps"], 1)

                def nat(i):
                    if i not in NAT:
                        return
                    n = NAT.index(i)
                    if i in ROPE:
                        pe.wait_ge(sems["rope_done"], at(pe, "rope_done", l, ROPE.index(i) + 1))
                    if n >= 2:
                        pe.wait_ge(sems["nat_ev"], at(pe, "nat_ev", l, n - 1))
                    for t in range(TT):
                        last = tp(ps[:, 6 + n % 2, t * P:(t + 1) * P], PT[:, i, t * P:(t + 1) * P], P)
                    last.then_inc(sems["nat_ps"], 1)

                for i in range(NT):
                    c = i // 4 if i < 8 else 2 if i < 10 else 3 + (i - 10) // 4
                    w = weights_in(pe, l, ("in", c)).rearrange("p (k n) -> p k n", k=KD)
                    j = i - (0, 4, 8, 10, 14, 18)[c]
                    if i >= 2:
                        pe.wait_ge(sems["proj_ev"], at(pe, "proj_ev", l, i - 1))
                    for k in range(KD):
                        if i == 0:
                            pe.wait_ge(sems["h_ready"], at(pe, "h_ready", l, k + 1))
                        mm(ps[:, 2 * (i % 2), 0:H2], w[:, k, j * P:(j + 1) * P], hT[:, k, 0:H2], start=k == 0, stop=k == KD - 1)
                        last = mm(ps[:, 2 * (i % 2) + 1, 0:H2], w[:, k, j * P:(j + 1) * P], hT[:, k, H2:T], start=k == 0, stop=k == KD - 1)
                    last.then_inc(sems["proj_ps"], 1)
                    if i == WINV:
                        pe.wait_ge(sems["rope_done"], at(pe, "rope_done", l, ROPE.index(WINK)))
                        for t in range(TT):
                            for k in range(KD):
                                mm(ps[:, 5, 264 + 28 * t:292 + 28 * t], hT[:, k, t * P:(t + 1) * P], w[:, k, 256:284], start=k == 0, stop=k == KD - 1)
                        for k in range(KD):
                            last = mm(ps[0:NS, 4, 264:292], hT[:, k, SEQ:T], w[:, k, 256:284], start=k == 0, stop=k == KD - 1)
                        last.then_inc(sems["gate_ps"], 1)
                    if i >= 1:
                        post(i - 1)
                    if i >= 2:
                        nat(i - 2)
                post(NT - 1)
                nat(NT - 2)
                nat(NT - 1)
                for n, i in enumerate(NAT):
                    last = tp(ps[0:NS, n // 4, n % 4 * P:(n % 4 + 1) * P], PT[:, i, SEQ:T], P)
                last.then_inc(sems["new_ps"], 1)

            def cumulate(l):
                pe.wait_ge(sems["nat_ev"], at(pe, "nat_ev", l, len(NAT)))
                pe.wait_ge(sems["new_ev"], at(pe, "new_ev", l, 1))
                pe.wait_ge(sems["lf_done"], at(pe, "lf_done", l, 1))
                for t in range(TT):
                    last = mm(ps[0:4, 4, t * P:SEQ], lfn[:, t, :], cum_fwd[:, 0:SEQ - t * P], start=t == 0, stop=True, skip_group_check=True)
                last.then_inc(sems["cum_ps"], 1)

            def compress(l):
                cumulate(l)

                def turned(q, kv):
                    for u in range(4):
                        b, h = 2 * q + u // 2, u % 2
                        step = 8 * q + 4 * kv + u
                        s = unit_in(pe, l, ("cmp", b, h)).rearrange("p (j c) -> p j c", j=4)
                        if step >= 2:
                            pe.wait_ge(sems["kt_ev"], at(pe, "kt_ev", l, step - 1))
                        for j in range(4):
                            last = tp(ps[:, 6 + step % 2, j * P:(j + 1) * P], s[:, j, kv * P:(kv + 1) * P], P)
                        last.then_inc(sems["kt_ps"], 1)

                def compressed(q, kv):
                    pe.wait_ge(sems["kt_ev"], at(pe, "kt_ev", l, 8 * q + 4 * kv + 4))
                    if q:
                        pe.wait_ge(sems["cs_ev"], at(pe, "cs_ev", l, 2 * q + kv - 1))
                    else:
                        if kv:
                            pe.wait_ge(sems["wv_in"], at(pe, "wv_in", l, PER["wv_in"]))
                        else:
                            weights_in(pe, l, ("cmp", 0))
                            pe.wait_ge(sems["cum_ev"], at(pe, "cum_ev", l, 1))
                        pe.wait_ge(sems["cmp_zero"], at(pe, "cmp_zero", l, kv + 1))
                        pe.wait_ge(sems["kc_own"], at(pe, "kc_own", l, kv + 1))
                    n = W_POS + 1 if q == 0 else W_OWN - 1
                    for c in range(CBLK):
                        last = mm(ps[:, 4 + kv, 0:n], WC[kv][:, c, :], KC[:, kv, c:c + STRIDE * (n - 1) + 1:STRIDE],
                                  start=c == 0, stop=c == CBLK - 1)
                    last.then_inc(sems["cs_ps"], 1)

                turned(0, 0)
                turned(0, 1)
                for q in range(4):
                    compressed(q, 0)
                    if q < 3:
                        turned(q + 1, 0)
                    compressed(q, 1)
                    if q < 3:
                        turned(q + 1, 1)
                    pe.wait_ge(sems["cs_ev"], at(pe, "cs_ev", l, 2 * q + 2))
                    if q == 0:
                        pe.wait_ge(sems["ck_ev"], at(pe, "ck_ev", l, 1))
                        tp(ps[0:NCP, 1, 0:P], ckP[:, 1, 0:NCP], P).then_inc(sems["cvt_ps"], 1)
                    if q == 2:
                        pe.wait_ge(sems["cvs_ev"], at(pe, "cvs_ev", l, 1))
                    apart(pe)
                    for i in range(2):
                        bb = 2 * (q % 2) + i
                        last = tp(ps[0:NCS, 0, bb * P:(bb + 1) * P], cvT[:, i, :], P)
                    if q % 2:
                        last.then_inc(sems["cvs_ps"], 1)

            def heads(idx):
                kind, t = PAIRS[idx]
                return t if kind == "nsa" else FXQ + t

            def scores(l, n):
                u, i = ITEMS[n]
                idx, br = SOFT[u]
                qt = heads(idx)
                if n >= 1:
                    pe.wait_ge(sems["exp_done"], at(pe, "exp_done", l, n))
                for hh in range(2):
                    r = slice(hh * DH, (hh + 1) * DH)
                    o = ps[:, hh, :]
                    q = PT[r, qt, i * P:(i + 1) * P]
                    if br == "cmp":
                        mm(o[:, 0:NCP], q, ckP[r, 0, 0:NCP], start=True, stop=True, skip_group_check=True)
                        last = mm(o[:, 0:NCP], identb, mcmpb[:, i * 32:i * 32 + NCP], start=False, stop=True, skip_group_check=True)
                        continue
                    kt = {"sel": SELK, "win": WINK}.get(br) or FXK + idx - 4
                    w = (i + 1) * P
                    mm(o[:, 0:w], q, PT[r, kt, 0:w], start=True, stop=True, skip_group_check=True)
                    if br == "fox":
                        h = 2 * (idx - 4) + hh
                        mm(o[:, 0:w], C("onehot", 4)[:, h * P:(h + 1) * P], ncum[:, 0:w], start=False, stop=True, skip_group_check=True)
                    last = mm(o[:, i * P:w], identb, mcausal, start=False, stop=True, skip_group_check=True)
                last.then_inc(sems["s_ps"], 1)

            def turn(l, n, hh):
                u, i = ITEMS[n]
                if hh == 0:
                    pe.wait_ge(sems["p_scaled"], at(pe, "p_scaled", l, n + 1))
                    if n >= 1:
                        pe.wait_ge(sems["pt_ev_d"], at(pe, "pt_ev_d", l, n))
                else:
                    pe.wait_ge(sems["pt_ev_a"], at(pe, "pt_ev_a", l, n + 1))
                if SOFT[u][1] == "cmp":
                    last = tp(ps[0:NCP, 2, 0:P], Pb[:, n % 2, hh, 0:NCP], P)
                else:
                    for j in range(i + 1):
                        last = tp(ps[:, 2, j * P:(j + 1) * P], Pb[:, n % 2, hh, j * P:(j + 1) * P], P)
                last.then_inc(sems["pt_ps"], 1)

            def values(l, u):
                idx, br = SOFT[u]
                n = u * TT + TT - 1
                pe.wait_ge(sems["pt_ev_a"], at(pe, "pt_ev_a", l, n + 1))
                pe.wait_ge(sems["pt_ev_d"], at(pe, "pt_ev_d", l, n + 1))
                if idx >= 1 and br in ("cmp", "fox"):
                    pe.wait_ge(sems["o_ev"], at(pe, "o_ev", l, idx))
                for hh in range(2):
                    r = slice(hh * DH, (hh + 1) * DH)
                    o = ps[r, 3, :]
                    if br == "cmp":
                        last = mm(o, cvP[0:NCP, r], PTb[0:NCP, hh, 0, :], start=True, stop=True, skip_group_check=True)
                        continue
                    v = {"sel": 0, "win": 1}.get(br)
                    v = idx if v is None else v
                    for j in range(TT):
                        last = mm(o[:, j * P:SEQ], vnat[:, v, j, r], PTb[:, hh, j, j * P:SEQ], start=br == "fox" and j == 0,
                                  stop=True, skip_group_check=True)
                last.then_inc(sems["pv_done"], 1)

            ZO = (0, 512, 1024, 896)

            zp = ps[:, 0:3, :].rearrange("p b c -> p (b c)")

            def stick(l, hd):
                f, hh = hd // 2, hd % 2
                r = slice(hh * DH, (hh + 1) * DH)
                if hd == 0:
                    pe.wait_ge(sems["exp_done"], at(pe, "exp_done", l, len(ITEMS)))
                    pe.wait_ge(sems["pt_ev_d"], at(pe, "pt_ev_d", l, len(ITEMS)))
                else:
                    pe.wait_ge(sems["sb_w"], at(pe, "sb_w", l, hd))
                for j in (0, 1, 3, 2):
                    w = SEQ - j * P
                    mm(zp[:, ZO[j]:ZO[j] + w], PT[r, SBK + f, j * P:(j + 1) * P], PT[r, SBQ + f, j * P:SEQ], start=j != 3, stop=True, skip_group_check=True)
                    last = mm(zp[:, ZO[j]:ZO[j] + P], identb, mstrict, start=False, stop=True, skip_group_check=True)
                last.then_inc(sems["sbz_ps"], 1)

            def behind(l, hd):
                pe.wait_ge(sems["sb_sp"], at(pe, "sb_sp", l, hd + 1))
                for j in range(TT):
                    w = SEQ - j * P
                    last = mm(zp[:, ZO[j]:ZO[j] + w], C("nupper"), spb[:, ZO[j]:ZO[j] + w], start=False, stop=True, skip_group_check=True)
                    for i in range(j + 1, TT):
                        w = SEQ - i * P
                        o = ZO[j] + (i - j) * P
                        last = mm(zp[:, o:o + w], C("nones"), spb[:, ZO[i]:ZO[i] + w], start=False, stop=True, skip_group_check=True)
                last.then_inc(sems["sbc_ps"], 1)

            def stick_v(l, hd):
                f, hh = hd // 2, hd % 2
                r = slice(hh * DH, (hh + 1) * DH)
                pe.wait_ge(sems["sb_w"], at(pe, "sb_w", l, hd + 1))
                if hh == 0:
                    pe.wait_ge(sems["o_ev"], at(pe, "o_ev", l, 6 + f))
                for j in range(TT):
                    w = SEQ - j * P
                    last = mm(ps[r, 3, j * P:SEQ], vnat[:, 2 + f, j, r], wb[:, ZO[j]:ZO[j] + w], start=j == 0, stop=True, skip_group_check=True)
                last.then_inc(sems["sb_pv"], 1)

            def sc(l, part):
                if part == 0:
                    for b in range(NS):
                        last = mm(ps[0:64, 5, 64:64 + NCS], qn[:, b, :], ckT[:, b, :], start=b == 0, stop=b == NS - 1)
                    last.then_inc(sems["sc_ps"], 1)
                elif part == 1:
                    pe.wait_ge(sems["sc_p"], at(pe, "sc_p", l, 1))
                    apart(pe)
                    mm(ps[0:64, 5, 128:128 + 64], C("group", 64), pc[:, :], start=True, stop=True).then_inc(sems["pg_ps"], 1)

            def turn_s(l, n):
                u, j = TURNS[n]
                if u[0] == "lf":
                    pe.wait_ge(sems["lf_in"], at(pe, "lf_in", l, PER["lf_in"]))
                elif u[0][0] != "p":
                    s = unit_in(pe, l, u)
                if u[0] in ("p_cmp", "p_sel", "p_win", "p_fox"):
                    i = ("p_sel", "p_win", "p_fox").index(u[0]) if u[0] != "p_cmp" else 0
                    pe.wait_ge(sems["s_p"], at(pe, "s_p", l, i + 1))
                if u[0] == "p_new":
                    pe.wait_ge(sems["dg"], at(pe, "dg", l, 3))
                pe.wait_ge(sems["kt_ev"], at(pe, "kt_ev", l, CMPT + n))
                bank = ps[:, 4, :]
                if u[0][0] == "p" or u[0] == "lf":
                    apart(pe)
                if u[0] == "lf":
                    for h in range(4):
                        last = tp(bank[:, h * 64:(h + 1) * 64], LFP[:, h:512:4], 64)
                elif u[0] == "p_cmp":
                    last = tp(ps[0:NCS, 4, 0:64], pc[:, 0:NCS], 64)
                elif u[0] == "p_sel":
                    for i in range(NPG):
                        last = tp(bank[:, i * 64:(i + 1) * 64], SS[0:64, i * P:(i + 1) * P], 64)
                elif u[0] == "p_win":
                    for i in range(4):
                        last = tp(bank[:, i * 64:(i + 1) * 64], SW[0:64, i * P:(i + 1) * P], 64)
                elif u[0] == "p_fox":
                    for i in range(NPG):
                        last = tp(bank[:, i * 32:(i + 1) * 32], SF[0:32, i * P:(i + 1) * P], 32)
                elif u[0] == "p_new":
                    mm(ps[0:NS, 4, 0:64], C("row8", 64), dg[:, 0, :], start=True, stop=True)
                    mm(ps[0:NS, 4, 64:128], C("row8", 64), dg[:, 1, :], start=True, stop=True)
                    last = mm(ps[0:NS, 4, 128:160], C("row4", 32), dg[0:32, 2, 0:32], start=True, stop=True)
                else:
                    v = s.rearrange("p (j c) -> p j c", c={"selk": 128, "wink": 128}.get(u[0], 256))
                    for i in range(4):
                        if u[0] in ("selk", "wink"):
                            last = tp(bank[:, i * P:(i + 1) * P], v[:, 4 * j + i, :], P)
                        else:
                            last = tp(bank[:, i * P:(i + 1) * P], v[:, i, j * P:(j + 1) * P], P)
                last.then_inc(sems["kt_ps"], 1)

            def score_s(l, n):
                u, j = TURNS[n]
                if u[0][0] == "p" or u[0] == "lf":
                    return
                kind, b, h = u
                pe.wait_ge(sems["kt_ev"], at(pe, "kt_ev", l, CMPT + n + 1))
                kt = KT[:, SCORE_OF[n] % 2, :]
                if kind == "selk":
                    last = mm(ps[0:64, 6 + j, :], qn[:, b, :], kt, start=b == 0, stop=b == NS - 1)
                elif kind == "wink":
                    if b == 0:
                        pe.wait_ge(sems["s_ev"], at(pe, "s_ev", l, 1))
                    last = mm(ps[0:64, 6, :], qn[:, b, :], kt, start=b == 0, stop=b == NS - 1)
                else:
                    if b == 0 and h == 0 and j == 0 and kind == "fxk":
                        pe.wait_ge(sems["s_ev"], at(pe, "s_ev", l, 2))
                    q, r = (qf, slice(0, 32)) if kind == "fxk" else (qs, slice(32, 64))
                    last = mm(ps[r, 6 + h, :], q[:, j, b, :], kt, start=b == 0 and j == 0, stop=True, skip_group_check=True)
                last.then_inc(sems["smm"], 1)

            def news(l, c):
                if c:
                    pe.wait_ge(sems["s_ev"], at(pe, "s_ev", l, c))
                else:
                    pe.wait_ge(sems["drop"], at(pe, "drop", l, 1))
                if c == 2:
                    pe.wait_ge(sems["kt_ev"], at(pe, "kt_ev", l, CMPT + TURN_OF[("lf",), 0] + 1))
                    for j in range(NPG):
                        for h in range(2):
                            w = min((j + 1) * P - h * 512, 512)
                            if w > 0:
                                a = (7 - j) * P + h * 512
                                mm(ps[0:32, 6 + h, 0:w], LF[:, j, :, :].rearrange("p b h -> p (b h)"), cum_bwd[:, a:a + w],
                                   start=False, stop=True, skip_group_check=True)
                pts = ([SELK], [WINK], [FXK, FXK + 1])[c]
                n = 0
                for b in range(NS):
                    for f, t in enumerate(pts):
                        q = qf[:, f, b, :] if c == 2 else qn[:, b, :]
                        last = mm(ps[0:32 if c == 2 else 64, 5, c:c + 1], q, PT[:, t, SEQ + b:SEQ + b + 1], start=n == 0, stop=n == NS * len(pts) - 1)
                        n += 1
                last.then_inc(sems["snew"], 1)

            def zs(l, part):
                if part == 1:
                    pe.wait_ge(sems["s_ev"], at(pe, "s_ev", l, 4))
                    apart(pe)
                    for j in range(NPG):
                        last = nc.tensor.transpose(ps[:, 7, j * 32:(j + 1) * 32], ZS[:, j * P:(j + 1) * P], ident[64:96, 64:96])
                    last.then_inc(sems["zt_ps"], 1)
                elif part == 2:
                    pe.wait_ge(sems["z_sp"], at(pe, "z_sp", l, 1))
                    mm(ps[:, 5, 0:256], C("nupper"), zsp[:, :], start=True, stop=True, skip_group_check=True)
                    for k in range(1, NPG):
                        last = mm(ps[:, 5, 0:(NPG - k) * 32], C("nones"), zsp[:, k * 32:256], start=False, stop=True, skip_group_check=True)
                    last.then_inc(sems["zc_ps"], 1)

            def value_s(l, n):
                kind, b, h = UNITS[n]
                sk = dict(stop=True, skip_group_check=True)
                if n == NKU:
                    pe.wait_ge(sems["kt_ev"], at(pe, "kt_ev", l, CMPT + len(TURNS)))
                    pe.wait_ge(sems["z_w"], at(pe, "z_w", l, 1))
                    mm(ps[:, 6, 0:64], vnew[:, 0, :], DM[:, 0:64], start=True, **sk)
                    mm(ps[:, 6, 0:64], vnew[:, 1, :], DM[:, 64:128], start=False, **sk)
                    for c in range(NS):
                        mm(ps[:, 6, c * 8:(c + 1) * 8], cvS[:, c, :], pcT[0:NCS, c * 8:(c + 1) * 8], start=False, **sk)
                    for f in range(2):
                        mm(ps[:, 6, 64 + f * 16:64 + (f + 1) * 16], vnew[:, 4 + f, :],
                           DM[:, 128:160].rearrange("a (b h) -> a b h", h=4)[:, :, 2 * f:2 * f + 2], start=False, **sk)
                s = unit_in(pe, l, UNITS[n])
                bank = ps[:, 4 + 3 * (b % 2), :]
                if kind == "selv" and b >= 2:
                    pe.wait_ge(sems["acc_up"], at(pe, "acc_up", l, b - 1))
                if kind in ("selv", "winv"):
                    s = s.rearrange("p (j c) -> p j c", j=8)
                    p, n_t = (PTs, NPG) if kind == "selv" else (PTw, 4)
                    for j in range(n_t):
                        last = mm(bank[0:64, 0:P], p[:, j, :], s[:, j, :], start=kind == "selv" and j == 0, **sk)
                else:
                    s = s.rearrange("p (j c) -> p j c", j=4)
                    p, rows = (PTf, slice(64, 96)) if kind == "fxv" else (zw, slice(96, 128))
                    for j in range(4):
                        last = mm(bank[rows, 0:256], p[:, 4 * h + j, :], s[:, j, :], start=h == 0 and j == 0, **sk)
                last.then_inc(sems["v_used"], 1)

            def attend(l):
                pe.wait_ge(sems["cum_ev"], at(pe, "cum_ev", l, 1))
                pe.wait_ge(sems["cvt_ev"], at(pe, "cvt_ev", l, 1))
                pe.wait_ge(sems["cvs_ev"], at(pe, "cvs_ev", l, 2))
                pe.wait_ge(sems["q_ev"], at(pe, "q_ev", l, 1))
                for part in PLAN:
                    {"scores": scores, "turn": turn, "values": values, "stick": stick, "behind": behind, "stick_v": stick_v,
                     "sc": sc, "turn_s": turn_s, "score_s": score_s, "news": news, "zs": zs, "value_s": value_s}.get(
                        part[0], lambda *_: None)(l, *part[1:])
                pe.wait_ge(sems["acc_up"], at(pe, "acc_up", l, NS))
                apart(pe)
                sk = dict(start=False, stop=True, skip_group_check=True)
                mm(ps[:, 6, 0:64], acc[:, 0:P], ident[:, 0:64], **sk)
                for p, o in ((64, 64), (96, 96)):
                    one = ident[:, p:p + 32].rearrange("a (b h) -> a b h", h=4)
                    for f in range(2):
                        last = mm(ps[:, 6, o + f * 16:o + (f + 1) * 16], acc[:, f * P:(f + 1) * P], one[:, :, 2 * f:2 * f + 2], **sk)
                last.then_inc(sems["so_ps"], 1)

            OT = [[0, 1, 2, 3], [SBQ, SBQ + 1], [FXQ, FXQ + 1]]

            def merge(l):
                pe.wait_ge(sems["so_ev"], at(pe, "so_ev", l, 1))
                pe.wait_ge(sems["o_ev"], at(pe, "o_ev", l, 8))
                n = 0
                for hf in range(2):
                    w = weights_in(pe, l, ("up", hf))
                    for br in range(3):
                        k0 = (0, 4, 6)[br]
                        for c in range(4):
                            if n >= 4:
                                pe.wait_ge(sems["mt_ev"], at(pe, "mt_ev", l, n - 3))
                            tile(2 * (n % 4), [(w[:, (k0 + k) * 512 + c * P:(k0 + k) * 512 + (c + 1) * P], PT[:, t, :]) for k, t in enumerate(OT[br])]
                                 ).then_inc(sems["mt_ps"], 1)
                            n += 1
                    for br in range(3):
                        w = weights_in(pe, l, ("mg", hf, br)).rearrange("p (k n) -> p k n", k=KD)
                        for c in range(4):
                            pe.wait_ge(sems["mt_ev"], at(pe, "mt_ev", l, n - 3))
                            tile(2 * (n % 4), [(w[:, k, c * P:(c + 1) * P], hT[:, k, :]) for k in range(KD)]).then_inc(sems["mt_ps"], 1)
                            n += 1
                for hf in range(2):
                    w = weights_in(pe, l, ("out", hf)).rearrange("p (k n) -> p k n", k=KD)
                    for c in range(4):
                        if n < 52:
                            pe.wait_ge(sems["mt_ev"], at(pe, "mt_ev", l, n - 3))
                        else:
                            pe.wait_ge(sems["x_upd"], at(pe, "x_upd", l, n - 51))
                        if hf == 0 and c == 0:
                            pe.wait_ge(sems["u_ready"], at(pe, "u_ready", l, 8))
                        tile(2 * (n % 4), [(w[:, k, c * P:(c + 1) * P], PT[:, UT[k], :]) for k in range(KD)]).then_inc(sems["mt_ps"], 1)
                        n += 1

            def ffn(l):
                for i in range(NF):
                    w = weights_in(pe, l, ("ffn", i // 2)).rearrange("p (j k n) -> p j k n", j=2, k=KD)
                    c = slice((i % 2) * P, (i % 2 + 1) * P)
                    if i >= 2:
                        pe.wait_ge(sems["ffn_s"], at(pe, "ffn_s", l, i - 1))
                    tile(2 * (i % 2), [(w[:, 0, k, c], hT[:, k, :]) for k in range(KD)],
                         lambda k: pe.wait_ge(sems["h_ready"], at(pe, "h_ready", l, KD + k + 1)) if i == 0 else None).then_inc(sems["ffn_g"], 1)
                    if i >= 2:
                        pe.wait_ge(sems["hid"], at(pe, "hid", l, i - 1))
                    tile(4 + 2 * (i % 2), [(w[:, 1, k, c], hT[:, k, :]) for k in range(KD)]).then_inc(sems["ffn_u"], 1)
                pe.wait_ge(sems["hid"], at(pe, "hid", l, NF))
                for n in range(4):
                    if n >= 2:
                        pe.wait_ge(sems["x_upd"], at(pe, "x_upd", l, KD + 2 * (n - 1)))
                    for h in range(2):
                        w = weights_in(pe, l, ("down", n, h))[:, 0:NF // 2 * 256].rearrange("p (k n) -> p k n", k=NF // 2)
                        for k in range(NF // 2):
                            for c in range(2):
                                for t in range(2):
                                    last = mm(ps[:, 4 * (n % 2) + 2 * c + t, 0:H2], w[:, k, c * P:(c + 1) * P], PT[:, h * (NF // 2) + k, t * H2:(t + 1) * H2],
                                              start=h == 0 and k == 0, stop=h == 1 and k == NF // 2 - 1)
                        last.then_inc(sems["down_ps"], 1)

            with pe.Fori(0, DEPTH) as i:
                l = in_layers(pe, i)
                norm(l, 0)
                project(l)
                compress(l)
                attend(l)
                merge(l)
                norm(l, 1)
                ffn(l)
            norm(DEPTH, 0)
            for k in range(KD):
                pe.wait_ge(sems["h_ready"], at(pe, "h_ready", DEPTH, k + 1))
                if k >= 2:
                    pe.wait_ge(sems["y_ev"], k - 1)
                for t in range(TT):
                    tp(ps[:, 4 + 2 * (k % 2), t * P:(t + 1) * P], hT[:, k, t * P:(t + 1) * P], P)
                tp(ps[0:NS, 5 + 2 * (k % 2), 0:P], hT[:, k, SEQ:T], P).then_inc(sems["y_ps"], 1)

        @block.scalar
        def _(act):
            fn = nc.scalar.activation
            act.wait_ge(sems["const_ok"], 1)
            act.wait_ge(sems["init_z"], 2)

            def norm(l, w):
                for k in range(KD):
                    act.wait_ge(sems["x_upd"], at(act, "x_upd", l, k + 1)) if w else act.wait_ge(sems["x_upd"], count(act, l, PER["x_upd"], k + 1))
                    if k >= 2:
                        act.wait_ge(sems["sq_used"], at(act, "sq_used", l, w * KD + k - 1))
                    fn(sq[:, k % 2, :], xT[:, k, :], ACT.Square).then_inc(sems["sq_ready"], 1)
                act.wait_ge(sems["sq_used"], at(act, "sq_used", l, (w + 1) * KD))
                fn(half(rs), pair(0), ACT.Sqrt, bias=epsb[:, 0:1], scale=1.0 / D).then_inc(sems["rs_ready"], 1)

            def project(l):
                rows = lambda a: a.rearrange("p (t c) -> p t c", t=TT)
                names = {CMPK: ("cmp", 0), CMPV: ("cmp", P), SELK: ("sel", 0), SELV: ("sel", P), WINK: ("win", 0), WINV: ("win", P),
                         SBK: ("sb", 0), SBK + 1: ("sb", P), SBV: ("sb", 256), SBV + 1: ("sb", 256 + P),
                         FXK: ("fox", 0), FXK + 1: ("fox", P), FXV: ("fox", 256), FXV + 1: ("fox", 256 + P)}

                def store(n):
                    t = NAT[n]
                    act.wait_ge(sems["nat_ev"], at(act, "nat_ev", l, n + 1))
                    src = vnat[:, NATV.index(t), :, :] if t in NATV else rows(knat[:, NATK.index(t), :])
                    name, c0 = names[t]
                    dst = out["p_" + name].rearrange("l a (t p) k h d -> (l a) p t (k h d)", p=P)[dl[0]][:, :, c0:c0 + P]
                    act.dma_start(dst, src).then_inc(sems["out_dma"], 16)

                def store_new(name, n, w):
                    if name == "win":
                        dst = out["s_win"].rearrange("l b r k h d -> l b r (k h d)")[dl[0]][:, WIN - 1, :]
                    else:
                        dst = out["s_" + name].rearrange("l b s k h d -> l (b s) (k h d)")[dl[0]]
                    act.dma_start(dst, natS[0:NS, n:n + w, :].rearrange("p a b -> p (a b)")).then_inc(sems["out_dma"], 16)

                def gates():
                    act.wait_ge(sems["gate_ev"], at(act, "gate_ev", l, 1))
                    fn(gnat[:, :, 0:24], gnat[:, :, 0:24], ACT.Sigmoid)
                    fn(gsmp[:, 0:24], gsmp[:, 0:24], ACT.Sigmoid).then_inc(sems["gate_sig"], 1)
                    fn(lft[:, :, :], lfn[:, :, :], ACT.Abs)
                    fn(lfst[:, :], lfs[:, :], ACT.Abs).then_inc(sems["lf_abs"], 1)
                    act.wait_ge(sems["lf_abs"], at(act, "lf_abs", l, 1))
                    link(fn(lft[:, :, :], lft[:, :, :], ACT.Exp, scale=-1.0))
                    link(fn(lfst[:, :], lfst[:, :], ACT.Exp, scale=-1.0))
                    fn(lft[:, :, :], lft[:, :, :], ACT.Ln, bias=1.0)
                    fn(lfst[:, :], lfst[:, :], ACT.Ln, bias=1.0).then_inc(sems["lf_ln"], 1)

                stored = 0
                for i in range(NT):
                    act.wait_ge(sems["proj_ps"], at(act, "proj_ps", l, i + 1))
                    fn(half(PT[:, i, :]), pair(2 * (i % 2)), ACT.Copy, scale=SCALE if i in QTILES else 1.0).then_inc(sems["proj_ev"], 1)
                    while stored < len(NAT) and NAT[stored] <= i - 4:
                        store(stored)
                        stored += 1
                    if i == 14:
                        gates()
                while stored < len(NAT):
                    store(stored)
                    stored += 1
                act.wait_ge(sems["new_ev"], at(act, "new_ev", l, 1))
                for name, n, w in STORED:
                    store_new(name, n, w)
                act.wait_ge(sems["lf_done"], at(act, "lf_done", l, 1))
                with nc.allow_non_contiguous_dma(reason="gates and log-forget values: a few kilobytes"):
                    act.dma_start(out["p_logf"].rearrange("l a (t p) h -> (l a) p t h", p=P)[dl[0]], lfn[:, :, :]).then_inc(sems["out_dma"], 16)
                    act.dma_start(out["s_logf"].rearrange("l b s h -> l (b s) h")[dl[0]], lfs[:, :]).then_inc(sems["out_dma"], 16)
                    act.wait_ge(sems["gate_sig"], at(act, "gate_sig", l, 1))
                    act.dma_start(g64[:, :], gsmp[:, 0:24]).then_inc(sems["sig_dma"], 16)
                    act.dma_start(l32[:, :], lfs[:, :]).then_inc(sems["sig_dma"], 16)
                act.wait_ge(sems["sig_dma"], at(act, "sig_dma", l, 32))
                act.wait_ge(sems["out_dma"], at(act, "out_dma", l, PER["out_dma"]))
                act.sem_inc(sems["new_ready"], 1)
                for kv in range(2):
                    fn(KC[:, kv, 2 * PAST:2 * PAST + SEQ], PT[:, CMPK + kv, 0:SEQ], ACT.Copy)
                    fn(KC[:, kv, 2 * PAST + SEQ:2 * PAST + SEQ + CBLK], posL[:, :], ACT.Copy).then_inc(sems["kc_own"], 1)

            acts, layer, dl = [0], [0], [0]

            def link(ins):
                acts[0] += 1
                ins.then_inc(sems["act_chain"], 1)
                act.wait_ge(sems["act_chain"], count(act, layer[0], ACT_CHAIN, acts[0]))

            def exponentials(l, n):
                u, i = ITEMS[n]
                w = NCP if SOFT[u][1] == "cmp" else (i + 1) * P
                act.wait_ge(sems["nm_ready"], at(act, "nm_ready", l, n + 1))
                if n >= 2:
                    act.wait_ge(sems["pt_ps"], at(act, "pt_ps", l, 2 * (n - 1)))
                for hh in range(2):
                    last = fn(Pb[:, n % 2, hh, 0:w], ps[:, hh, 0:w], ACT.Exp, bias=nm[:, n % 2, hh:hh + 1], accum_out=sm[:, n % 2, hh:hh + 1])
                last.then_inc(sems["exp_done"], 1)

            def turn(l, n, hh):
                if hh:
                    return
                u, i = ITEMS[n]
                act.wait_ge(sems["pt_ps"], at(act, "pt_ps", l, 2 * n + 1))
                if i == 0 and u >= 1:
                    act.wait_ge(sems["pv_done"], at(act, "pv_done", l, u))
                if SOFT[u][1] == "cmp":
                    fn(PTb[0:NCP, 0, 0, i * P:(i + 1) * P], ps[0:NCP, 2, 0:P], ACT.Copy).then_inc(sems["pt_ev_a"], 1)
                else:
                    fn(PTb[:, 0, 0:i + 1, i * P:(i + 1) * P], ps[:, 2, 0:(i + 1) * P].rearrange("p (j c) -> p j c", c=P), ACT.Copy
                       ).then_inc(sems["pt_ev_a"], 1)

            def values(l, u):
                idx, br = SOFT[u]
                if br in ("win", "fox"):
                    act.wait_ge(sems["pv_done"], at(act, "pv_done", l, u + 1))
                    fn(PT[:, idx if idx < 4 else FXQ + idx - 4, 0:SEQ], ps[:, 3, :], ACT.Copy).then_inc(sems["o_ev"], 1)

            zp = ps[:, 0:3, :].rearrange("p b c -> p (b c)")[:, 0:1280]

            def stick(l, hd):
                act.wait_ge(sems["sbz_ps"], at(act, "sbz_ps", l, hd + 1))
                if hd == 0:
                    act.wait_ge(sems["pv_done"], at(act, "pv_done", l, len(SOFT)))
                else:
                    act.wait_ge(sems["sb_sp"], at(act, "sb_sp", l, hd))
                link(fn(zt, zp, ACT.Abs))
                link(fn(zt, zt, ACT.Exp, scale=-1.0))
                fn(zt, zt, ACT.Ln, bias=1.0).then_inc(sems["sb_ln"], 1)

            def behind(l, hd):
                act.wait_ge(sems["sbc_ps"], at(act, "sbc_ps", l, hd + 1))
                if hd:
                    act.wait_ge(sems["sb_pv"], at(act, "sb_pv", l, hd))
                fn(wb, zp, ACT.Exp).then_inc(sems["sb_w"], 1)

            def stick_v(l, hd):
                if hd % 2:
                    act.wait_ge(sems["sb_pv"], at(act, "sb_pv", l, hd + 1))
                    fn(PT[:, SBQ + hd // 2, 0:SEQ], ps[:, 3, :], ACT.Copy).then_inc(sems["o_ev"], 1)

            def sc(l, part):
                if part == 0:
                    act.wait_ge(sems["sc_nm"], at(act, "sc_nm", l, 1))
                    fn(pc[:, 0:NCS], ps[0:64, 5, 64:64 + NCS], ACT.Exp, bias=s1[:, 0:1], accum_out=s1[:, 1:2]).then_inc(sems["sc_exp"], 1)

            def soft(l, i):
                S, rows = ((SS, 64), (SW, 64), (SF, 32))[i]
                act.wait_ge(sems["s_nm"], at(act, "s_nm", l, i + 1))
                fn(S[0:rows], S[0:rows], ACT.Exp, bias=s1[0:rows, 4 + 4 * i:5 + 4 * i], accum_out=s1[0:rows, 5 + 4 * i:6 + 4 * i]).then_inc(sems["s_exp"], 1)

            def zs(l, part):
                if part == 1:
                    act.wait_ge(sems["zt_ps"], at(act, "zt_ps", l, 1))
                    link(fn(za, ps[:, 7, 0:256], ACT.Abs))
                    link(fn(za, za, ACT.Exp, scale=-1.0))
                    fn(za, za, ACT.Ln, bias=1.0).then_inc(sems["z_abs"], 1)
                elif part == 3:
                    act.wait_ge(sems["z_sum"], at(act, "z_sum", l, 1))
                    fn(zw[:, :, :].rearrange("p j c -> p (j c)"), za, ACT.Exp).then_inc(sems["z_w"], 1)

            def attend(l):
                for part in PLAN:
                    {"exp": exponentials, "turn": turn, "values": values, "stick": stick, "behind": behind, "stick_v": stick_v,
                     "sc": sc, "soft": soft, "zs": zs}.get(part[0], lambda *_: None)(l, *part[1:])

            def merge(l):
                for n in range(48):
                    act.wait_ge(sems["mt_ps"], at(act, "mt_ps", l, n + 1))
                    hf, m = n // 24, n % 24
                    if m < 12:
                        if n >= 24:
                            act.wait_ge(sems["u_ready"], at(act, "u_ready", l, 4))
                        fn(half(UP[:, m, :]), pair(2 * (n % 4)), ACT.Copy).then_inc(sems["mt_ev"], 1)
                    else:
                        k = 12 * hf + m - 12
                        if k >= 2:
                            act.wait_ge(sems["mul"], at(act, "mul", l, k - 1))
                        fn(half(sg[k % 2]), pair(2 * (n % 4)), ACT.Sigmoid).then_inc(sems["mt_ev"], 1)

            def ffn(l):
                for i in range(NF):
                    act.wait_ge(sems["ffn_g"], at(act, "ffn_g", l, i + 1))
                    if i >= 2:
                        act.wait_ge(sems["hid"], at(act, "hid", l, i - 1))
                    fn(half(fs[:, i % 2, :]), pair(2 * (i % 2)), ACT.Silu).then_inc(sems["ffn_s"], 1)

            with act.Fori(0, DEPTH) as i:
                dl[0] = i
                l = layer[0] = in_layers(act, i)
                norm(l, 0)
                project(l)
                attend(l)
                merge(l)
                norm(l, 1)
                ffn(l)
            assert acts[0] == ACT_CHAIN, acts
            norm(DEPTH, 0)
            act.wait_ge(sems["y_ev"], KD)
            act.dma_start(out["y_prompt"][0].rearrange("(t p) d -> p t d", p=P), PT[:, 0:8, :].rearrange("p a b -> p (a b)")[:, 0:4096]
                          .rearrange("p (t d) -> p t d", t=TT)).then_inc(sems["y_dma"], 16)
            act.dma_start(out["y_sample"].rearrange("b s d -> (b s) d"), PT[0:NS, 8:10, :].rearrange("p a b -> p (a b)")[:, 0:D]).then_inc(sems["y_dma"], 16)
            act.wait_ge(sems["y_dma"], 32)
            act.wait_ge(sems["out_dma"], DEPTH * PER["out_dma"])

        @block.gpsimd
        def _(pool):
            with pool.Fori(0, DEPTH) as i0:
                l = in_layers(pool, i0)
                for j, c in enumerate((3, 5)):
                    pool.wait_ge(sems[chunk_read[c][0]], at(pool, chunk_read[c][0], l, chunk_read[c][1]))
                    apart(pool)
                    nc.gpsimd.memset(WC[j][0:DH, :, DH:P], 0.0)
                    nc.gpsimd.memset(WC[j][DH:P, :, 0:DH], 0.0).then_inc(sems["cmp_zero"], 1)
                for n, (u, i) in enumerate(ITEMS):
                    idx, br = SOFT[u]
                    b = n % 2
                    w = NCP if br == "cmp" else (i + 1) * P
                    pool.wait_ge(sems["rr_ready"], at(pool, "rr_ready", l, n + 1))
                    apart(pool)
                    for hh in range(2):
                        p, one = Pb[:, b, hh, 0:w], rr[:, b, hh:hh + 1]
                        if br == "fox":
                            last = nc.gpsimd.tensor_scalar(p, p, one, None, ALU.mult)
                        else:
                            c = (idx + 4 * hh) * 3 + ("cmp", "sel", "win").index(br)
                            last = nc.gpsimd.tensor_scalar(p, p, one, gnat[:, i, c:c + 1], ALU.mult, ALU.mult)
                    last.then_inc(sems["p_scaled"], 1)

        @block.vector
        def _(dve):
            v = nc.vector
            chain, layer = [0], [0]

            def link(ins):
                chain[0] += 1
                ins.then_inc(sems["dve_chain"], 1)
                dve.wait_ge(sems["dve_chain"], count(dve, layer[0], DVE_CHAIN, chain[0]))

            def own(ins, name, l, n):
                ins.then_inc(sems[name], 1)
                dve.wait_ge(sems[name], at(dve, name, l, n))

            dve.wait_ge(sems["const_in"], 16 * 12)
            v.memset(epsb[:, :], EPS)
            v.tensor_copy(identb, ident)
            last = v.tensor_copy(maskb[:, P:4 * P], hT[:, :, :].rearrange("p a b -> p (a b)")[:, 0:3 * P])
            last.then_inc(sems["const_ok"], 1)
            for b in (qn[:, :, :], qs[:, :, :, :], qf[:, :, :, :], pc[:, :], pgb[:, :]):
                last = v.memset(b, 0.0)
            last.then_inc(sems["init_z"], 1)
            dve.wait_ge(sems["init_z"], 1)
            for k in range(KD):
                dve.wait_ge(sems["xt_ps"], k + 1)
                v.tensor_copy(xT[:, k, 0:SEQ], ps[:, 2 * (k % 2), :])
                v.tensor_copy(xT[:, k, SEQ:T], ps[:, 2 * (k % 2) + 1, 0:NS]).then_inc(sems["x_upd"], 1)
            dve.wait_ge(sems["post_ps"], 1)
            v.tensor_copy(posT[:, :, :], ps[:, 4, 0:DEPTH * CBLK].rearrange("p (l c) -> p l c", l=DEPTH)).then_inc(sems["init_z"], 1)
            dve.wait_ge(sems["init_z"], 2)

            def norm(l, w, g):
                dve.wait_ge(sems["rs_ready"], at(dve, "rs_ready", l, w + 1))
                link(v.reciprocal(rinv, rs))
                if w:
                    dve.wait_ge(sems["mt_ps"], at(dve, "mt_ps", l, 48))
                for k in range(KD):
                    v.scalar_tensor_tensor(hT[:, k, :], xT[:, k, :], g(k), rinv, ALU.mult, ALU.mult).then_inc(sems["h_ready"], 1)

            def project(l):
                def rope(i):
                    r = ROPE.index(i)
                    dve.wait_ge(sems["proj_ev"], at(dve, "proj_ev", l, i + 1))
                    dve.wait_ge(sems["rot_ps"], at(dve, "rot_ps", l, r + 1))
                    v.tensor_tensor(half(ropet), pair(4), half(C("sin")), ALU.mult)
                    link(v.tensor_tensor(PT[:, i, :], PT[:, i, :], C("cos"), ALU.mult))
                    v.tensor_tensor(PT[:, i, :], PT[:, i, :], ropet, ALU.add).then_inc(sems["rope_done"], 1)

                def nat(i):
                    n = NAT.index(i)
                    dve.wait_ge(sems["nat_ps"], at(dve, "nat_ps", l, n + 1))
                    dst = vnat[:, NATV.index(i), :, :].rearrange("p t c -> p (t c)") if i in NATV else knat[:, NATK.index(i), :]
                    v.tensor_copy(dst, ps[:, 6 + n % 2, :]).then_inc(sems["nat_ev"], 1)

                for i in range(NT + 2):
                    if i == WINK:
                        dve.wait_ge(sems["gate_ps"], at(dve, "gate_ps", l, 1))
                        v.tensor_copy(gnat[:, :, :], ps[:, 5, 264:264 + 28 * TT].rearrange("p (t c) -> p t c", t=TT))
                        link(v.tensor_copy(gsmp[:, :], ps[0:NS, 4, 264:292]))
                        b = bfl[:, :]
                        v.tensor_tensor(lfn[:, :, :], gnat[:, :, 24:28], b.rearrange("p (a h) -> p a h", a=1).broadcast_to([P, TT, 4]), ALU.add)
                        v.tensor_tensor(lfs[:, :], gsmp[:, 24:28], b[0:NS, :], ALU.add).then_inc(sems["gate_ev"], 1)
                    if i < NT and i in ROPE:
                        rope(i)
                    if i - 1 in NAT:
                        nat(i - 1)
                dve.wait_ge(sems["new_ps"], at(dve, "new_ps", l, 1))
                for n in range(0, len(NAT), 4):
                    w = min(4, len(NAT) - n)
                    last = v.tensor_copy(natS[0:NS, n:n + w, :].rearrange("p a b -> p (a b)"), ps[0:NS, n // 4, 0:w * P])
                last.then_inc(sems["new_ev"], 1)
                dve.wait_ge(sems["new_ev"], at(dve, "new_ev", l, 1))
                for i, t in enumerate(NATV):
                    v.tensor_copy(vnew[:, i, :], natS[0:NS, NAT.index(t), :])
                dve.wait_ge(sems["gate_ev"], at(dve, "gate_ev", l, 1))
                dve.wait_ge(sems["lf_ln"], at(dve, "lf_ln", l, 1))
                v.scalar_tensor_tensor(lfn[:, :, :], lfn[:, :, :], 0.0, lft[:, :, :], ALU.min, ALU.subtract)
                v.scalar_tensor_tensor(lfs[:, :], lfs[:, :], 0.0, lfst[:, :], ALU.min, ALU.subtract).then_inc(sems["lf_done"], 1)
                for g in range(G):
                    r = slice(g * DH, (g + 1) * DH)
                    dst = qn[r, :, :].rearrange("p b c -> p (b c)")
                    for t in range(4):
                        v.tensor_copy(dst[:, g * 4 + t:g * 4 + t + 72 * 7 + 1:72], PT[r, t, SEQ:T])
                    for f in range(2):
                        c = 2 * f + g
                        v.tensor_copy(qs[r, f, :, :].rearrange("p b c -> p (b c)")[:, c:c + 36 * 7 + 1:36], PT[r, SBQ + f, SEQ:T])
                        last = v.tensor_copy(qf[r, f, :, :].rearrange("p b c -> p (b c)")[:, c:c + 36 * 7 + 1:36], PT[r, FXQ + f, SEQ:T])
                last.then_inc(sems["q_ev"], 1)
                dve.wait_ge(sems["cum_ps"], at(dve, "cum_ps", l, 1))
                v.tensor_scalar(ncum[:, :], ps[0:4, 4, :], -1.0, None, ALU.mult).then_inc(sems["cum_ev"], 1)

            def compress(l):
                dve.wait_ge(sems["new_ready"], at(dve, "new_ready", l, 1))

                def turned(q, kv):
                    for u in range(4):
                        step = 8 * q + 4 * kv + u
                        dve.wait_ge(sems["kt_ps"], at(dve, "kt_ps", l, step + 1))
                        v.tensor_copy(KC[:, kv, u * 512:(u + 1) * 512], ps[:, 6 + step % 2, :]).then_inc(sems["kt_ev"], 1)

                def compressed(q, kv):
                    dve.wait_ge(sems["cs_ps"], at(dve, "cs_ps", l, 2 * q + kv + 1))
                    if q == 0:
                        link(v.tensor_copy(cbias[:, kv:kv + 1], ps[:, 4 + kv, W_POS:W_POS + 1]))
                        last = v.tensor_scalar(ckP[:, kv, 0:NCP], ps[:, 4 + kv, W_OWN:W_OWN + NCP], cbias[:, kv:kv + 1], None, ALU.add)
                        if kv:
                            last.then_inc(sems["ck_ev"], 1)
                    v.tensor_scalar(cvT[:, :, :] if kv else ckT[:, 2 * q:2 * q + 2, :],
                                    ps[:, 4 + kv, 0:W_OWN].rearrange("p (b n) -> p b n", b=2)[:, :, 0:NCS], cbias[:, kv:kv + 1], None, ALU.add
                                    ).then_inc(sems["cs_ev"], 1)

                turned(0, 0)
                turned(0, 1)
                for q in range(4):
                    compressed(q, 0)
                    if q < 3:
                        turned(q + 1, 0)
                    compressed(q, 1)
                    if q < 3:
                        turned(q + 1, 1)
                    if q == 0:
                        dve.wait_ge(sems["cvt_ps"], at(dve, "cvt_ps", l, 1))
                        v.tensor_copy(cvP[0:NCP, :], ps[0:NCP, 1, 0:P]).then_inc(sems["cvt_ev"], 1)
                    if q % 2:
                        dve.wait_ge(sems["cvs_ps"], at(dve, "cvs_ps", l, q // 2 + 1))
                        v.tensor_copy(cvS[:, 2 * q - 2:2 * q + 2, :].rearrange("p b n -> p (b n)"), ps[0:NCS, 0, :]).then_inc(sems["cvs_ev"], 1)

            def scores(l, n):
                u, i = ITEMS[n]
                w = NCP if SOFT[u][1] == "cmp" else (i + 1) * P
                dve.wait_ge(sems["s_ps"], at(dve, "s_ps", l, n + 1))
                v.tensor_reduce(nm[:, n % 2, :], ps[:, 0:2, 0:w], AX.X, ALU.max, negate=True).then_inc(sems["nm_ready"], 1)

            def weigh(l, n):
                u, i = ITEMS[n]
                b = n % 2
                dve.wait_ge(sems["exp_done"], at(dve, "exp_done", l, n + 1))
                if SOFT[u][1] == "cmp":
                    m = CONST["cmp01"][0] + i * 32
                    link(v.tensor_tensor(Pb[:, b, :, 0:NCP], Pb[:, b, :, 0:NCP],
                                         cst[:, m:m + NCP].rearrange("p (a c) -> p a c", a=1).broadcast_to([P, 2, NCP]), ALU.mult))
                    link(v.reduce_sum(sm[:, b, :], Pb[:, b, :, 0:NCP], AX.X))
                    link(v.tensor_scalar(sm[:, b, :], sm[:, b, :], 1e-30, None, ALU.max))
                v.reciprocal(rr[:, b, :], sm[:, b, :]).then_inc(sems["rr_ready"], 1)

            def turn(l, n, hh):
                if not hh:
                    return
                u, i = ITEMS[n]
                dve.wait_ge(sems["pt_ps"], at(dve, "pt_ps", l, 2 * n + 2))
                if i == 0 and u >= 1:
                    dve.wait_ge(sems["pv_done"], at(dve, "pv_done", l, u))
                if SOFT[u][1] == "cmp":
                    v.tensor_copy(PTb[0:NCP, 1, 0, i * P:(i + 1) * P], ps[0:NCP, 2, 0:P]).then_inc(sems["pt_ev_d"], 1)
                else:
                    v.tensor_copy(PTb[:, 1, 0:i + 1, i * P:(i + 1) * P], ps[:, 2, 0:(i + 1) * P].rearrange("p (j c) -> p j c", c=P)
                                  ).then_inc(sems["pt_ev_d"], 1)

            zp = ps[:, 0:3, :].rearrange("p b c -> p (b c)")[:, 0:1280]

            def stick(l, hd):
                dve.wait_ge(sems["sb_ln"], at(dve, "sb_ln", l, hd + 1))
                if hd:
                    dve.wait_ge(sems["sbc_ps"], at(dve, "sbc_ps", l, hd))
                v.scalar_tensor_tensor(spb, zp, 0.0, zt, ALU.max, ALU.add).then_inc(sems["sb_sp"], 1)

            nb = NBLK

            def sc(l, part):
                if part == 0:
                    dve.wait_ge(sems["sc_ps"], at(dve, "sc_ps", l, 1))
                    v.tensor_reduce(s1[:, 0:1], ps[0:64, 5, 64:64 + NCS], AX.X, ALU.max, negate=True).then_inc(sems["sc_nm"], 1)
                elif part == 1:
                    dve.wait_ge(sems["sc_exp"], at(dve, "sc_exp", l, 1))
                    link(v.tensor_scalar(s1[:, 2:3], s1[:, 1:2], 1e-30, None, ALU.max))
                    link(v.reciprocal(s1[:, 2:3], s1[:, 2:3]))
                    v.tensor_scalar(pc[:, 0:NCS], pc[:, 0:NCS], s1[:, 2:3], None, ALU.mult).then_inc(sems["sc_p"], 1)
                else:
                    dve.wait_ge(sems["pg_ps"], at(dve, "pg_ps", l, 1))
                    link(v.tensor_copy(pgb[:, 1:65], ps[0:64, 5, 128:192]))
                    link(v.tensor_tensor(dg[:, 0, :], pgb[:, 0:64], pgb[:, 1:65], ALU.add))
                    link(v.reduce_sum(t17[:, 0, 0:nb], dg[:, 0, :].rearrange("p (b c) -> p b c", c=4), AX.X))
                    imp = t17[:, 0, 1:nb - 1]
                    link(v.tensor_reduce(s1[:, 3:4], imp, AX.X, ALU.min))
                    link(v.tensor_scalar(t17[:, 1, 1:nb - 1], imp, s1[:, 3:4], None, ALU.is_le))
                    link(v.tensor_tensor(t17[:, 1, 1:nb - 1], t17[:, 1, 1:nb - 1], C("blk", 64), ALU.mult))
                    link(v.tensor_reduce(s1[:, 3:4], t17[:, 1, 1:nb - 1], AX.X, ALU.max))
                    link(v.memset(t17[:, 2, 0:nb], 0.0))
                    link(v.tensor_scalar(t17[:, 2, 1:nb - 1], C("blk", 64), s1[:, 3:4], NEG, ALU.is_equal, ALU.mult))
                    own(v.tensor_scalar(pc[:, 0:NCS], pc[:, 0:NCS], g64[:, 0:1], None, ALU.mult), "drop", l, 1)

            def turn_s(l, n):
                u, j = TURNS[n]
                dve.wait_ge(sems["kt_ps"], at(dve, "kt_ps", l, CMPT + n + 1))
                bank = ps[:, 4, :]
                if u[0] == "lf":
                    for hh in range(4):
                        last = v.tensor_copy(LF[:, :, :, hh], bank[:, hh * 64:(hh + 1) * 64].rearrange("p (b j) -> p j b", b=NS))
                    last.then_inc(sems["kt_ev"], 1)
                elif u[0] == "p_cmp":
                    v.tensor_copy(pcT[0:NCS, :], ps[0:NCS, 4, 0:64]).then_inc(sems["kt_ev"], 1)
                elif u[0] == "p_sel":
                    v.tensor_copy(PTs[:, :, :].rearrange("p j c -> p (j c)"), bank).then_inc(sems["kt_ev"], 1)
                elif u[0] == "p_win":
                    v.tensor_copy(PTw[:, :, :].rearrange("p j c -> p (j c)"), bank[:, 0:256]).then_inc(sems["kt_ev"], 1)
                elif u[0] == "p_fox":
                    v.tensor_copy(PTf[:, :, :].rearrange("p j c -> p (j c)"), bank[:, 0:256]).then_inc(sems["kt_ev"], 1)
                elif u[0] == "p_new":
                    v.tensor_copy(DM[:, :], ps[0:NS, 4, 0:160]).then_inc(sems["kt_ev"], 1)
                else:
                    m = SCORE_OF[n]
                    if m >= 2:
                        dve.wait_ge(sems["smm"], at(dve, "smm", l, m - 1))
                    v.tensor_copy(KT[:, m % 2, :], bank).then_inc(sems["kt_ev"], 1)

            SOFTS = ((SS, 64, 1024), (SW, 64, 512), (SF, 32, 1024))

            def soft(l, i):
                S, rows, n = SOFTS[i]
                dve.wait_ge(sems["snew"], at(dve, "snew", l, i + 1))
                v.tensor_copy(S[0:rows, n:n + 1], ps[0:rows, 5, i:i + 1])
                if i == 0:
                    own(v.tensor_tensor(SS[0:64, 0:1024].rearrange("p (b c) -> p b c", c=64),
                                        ps[0:64, 6:8, :].rearrange("p a (b c) -> p (a b) c", c=64),
                                        t17[:, 2, 0:nb].rearrange("p (b a) -> p b a", a=1).broadcast_to([64, nb, 64]), ALU.add), "s_ev", l, 1)
                elif i == 1:
                    own(v.tensor_copy(SW[0:64, 0:512], ps[0:64, 6, :]), "s_ev", l, 2)
                else:
                    own(v.tensor_scalar(SF[0:32, 0:1024], ps[0:32, 6:8, :].rearrange("p a c -> p (a c)"), l32[:, 0:1], None, ALU.add), "s_ev", l, 3)
                c = 4 + 4 * i
                v.tensor_reduce(s1[0:rows, c:c + 1], S[0:rows], AX.X, ALU.max, negate=True).then_inc(sems["s_nm"], 1)

            def weigh_s(l, i):
                S, rows, n = SOFTS[i]
                c = 4 + 4 * i
                dve.wait_ge(sems["s_exp"], at(dve, "s_exp", l, i + 1))
                link(v.reciprocal(s1[0:rows, c + 2:c + 3], s1[0:rows, c + 1:c + 2]))
                if i < 2:
                    link(v.tensor_tensor(s1[0:rows, c + 2:c + 3], s1[0:rows, c + 2:c + 3], g64[:, i + 1:i + 2], ALU.mult))
                own(v.tensor_scalar(S[0:rows], S[0:rows], s1[0:rows, c + 2:c + 3], None, ALU.mult), "s_p", l, i + 1)
                v.tensor_scalar(dg[0:rows, i, 0:rows], ident[0:rows, 0:rows], S[0:rows, n:n + 1], None, ALU.mult).then_inc(sems["dg"], 1)

            def zs(l, part):
                if part == 0:
                    v.tensor_copy(ZS, ps[32:64, 6:8, :].rearrange("p a c -> p (a c)")).then_inc(sems["s_ev"], 1)
                elif part == 2:
                    dve.wait_ge(sems["z_abs"], at(dve, "z_abs", l, 1))
                    own(v.scalar_tensor_tensor(zsp, ps[:, 7, 0:256], 0.0, za, ALU.max, ALU.add), "z_sp", l, 1)
                elif part == 3:
                    dve.wait_ge(sems["zc_ps"], at(dve, "zc_ps", l, 1))
                    link(v.tensor_copy(za, ps[:, 5, 0:256]))
                    v.tensor_tensor(za, za, ps[:, 7, 0:256], ALU.add).then_inc(sems["z_sum"], 1)

            def value_s(l, n):
                kind, b, h = UNITS[n]
                if kind != "winv":
                    return
                dve.wait_ge(sems["v_used"], at(dve, "v_used", l, n - NKU + 1))
                if b == 0:
                    v.memset(acc[0:64, P:256], 0.0)
                for rows, w in ((slice(0, 64), P), (slice(64, 128), 256)):
                    o, mine = ps[rows, 4 + 3 * (b % 2), 0:w], C("mine")[rows, b:b + 1]
                    if b == 0:
                        last = v.tensor_scalar(acc[rows, 0:w], o, mine, None, ALU.mult)
                    else:
                        last = v.scalar_tensor_tensor(acc[rows, 0:w], o, mine, acc[rows, 0:w], ALU.mult, ALU.add)
                own(last, "acc_up", l, b + 1)

            def attend(l):
                dve.wait_ge(sems["sig_dma"], at(dve, "sig_dma", l, 32))
                for part in PLAN:
                    {"scores": scores, "weigh": weigh, "turn": turn, "stick": stick, "sc": sc, "turn_s": turn_s, "soft": soft,
                     "weigh_s": weigh_s, "zs": zs, "value_s": value_s}.get(part[0], lambda *_: None)(l, *part[1:])
                dve.wait_ge(sems["so_ps"], at(dve, "so_ps", l, 1))
                for g in range(G):
                    r = slice(g * DH, (g + 1) * DH)
                    for t in range(4):
                        v.tensor_copy(PT[r, t, SEQ:T], ps[r, 6, g * 4 + t:g * 4 + t + 57:8])
                    for f in range(2):
                        v.tensor_copy(PT[r, FXQ + f, SEQ:T], ps[r, 6, 64 + f * 16 + g:64 + f * 16 + g + 15:2])
                        last = v.tensor_copy(PT[r, SBQ + f, SEQ:T], ps[r, 6, 96 + f * 16 + g:96 + f * 16 + g + 15:2])
                last.then_inc(sems["so_ev"], 1)

            def merge(l):
                for k in range(24):
                    hf, br, c = k // 12, k % 12 // 4, k % 4
                    dve.wait_ge(sems["mt_ev"], at(dve, "mt_ev", l, 24 * hf + 12 + k % 12 + 1))
                    u = PT[:, UT[4 * hf + c], :]
                    if br == 0:
                        v.tensor_tensor(u, sg[k % 2], UP[:, 4 * br + c, :], ALU.mult).then_inc(sems["mul"], 1)
                        continue
                    own(v.tensor_tensor(UP[:, 4 * br + c, :], sg[k % 2], UP[:, 4 * br + c, :], ALU.mult), "mul", l, k + 1)
                    if br == 1:
                        link(v.tensor_tensor(u, u, UP[:, 4 * br + c, :], ALU.add))
                    else:
                        v.tensor_tensor(u, u, UP[:, 4 * br + c, :], ALU.add).then_inc(sems["u_ready"], 1)
                for n in range(8):
                    dve.wait_ge(sems["mt_ps"], at(dve, "mt_ps", l, 48 + n + 1))
                    v.tensor_tensor(half(xT[:, n, :]), half(xT[:, n, :]), pair(2 * (n % 4)), ALU.add).then_inc(sems["x_upd"], 1)

            def ffn(l):
                for i in range(NF):
                    dve.wait_ge(sems["ffn_s"], at(dve, "ffn_s", l, i + 1))
                    dve.wait_ge(sems["ffn_u"], at(dve, "ffn_u", l, i + 1))
                    v.tensor_tensor(half(PT[:, i, :]), half(fs[:, i % 2, :]), pair(4 + 2 * (i % 2)), ALU.mult).then_inc(sems["hid"], 1)
                for n in range(4):
                    dve.wait_ge(sems["down_ps"], at(dve, "down_ps", l, 2 * n + 2))
                    for c in range(2):
                        v.tensor_tensor(half(xT[:, 2 * n + c, :]), half(xT[:, 2 * n + c, :]), pair(4 * (n % 2) + 2 * c), ALU.add).then_inc(sems["x_upd"], 1)

            with dve.Fori(0, DEPTH) as i:
                l = layer[0] = in_layers(dve, i)
                v.tensor_copy(gl[:, :, :], gam[:, bass.ds(2 * i, 2), :])
                v.tensor_copy(posL[:, :], posT[:, bass.ds(i, 1), :].rearrange("p a c -> p (a c)"))
                link(v.tensor_copy(bfl[:, :], bfb[:, bass.ds(i, 1), :].rearrange("p a c -> p (a c)")))
                norm(l, 0, lambda k: gl[:, 0, k:k + 1])
                project(l)
                compress(l)
                attend(l)
                merge(l)
                norm(l, 1, lambda k: gl[:, 1, k:k + 1])
                ffn(l)
            assert chain[0] == DVE_CHAIN, chain
            layer[0] = DEPTH
            chain[0] = 0
            norm(DEPTH, 0, lambda k: gam[:, 2 * DEPTH, k:k + 1])
            yp = PT[:, 0:8, :].rearrange("p a b -> p (a b)")[:, 0:4096].rearrange("p (t d) -> p t d", t=TT)
            ysm = PT[0:NS, 8:10, :].rearrange("p a b -> p (a b)")[:, 0:D]
            for k in range(KD):
                dve.wait_ge(sems["y_ps"], k + 1)
                v.tensor_copy(yp[:, :, k * P:(k + 1) * P], ps[:, 4 + 2 * (k % 2), :].rearrange("p (t c) -> p t c", t=TT))
                v.tensor_copy(ysm[:, k * P:(k + 1) * P], ps[0:NS, 5 + 2 * (k % 2), 0:P]).then_inc(sems["y_ev"], 1)


def constants():
    t = np.zeros((P, NCONST), np.float32)

    def put(name, a):
        c, n = CONST[name]
        t[0:a.shape[0], c:c + n] = a.reshape(a.shape[0], n)

    i, j = np.arange(P)[:, None], np.arange(P)[None, :]
    put("ident", np.eye(P))
    rot = np.zeros((P, P))
    for h in range(P // DH):
        for d in range(8):
            rot[h * DH + d + 8, h * DH + d] = -1.0
            rot[h * DH + d, h * DH + d + 8] = 1.0
    put("rot", rot)
    put("upper", (i <= j).astype(np.float32))
    put("ones", np.ones((P, 7 * P)))
    put("later", (i > j).astype(np.float32))
    put("nupper", -(i >= j).astype(np.float32))
    put("nones", -np.ones((P, P)))
    inv = (np.float32(500000.0) ** (-np.arange(8, dtype=np.float32) / np.float32(8))).astype(np.float32)
    pos = np.concatenate([np.arange(SEQ), np.full(NS, PAST)]).astype(np.float32)
    ang = (pos[None, :] * inv[:, None]).astype(np.float32)
    cos, sin = np.ones((P, T), np.float32), np.zeros((P, T), np.float32)
    for h in range(P // DH):
        for o in (0, 8):
            cos[h * DH + o:h * DH + o + 8], sin[h * DH + o:h * DH + o + 8] = np.cos(ang), np.sin(ang)
    put("cos", cos)
    put("sin", sin)
    r, c = np.arange(64)[:, None], np.arange(64)[None, :]
    put("group", (r // 4 == c // 4).astype(np.float32))
    put("row8", (r // 8 == np.arange(8)[None, :]).astype(np.float32))
    put("row4", (np.arange(32)[:, None] // 4 == np.arange(8)[None, :]).astype(np.float32))
    q = np.arange(P)[:, None]
    put("mine", (np.where(q < 64, q // 8, q % 32 // 4) == np.arange(8)[None, :]).astype(np.float32))
    put("blk", np.tile(np.arange(1, NBLK - 1), (64, 1)).astype(np.float32))
    put("onehot", np.repeat(np.eye(4), P, axis=1))
    tok = np.arange(TT)[None, :, None] * P + np.arange(P)[:, None, None]
    sees = (np.arange(32)[None, None, :] * STRIDE + CBLK - 1 <= tok) & (np.arange(32) < NCP)
    put("cmp01", sees.astype(np.float32))
    put("mcausal", np.where(j > i, NEG, 0.0))
    put("mstrict", np.where(i >= j, NEG, 0.0))
    put("mcmp", np.where(sees, 0.0, NEG))
    return t


_INS = ["x_prompt", "x_sample", "cache_nsa_cmp_kv", "cache_nsa_sel_kv", "cache_sb_kv", "cache_fox_kv", "cache_fox_logf",
        "state_nsa_win_kv", "page_table", "norm_mix_g", "norm_ffn_g", "norm_final_g", "w_in", "b_forget", "cmp_pos",
        "w_cmp_k", "w_cmp_v", "w_up_nsa", "w_up_sb", "w_up_fox", "w_out", "w_ffn_gate", "w_ffn_up", "w_ffn_down"]
_OUTS = [("y_prompt", (1, SEQ, D)), ("y_sample", (NS, 1, D)),
         ("p_cmp", (DEPTH, 1, SEQ, 2, G, DH)), ("p_sel", (DEPTH, 1, SEQ, 2, G, DH)), ("p_sb", (DEPTH, 1, SEQ, 2, 4, DH)),
         ("p_fox", (DEPTH, 1, SEQ, 2, 4, DH)), ("p_logf", (DEPTH, 1, SEQ, 4)), ("p_win", (DEPTH, 1, WIN, 2, G, DH)),
         ("s_cmp", (DEPTH, NS, 1, 2, G, DH)), ("s_sel", (DEPTH, NS, 1, 2, G, DH)), ("s_sb", (DEPTH, NS, 1, 2, 4, DH)),
         ("s_fox", (DEPTH, NS, 1, 2, 4, DH)), ("s_logf", (DEPTH, NS, 1, 4)), ("s_win", (DEPTH, NS, WIN, 2, G, DH))]


def kernel(**inputs):
    import concourse.bacc as bacc
    from concourse.bass_utils import run_bass_kernel_spmd

    nc = bacc.Bacc("TRN2", target_bir_lowering=False, num_devices=1, dynamic_dma_scratch_size=1024)
    arrays = {f"in_{n}": np.ascontiguousarray(inputs[n]) for n in _INS}
    arrays["in_consts"] = constants()
    args = {n[3:]: nc.dram_tensor(n, a.shape, mybir.dt.from_np(a.dtype), kind="ExternalInput").ap() for n, a in arrays.items()}
    outs = {n: nc.dram_tensor(f"out_{n}", s, mybir.dt.float32, kind="ExternalOutput").ap() for n, s in _OUTS}
    build(nc, args, outs)
    r = run_bass_kernel_spmd(nc, [arrays], core_ids=[0])
    return tuple(r.results[0][f"out_{n}"] for n, _ in _OUTS)
```
